# Optimizing a Trainium2 kernel written in Bass

```python
import math
import jax, jax.numpy as jnp
from jax import lax
import numpy as np

D_MODEL = 1024
BATCH = 1
SEQ = 256
DEPTH = 2

N_A = DEPTH // 2
N_B = DEPTH - N_A
N_EVEN = (DEPTH + 1) // 2
N_ODD = DEPTH // 2

SSM_GROUP = 16
N_GROUPS = D_MODEL // SSM_GROUP
SSM_STATE = 64
SSM_CHUNK = 128
DT_MIN = 1e-3
DT_MAX = 1e-1

N_HEADS = 8
HEAD_DIM = D_MODEL // N_HEADS
MOBA_BLOCK = 256
MOBA_TOPK = 3
QUERY_CHUNK = 16
ROPE_THETA = 500000.0
ROT_DIM = HEAD_DIM // 4

D_FF_DENSE = 2816
N_EXPERTS = 8
MOE_TOPK = 2
D_FF_EXPERT = 3584
MOE_ROWS = 256

NORM_EPS = 1e-6
NEG_INF = -1e30

kernel_name = "yoco_s5_moba_moe_hybrid"

def rmsnorm(x, g):
    xf = x.astype(jnp.float32)
    y = xf * lax.rsqrt(jnp.mean(xf * xf, axis=-1, keepdims=True) + NORM_EPS)
    return (y * g.astype(jnp.float32)).astype(x.dtype)

def partial_rotary(x, positions):
    half = ROT_DIM // 2
    inv_freq = 1.0 / (ROPE_THETA ** (jnp.arange(half, dtype=jnp.float32) / half))
    ang = positions[:, None, :, None].astype(jnp.float32) * inv_freq
    cos, sin = jnp.cos(ang), jnp.sin(ang)
    xr = x[..., :ROT_DIM].astype(jnp.float32)
    x1, x2 = xr[..., :half], xr[..., half:]
    rot = jnp.concatenate([x1 * cos - x2 * sin, x2 * cos + x1 * sin], axis=-1)
    return jnp.concatenate([rot.astype(x.dtype), x[..., ROT_DIM:]], axis=-1)

def _complex_combine(e1, e2):
    a1r, a1i, b1r, b1i = e1
    a2r, a2i, b2r, b2i = e2
    return (a2r * a1r - a2i * a1i,
            a2r * a1i + a2i * a1r,
            a2r * b1r - a2i * b1i + b2r,
            a2r * b1i + a2i * b1r + b2i)

def s5_mixer(h, lam_re, lam_im, log_dt, b_re, b_im, c_re, c_im, d_skip, w_glu):
    f32 = jnp.float32
    Bsz, S, D = h.shape
    G, P = lam_re.shape
    lr, li = lam_re.astype(f32), lam_im.astype(f32)
    dt = jnp.exp(log_dt.astype(f32))[:, None]
    zr, zi = lr * dt, li * dt
    mag = jnp.exp(zr)
    a_r, a_i = mag * jnp.cos(zr * 0 + zi), mag * jnp.sin(zi)
    den = lr * lr + li * li
    coef_r = ((a_r - 1.0) * lr + a_i * li) / den
    coef_i = (a_i * lr - (a_r - 1.0) * li) / den
    br, bi = b_re.astype(f32), b_im.astype(f32)
    bb_r = coef_r[:, :, None] * br - coef_i[:, :, None] * bi
    bb_i = coef_r[:, :, None] * bi + coef_i[:, :, None] * br
    cr, ci = c_re.astype(f32), c_im.astype(f32)

    L = SSM_CHUNK
    nc = S // L
    steps = jnp.arange(1, L + 1, dtype=f32)[:, None, None]
    pmag = jnp.exp(steps * zr)
    pw_r, pw_i = pmag * jnp.cos(steps * zi), pmag * jnp.sin(steps * zi)
    ar_full = jnp.broadcast_to(a_r, (Bsz, L, G, P))
    ai_full = jnp.broadcast_to(a_i, (Bsz, L, G, P))

    u = h.astype(f32).reshape(Bsz, nc, L, G, SSM_GROUP).transpose(1, 0, 2, 3, 4)

    def chunk_step(carry, u_c):
        sr0, si0 = carry
        bu_r = jnp.einsum('blgi,gpi->blgp', u_c, bb_r)
        bu_i = jnp.einsum('blgi,gpi->blgp', u_c, bb_i)
        _, _, sr, si = lax.associative_scan(_complex_combine, (ar_full, ai_full, bu_r, bu_i), axis=1)
        sr = sr + pw_r * sr0[:, None] - pw_i * si0[:, None]
        si = si + pw_r * si0[:, None] + pw_i * sr0[:, None]
        y = jnp.einsum('blgp,gip->blgi', sr, cr) - jnp.einsum('blgp,gip->blgi', si, ci)
        return (sr[:, -1], si[:, -1]), y

    init = (jnp.zeros((Bsz, G, P), f32), jnp.zeros((Bsz, G, P), f32))
    _, ys = lax.scan(chunk_step, init, u)
    y = ys.transpose(1, 0, 2, 3, 4).reshape(Bsz, S, D) + d_skip.astype(f32) * h.astype(f32)
    g = jax.nn.gelu(y).astype(h.dtype)
    z = jnp.dot(g, w_glu)
    val, gate = z[..., :D], z[..., D:]
    return (val.astype(f32) * jax.nn.sigmoid(gate.astype(f32))).astype(h.dtype)

def shared_kv(s, g_kv, w_kv, positions):
    Bsz, S, D = s.shape
    hk = rmsnorm(s, g_kv)
    kv = jnp.dot(hk, w_kv)
    k = kv[..., :N_HEADS * HEAD_DIM].reshape(Bsz, S, N_HEADS, HEAD_DIM).transpose(0, 2, 1, 3)
    v = kv[..., N_HEADS * HEAD_DIM:].reshape(Bsz, S, N_HEADS, HEAD_DIM).transpose(0, 2, 1, 3)
    k = partial_rotary(k, positions)
    nb = -(-S // MOBA_BLOCK)
    pad = nb * MOBA_BLOCK - S
    k = jnp.pad(k, ((0, 0), (0, 0), (0, pad), (0, 0)))
    v = jnp.pad(v, ((0, 0), (0, 0), (0, pad), (0, 0)))
    kb = k.reshape(Bsz, N_HEADS, nb, MOBA_BLOCK, HEAD_DIM)
    vb = v.reshape(Bsz, N_HEADS, nb, MOBA_BLOCK, HEAD_DIM)
    kmean = jnp.mean(kb.astype(jnp.float32), axis=3)
    return kb, vb, kmean

def moba_attention(q, kb, vb, kmean):
    Bsz, H, S, Dh = q.shape
    nb = kb.shape[2]
    scale = Dh ** -0.5
    qblk = jnp.arange(S) // MOBA_BLOCK
    gate = jnp.einsum('bhsd,bhnd->bhsn', q.astype(jnp.float32), kmean)
    past = jnp.arange(nb)[None, :] < qblk[:, None]
    gate = jnp.where(past, gate, NEG_INF)
    k_sel = min(MOBA_TOPK, nb)
    _, idx = lax.top_k(gate, k_sel)
    valid = jnp.arange(k_sel)[None, :] < qblk[:, None]

    nq = S // QUERY_CHUNK
    q_c = q.reshape(Bsz, H, nq, QUERY_CHUNK, Dh).transpose(2, 0, 1, 3, 4)
    idx_c = idx.reshape(Bsz, H, nq, QUERY_CHUNK, k_sel).transpose(2, 0, 1, 3, 4)
    valid_c = valid.reshape(nq, QUERY_CHUNK, k_sel)
    b_ix = jnp.arange(Bsz)[:, None, None, None]
    h_ix = jnp.arange(H)[None, :, None, None]

    def one_chunk(args):
        qc, ic, vc, c = args
        t0 = c * QUERY_CHUNK
        qpos = t0 + jnp.arange(QUERY_CHUNK)
        j = t0 // MOBA_BLOCK
        ok = lax.dynamic_index_in_dim(kb, j, axis=2, keepdims=False)
        ov = lax.dynamic_index_in_dim(vb, j, axis=2, keepdims=False)
        gk = kb[b_ix, h_ix, ic]
        gv = vb[b_ix, h_ix, ic]
        s_sel = jnp.einsum('bhtd,bhtkid->bhtki', qc, gk).astype(jnp.float32) * scale
        s_sel = jnp.where(vc[None, None, :, :, None], s_sel, NEG_INF)
        s_sel = s_sel.reshape(Bsz, H, QUERY_CHUNK, k_sel * MOBA_BLOCK)
        s_own = jnp.einsum('bhtd,bhid->bhti', qc, ok).astype(jnp.float32) * scale
        kpos = j * MOBA_BLOCK + jnp.arange(MOBA_BLOCK)
        s_own = jnp.where(kpos[None, :] <= qpos[:, None], s_own, NEG_INF)
        p = jax.nn.softmax(jnp.concatenate([s_sel, s_own], axis=-1), axis=-1)
        p_sel = p[..., :k_sel * MOBA_BLOCK].reshape(Bsz, H, QUERY_CHUNK, k_sel, MOBA_BLOCK).astype(vb.dtype)
        p_own = p[..., k_sel * MOBA_BLOCK:].astype(vb.dtype)
        return (jnp.einsum('bhtki,bhtkid->bhtd', p_sel, gv)
                + jnp.einsum('bhti,bhid->bhtd', p_own, ov))

    outs = lax.map(one_chunk, (q_c, idx_c, valid_c, jnp.arange(nq)))
    return outs.transpose(1, 2, 0, 3, 4).reshape(Bsz, H, S, Dh)

def moba_mixer(h, w_q, w_o, kb, vb, kmean, positions):
    Bsz, S, D = h.shape
    q = jnp.dot(h, w_q).reshape(Bsz, S, N_HEADS, HEAD_DIM).transpose(0, 2, 1, 3)
    q = partial_rotary(q, positions)
    o = moba_attention(q, kb, vb, kmean)
    o = o.transpose(0, 2, 1, 3).reshape(Bsz, S, N_HEADS * HEAD_DIM)
    return jnp.dot(o, w_o)

def dense_swiglu(h, w1, w3, w2):
    return jnp.dot(jax.nn.silu(jnp.dot(h, w1)) * jnp.dot(h, w3), w2)

def moe_swiglu(h, w_router, b_router, w1, w3, w2):
    Bsz, S, D = h.shape
    N = Bsz * S
    E, R = N_EXPERTS, MOE_ROWS
    t = h.reshape(N, D)
    logits = jnp.dot(t, w_router).astype(jnp.float32) + b_router.astype(jnp.float32)
    top_v, top_e = lax.top_k(logits, MOE_TOPK)
    top_w = jax.nn.softmax(top_v, axis=-1)
    A = N * MOE_TOPK
    flat_e = top_e.reshape(A)
    flat_w = top_w.reshape(A)
    flat_tok = jnp.arange(A, dtype=jnp.int32) // MOE_TOPK
    order = jnp.argsort(flat_e)
    se = flat_e[order]
    counts = jnp.zeros((E,), jnp.int32).at[flat_e].add(1)
    starts = jnp.cumsum(counts) - counts
    pcounts = (counts + R - 1) // R * R
    pends = jnp.cumsum(pcounts)
    pstarts = pends - pcounts
    dest = pstarts[se] + jnp.arange(A, dtype=jnp.int32) - starts[se]
    total = A + E * R
    nblk = total // R
    row_tok = jnp.full((total,), N, jnp.int32).at[dest].set(flat_tok[order])
    row_w = jnp.zeros((total,), jnp.float32).at[dest].set(flat_w[order])
    blk_e = jnp.minimum(jnp.searchsorted(pends, jnp.arange(nblk, dtype=jnp.int32) * R, side='right'), E - 1)
    t_pad = jnp.concatenate([t, jnp.zeros((1, D), t.dtype)], axis=0)
    xin = t_pad[row_tok].reshape(nblk, R, D)

    def expert_block(args):
        xb, e = args
        return jnp.dot(jax.nn.silu(jnp.dot(xb, w1[e])) * jnp.dot(xb, w3[e]), w2[e])

    yb = lax.map(expert_block, (xin, blk_e)).reshape(total, D)
    out = jnp.zeros((N + 1, D), t.dtype).at[row_tok].add(
        (yb.astype(jnp.float32) * row_w[:, None]).astype(t.dtype))
    return out[:N].reshape(Bsz, S, D)

def setup_inputs(seed: int = 0) -> dict:
    key = jax.random.key(seed)
    ks = jax.random.split(key, 24)
    f32 = jnp.float32
    D, G, P, Q = D_MODEL, N_GROUPS, SSM_STATE, SSM_GROUP
    HD = N_HEADS * HEAD_DIM
    nrm = lambda k, shape, s: jax.random.normal(k, shape, f32) * s
    x = jax.random.normal(ks[0], (BATCH, SEQ, D), f32)
    offset = jax.random.randint(ks[1], (BATCH, 1), 0, 4096, dtype=jnp.int32)
    positions = offset + jnp.arange(SEQ, dtype=jnp.int32)[None, :]
    norms = 1.0 + nrm(ks[2], (DEPTH, 4, D), 0.02)
    s5_lam_re = -0.5 + nrm(ks[3], (N_A, G, P), 0.01)
    s5_lam_im = math.pi * jnp.arange(P, dtype=f32)[None, None, :] + nrm(ks[4], (N_A, G, P), 0.01)
    s5_log_dt = jax.random.uniform(ks[5], (N_A, G), f32, math.log(DT_MIN), math.log(DT_MAX))
    s5_b_re = nrm(ks[6], (N_A, G, P, Q), (2 * Q) ** -0.5)
    s5_b_im = nrm(ks[7], (N_A, G, P, Q), (2 * Q) ** -0.5)
    s5_c_re = nrm(ks[8], (N_A, G, Q, P), 0.5)
    s5_c_im = nrm(ks[9], (N_A, G, Q, P), 0.5)
    s5_d = nrm(ks[10], (N_A, D), 0.5)
    s5_w_glu = nrm(ks[11], (N_A, D, 2 * D), D ** -0.5)
    kv_norm = 1.0 + nrm(ks[12], (D,), 0.02)
    w_kv = nrm(ks[13], (D, 2 * HD), D ** -0.5)
    w_q = nrm(ks[14], (N_B, D, HD), D ** -0.5)
    w_o = nrm(ks[15], (N_B, HD, D), HD ** -0.5)
    ffn_w1 = nrm(ks[16], (N_EVEN, D, D_FF_DENSE), D ** -0.5)
    ffn_w3 = nrm(ks[17], (N_EVEN, D, D_FF_DENSE), D ** -0.5)
    ffn_w2 = nrm(ks[18], (N_EVEN, D_FF_DENSE, D), D_FF_DENSE ** -0.5)
    moe_router = nrm(ks[19], (N_ODD, D, N_EXPERTS), D ** -0.5)
    moe_bias = nrm(ks[20], (N_ODD, N_EXPERTS), 0.01)
    moe_w1 = nrm(ks[21], (N_ODD, N_EXPERTS, D, D_FF_EXPERT), D ** -0.5)
    moe_w3 = nrm(ks[22], (N_ODD, N_EXPERTS, D, D_FF_EXPERT), D ** -0.5)
    moe_w2 = nrm(ks[23], (N_ODD, N_EXPERTS, D_FF_EXPERT, D), D_FF_EXPERT ** -0.5)
    return {"x": x, "positions": positions, "norms": norms,
            "s5_lam_re": s5_lam_re, "s5_lam_im": s5_lam_im, "s5_log_dt": s5_log_dt,
            "s5_b_re": s5_b_re, "s5_b_im": s5_b_im, "s5_c_re": s5_c_re, "s5_c_im": s5_c_im,
            "s5_d": s5_d, "s5_w_glu": s5_w_glu,
            "kv_norm": kv_norm, "w_kv": w_kv, "w_q": w_q, "w_o": w_o,
            "ffn_w1": ffn_w1, "ffn_w3": ffn_w3, "ffn_w2": ffn_w2,
            "moe_router": moe_router, "moe_bias": moe_bias,
            "moe_w1": moe_w1, "moe_w3": moe_w3, "moe_w2": moe_w2}

def reference(x, positions, norms, s5_lam_re, s5_lam_im, s5_log_dt, s5_b_re, s5_b_im,
              s5_c_re, s5_c_im, s5_d, s5_w_glu, kv_norm, w_kv, w_q, w_o,
              ffn_w1, ffn_w3, ffn_w2, moe_router, moe_bias, moe_w1, moe_w3, moe_w2):
    h = x
    kb = vb = kmean = None
    for layer in range(DEPTH):
        g = norms[layer]
        if layer < N_A:
            mix = s5_mixer(rmsnorm(h, g[0]), s5_lam_re[layer], s5_lam_im[layer], s5_log_dt[layer],
                           s5_b_re[layer], s5_b_im[layer], s5_c_re[layer], s5_c_im[layer],
                           s5_d[layer], s5_w_glu[layer])
        else:
            if layer == N_A:
                kb, vb, kmean = shared_kv(h, kv_norm, w_kv, positions)
            i = layer - N_A
            mix = moba_mixer(rmsnorm(h, g[0]), w_q[i], w_o[i], kb, vb, kmean, positions)
        h = h + rmsnorm(mix, g[1])
        f_in = rmsnorm(h, g[2])
        if layer % 2 == 0:
            j = layer // 2
            f = dense_swiglu(f_in, ffn_w1[j], ffn_w3[j], ffn_w2[j])
        else:
            j = layer // 2
            f = moe_swiglu(f_in, moe_router[j], moe_bias[j], moe_w1[j], moe_w3[j], moe_w2[j])
        h = h + rmsnorm(f, g[3])
    return h


_drawn_inputs = setup_inputs


def setup_inputs(seed=0):
    import zlib

    import numpy as np

    out = dict(_drawn_inputs(seed))
    spreads = {}
    factors = {}
    for name, (base, spread) in spreads.items():
        noise = np.random.default_rng([zlib.crc32(name.encode()), seed]).standard_normal(out[name].shape)
        drawn = base * np.exp(spread * noise) if base else spread * noise
        out[name] = __import__('jax').numpy.asarray(drawn.astype(out[name].dtype))
    for name, factor in factors.items():
        out[name] = (out[name] * factor).astype(out[name].dtype)
    return out
```

```python
from contextlib import ExitStack

import numpy as np

import numpy as np

import numpy as np

import numpy as np

import numpy as np

import concourse.bass as bass
from concourse import mybir

F32 = mybir.dt.float32
I32 = mybir.dt.int32
ALU = mybir.AluOpType
ACT = mybir.ActivationFunctionType
AX_X = mybir.AxisListType.X

P = 128
D = 1024
S = 256
NT = S // P
KT = D // P
G, NSTATE, CH = 64, 64, 16
STEP = 8
NC = S // STEP
GB = 8
NB = G // GB
GQ = G // 4
HEADS, DH, ROT = 8, 128, 32
HALF = ROT // 2
FD = 2816
E, FE = 8, 3584
BK = 512
EPS = 1e-6
NEG = -1e30
INV_2PI = 0.15915494309189535
TWO_PI_HI = 6.28125
TWO_PI_LO = 0.0019353071795864769
ROUND = 12582912.0
PI_BELOW = 3.1415925
HALF_PI = 1.5707963267948966

RING = 7
SLOT = KT * BK
GLU_CHUNKS, KV_CHUNKS, Q_CHUNKS, O_CHUNKS = 4, 4, 2, 2
FULL = FD // BK
TAIL = FD - FULL * BK
UNITS = FE // BK
BLOCKS = S // P
STEPS = BLOCKS * UNITS
NPOW = 2 * STEP + 1
WORK = 15900
INV_FREQ = [float(1.0 / f) for f in
            (np.float32(500000.0) ** (np.arange(HALF, dtype=np.float32) / np.float32(HALF)))]
STAGES = ["s5", "ffn", "attn", "all"]

NPOW = 2 * STEP + 1
WORK = 15900
INV_FREQ = [float(1.0 / f) for f in
            (np.float32(500000.0) ** (np.arange(HALF, dtype=np.float32) / np.float32(HALF)))]
STAGES = ["s5", "ffn", "attn", "all"]

NPOW = 2 * STEP + 1
WORK = 15900
INV_FREQ = [float(1.0 / f) for f in
            (np.float32(500000.0) ** (np.arange(HALF, dtype=np.float32) / np.float32(HALF)))]
STAGES = ["s5", "ffn", "attn", "all"]

NPOW = 2 * STEP + 1
WORK = 15900
INV_FREQ = [float(1.0 / f) for f in
            (np.float32(500000.0) ** (np.arange(HALF, dtype=np.float32) / np.float32(HALF)))]
STAGES = ["s5", "ffn", "attn", "all"]

NPOW = 2 * STEP + 1
WORK = 15900
INV_FREQ = [float(1.0 / f) for f in
            (np.float32(500000.0) ** (np.arange(HALF, dtype=np.float32) / np.float32(HALF)))]
STAGES = ["s5", "ffn", "attn", "all"]

GLU0 = 0
FFN0 = GLU0 + GLU_CHUNKS
KV0 = FFN0 + 3 * FULL + 2
Q0 = KV0 + KV_CHUNKS
O0 = Q0 + Q_CHUNKS
MOE0 = O0 + O_CHUNKS
PER_EXPERT = 3 * UNITS


ORDER = [(kind, j) for j in range(UNITS) for kind in ("w1", "w3", "w2")]
assert len(ORDER) == PER_EXPERT and PER_EXPERT % RING == 0


def release(n):
    if n < FFN0:
        return "glu_gate", n // 2 * 2 + 2
    if n < FFN0 + 3 * FULL:
        j, kind = divmod(n - FFN0, 3)
        return ("ffn_down", 2 * j + 2) if kind == 2 else (("ffn_up", "ffn_up3")[kind], 2 * j + 2)
    if n < KV0:
        return ("ffn_up", "ffn_down")[n - FFN0 - 3 * FULL], 2 * FULL + 2
    for first, end, name in ((KV0, Q0, "kv_made"), (Q0, O0, "q_made"), (O0, MOE0, "proj_made")):
        if n < end:
            return name, NT * (n - first + 1)
    kind, j = ORDER[n - MOE0]
    return {"w1": "up1", "w3": "up3", "w2": "down"}[kind], 2 * j + 2


def wait(eng, sem, value):
    if not isinstance(value, int) or value > 0:
        eng.wait_ge(sem, value)


class Chain:

    def __init__(self, eng, sem):
        self.eng, self.sem, self.n, self.extra = eng, sem, 0, 0

    def __call__(self, ins):
        ins.then_inc(self.sem, 1)
        self.n += 1
        self.eng.wait_ge(self.sem, self.n + self.extra)


def lay_out(inputs):
    a = {k: np.asarray(v) for k, v in inputs.items()}
    a["positions"] = a["positions"].reshape(NT, P).T
    a["norm_cols"] = a["norms"].reshape(8, KT, P).transpose(2, 0, 1)
    a["kv_norm"] = a["kv_norm"].reshape(KT, P).T
    a["moe_router"] = a["moe_router"].reshape(KT, P, E).transpose(1, 0, 2)
    a["lam_re"], a["lam_im"] = a.pop("s5_lam_re")[0].T, a.pop("s5_lam_im")[0].T
    for k in ("re", "im"):
        a["b_" + k] = a.pop("s5_b_" + k)[0].transpose(1, 0, 2)
        a["c_" + k] = a.pop("s5_c_" + k)[0].transpose(2, 0, 1)
    return a


def lay_out(inputs):
    a = {k: np.asarray(v) for k, v in inputs.items()}
    a["positions"] = a["positions"].reshape(NT, P).T
    a["norm_cols"] = a["norms"].reshape(8, KT, P).transpose(2, 0, 1)
    a["kv_norm"] = a["kv_norm"].reshape(KT, P).T
    a["moe_router"] = a["moe_router"].reshape(KT, P, E).transpose(1, 0, 2)
    a["lam_re"], a["lam_im"] = a.pop("s5_lam_re")[0].T, a.pop("s5_lam_im")[0].T
    for k in ("re", "im"):
        a["b_" + k] = a.pop("s5_b_" + k)[0].transpose(1, 0, 2)
        a["c_" + k] = a.pop("s5_c_" + k)[0].transpose(2, 0, 1)
    return a


def lay_out(inputs):
    a = {k: np.asarray(v) for k, v in inputs.items()}
    a["positions"] = a["positions"].reshape(NT, P).T
    a["norm_cols"] = a["norms"].reshape(8, KT, P).transpose(2, 0, 1)
    a["kv_norm"] = a["kv_norm"].reshape(KT, P).T
    a["moe_router"] = a["moe_router"].reshape(KT, P, E).transpose(1, 0, 2)
    a["lam_re"], a["lam_im"] = a.pop("s5_lam_re")[0].T, a.pop("s5_lam_im")[0].T
    for k in ("re", "im"):
        a["b_" + k] = a.pop("s5_b_" + k)[0].transpose(1, 0, 2)
        a["c_" + k] = a.pop("s5_c_" + k)[0].transpose(2, 0, 1)
    return a


def lay_out(inputs):
    a = {k: np.asarray(v) for k, v in inputs.items()}
    a["positions"] = a["positions"].reshape(NT, P).T
    a["norm_cols"] = a["norms"].reshape(8, KT, P).transpose(2, 0, 1)
    a["kv_norm"] = a["kv_norm"].reshape(KT, P).T
    a["moe_router"] = a["moe_router"].reshape(KT, P, E).transpose(1, 0, 2)
    a["lam_re"], a["lam_im"] = a.pop("s5_lam_re")[0].T, a.pop("s5_lam_im")[0].T
    for k in ("re", "im"):
        a["b_" + k] = a.pop("s5_b_" + k)[0].transpose(1, 0, 2)
        a["c_" + k] = a.pop("s5_c_" + k)[0].transpose(2, 0, 1)
    return a


def lay_out(inputs):
    a = {k: np.asarray(v) for k, v in inputs.items()}
    a["positions"] = a["positions"].reshape(NT, P).T
    a["norm_cols"] = a["norms"].reshape(8, KT, P).transpose(2, 0, 1)
    a["kv_norm"] = a["kv_norm"].reshape(KT, P).T
    a["moe_router"] = a["moe_router"].reshape(KT, P, E).transpose(1, 0, 2)
    a["lam_re"], a["lam_im"] = a.pop("s5_lam_re")[0].T, a.pop("s5_lam_im")[0].T
    for k in ("re", "im"):
        a["b_" + k] = a.pop("s5_b_" + k)[0].transpose(1, 0, 2)
        a["c_" + k] = a.pop("s5_c_" + k)[0].transpose(2, 0, 1)
    return a


def trunk(nc, a, out, until="all"):
    ctx = ExitStack()
    with ctx:
        def sb(name, shape, dt=F32):
            return ctx.enter_context(nc.sbuf_tensor(name, shape, dt))

        sems = {}

        def sem(name):
            if name not in sems:
                sems[name] = ctx.enter_context(nc.semaphore(name))
            return sems[name]

        x = sb("x", [P, NT, D])
        xn = sb("xn", [P, NT, D])
        gain_a = sb("gain_a", [P, D])
        gain_b = sb("gain_b", [P, D])
        ident = sb("ident", [P, P])
        swap = sb("swap", [P, P])
        tri = sb("tri", [P, P])
        ones = sb("ones", [P, P])
        iota_c = sb("iota_c", [P, S])
        mask = sb("mask", [P, P])
        powers = sb("powers", [P, NPOW])
        gcol = sb("gcol", [P, 8, KT])
        kvcol = sb("kvcol", [P, KT])
        ss = sb("ss", [P, NT])
        sd = sb("sd", [P, NT])
        rstd = sb("rstd", [P, NT])
        const = sb("const", [P, 3])
        wr = sb("wr", [P, KT, E])
        rbias = sb("rbias", [P, E])
        rt = sb("rt", [P, 9, NT, E])
        rs = sb("rs", [P, 8, NT])
        slot = sb("slot", [P, NT, E + 1])
        wgt = sb("wgt", [P, NT, E + 1])
        count = sb("count", [P, E + 1], I32)
        posi = sb("posi", [P, NT], I32)
        posf = sb("posf", [P, NT])
        freq = sb("freq", [P, HALF])
        rope_sin = sb("rope_sin", [P, NT * HALF])
        rope_cos = sb("rope_cos", [P, NT * HALF])
        rope_tmp = sb("rope_tmp", [P, NT * HALF])
        small = sb("small", [P, 14, G])
        ring = sb("ring", [P, RING * SLOT])
        work = sb("work", [P, WORK])
        ps = ctx.enter_context(nc.psum_tensor("ps", [P, 8, BK], F32))

        def view(buf, at, *shape):
            n = 1
            for k in shape:
                n *= k
            if len(shape) == 1:
                return buf[:, at:at + n]
            names = "abcd"[:len(shape)]
            return buf[:, at:at + n].rearrange(f"p ({' '.join(names)}) -> p {' '.join(names)}",
                                               **{names[i]: shape[i] for i in range(1, len(shape))})

        xT = view(work, 0, KT, S)
        mix = view(work, 2048, NT, D)
        cr, ci, br, bi = (view(ring, 1024 * k, G, CH) for k in range(4))
        bbr, bbi, bstk = (view(ring, SLOT + 1024 * k, G, CH) for k in range(3))
        ca = view(ring, 2 * SLOT, G, STEP + 1, CH)
        vtok = ring[0:NC, 2 * SLOT + 9216:2 * SLOT + 9216 + STEP * D].rearrange("p (l d) -> p l d", l=STEP)
        vgrp = ring[0:NC, 2 * SLOT:2 * SLOT + STEP * D].rearrange("p (g l i) -> p g l i", l=STEP, i=CH)
        toep = view(ring, 2 * SLOT + 9216, G, P)
        cos_c = view(ring, 2 * SLOT + 17408, G, NC)
        useq = view(work, 0, G, NC)
        sin_c = view(work, 2048, G, NC)
        decay = view(work, 4096, G, NC)
        sprev = view(work, 6144, G, NC + 1)
        xx, yy = (view(work, 8256 + 576 * k, STEP + 1, G) for k in range(2))
        xx2, yy2 = (view(work, 9408 + 512 * k, STEP, G) for k in range(2))
        ang, mag, cosn, sinn, tmpn = (view(work, 10432 + 1088 * k, NPOW, G) for k in range(5))
        prod = [work[:, 4096 + 1152 * k:4096 + 1152 * (k + 1)] for k in range(2)]
        ba = [view(work, 10432 + 1024 * k, GB, P) for k in range(2)]
        wint = [view(work, 12480 + 1024 * k, GB, P) for k in range(2)]
        taps = [view(work, 10432, G // 2, P), view(ring, 2048, G // 2, P)]
        bsum = view(work, 8256, G, NC)
        turn = view(work, 10304, G, NC)
        state = view(work, 12352, G, NC)
        ytile = view(work, 10304, STEP, GQ, CH)
        gate_sb = [view(work, 5120 + 512 * k, BK) for k in range(2)]
        hid = [view(work, 6144 + 512 * k, BK) for k in range(2)]
        hidT = view(work, 7168, 4, P)
        kT, qT = view(work, 4096, HEADS, S), view(work, 6144, HEADS, S)
        v = view(work, 8192, NT, D)
        xTq = view(work, 10240, KT, S)
        att = [view(work, 12288 + 384 * k, 384) for k in range(2)]
        prob = [view(work, 13056 + 384 * k, 384) for k in range(2)]
        probT = [view(work, 13824 + 384 * k, 3, P) for k in range(2)]
        rot = [view(work, 14592 + 64 * k, 4, HALF) for k in range(4)]
        soft = view(work, 14848, HEADS, 4, NT)
        oT = xT
        acc = mix
        xTe = view(work, 0, BLOCKS, KT, P)
        y_rows = view(work, 8192, BLOCKS, D)
        onehot = view(work, 10240, NT, S)
        weighted = view(work, 10752, NT, S)
        weightedT = view(work, 11264, BLOCKS, S)

        h_dram = nc.dram_tensor("h_tokens", [S, D], F32).ap()
        y_dram = nc.dram_tensor("y_tokens", [S, D], F32).ap()

        def bcast_last(ap, n):
            return ap.rearrange("p (k o) -> p k o", o=1).broadcast_to([P, ap.shape[1], n])

        def bcast_mid(ap, n):
            return ap.rearrange("p (o k) -> p o k", o=1).broadcast_to([P, n, ap.shape[1]])

        def by_blocks(eng, i, steps):
            tokens = eng.value_load(count[0:1, bass.ds(i, 1)], min_val=0, max_val=S)
            with eng.If(tokens > P):
                steps(i, 2)
            with eng.Else():
                steps(i, 1)

        def after_step(i, s, blocks):
            return i * STEPS + (s + 1) * (BLOCKS // blocks)

        def slot_of(n):
            return view(ring, (n % RING) * SLOT, KT, BK)

        def down_slot(n):
            return view(ring, (n % RING) * SLOT, 4, D)

        landed = [sem(f"weights_landed_{k}") for k in range(RING)]
        used = sem("weights_used")

        def arrived(eng, n):
            eng.wait_ge(landed[n % RING], 16 * (n // RING + 1))

        stop = STAGES.index(until)
        ffn, attn, moe = stop >= 1, stop >= 2, stop >= 3

        block = ctx.enter_context(nc.Block())

        @block.sync
        def _(sp):
            sp.dma_start(x[:], a["x"].rearrange("b (t p) d -> p (b t) d", p=P)).then_inc(sem("x_in"), 16)
            sp.dma_start(gain_a[:], a["norms"][0, 0:1, :].broadcast_to([P, D])).then_inc(sem("gain_a_in"), 16)
            for half in range(2):
                rows = slice(64 * half, 64 * half + 64)
                sp.dma_start(small[rows, 0, :], a["lam_re"]).then_inc(sem("lam_in"), 16)
                sp.dma_start(small[rows, 1, :], a["lam_im"]).then_inc(sem("lam_in"), 16)
            sp.dma_start(small[:, 2, :], a["s5_log_dt"].broadcast_to([P, G])).then_inc(sem("lam_in"), 16)
            sp.dma_start(posi[:], a["positions"]).then_inc(sem("pos_in"), 16)
            for name, dst in (("b_re", br), ("b_im", bi), ("c_re", cr), ("c_im", ci)):
                for half in range(2):
                    sp.dma_start(dst[64 * half:64 * half + 64], a[name]).then_inc(sem("bc_in"), 16)
            sp.dma_start(gain_b[:], a["s5_d"].broadcast_to([P, D])).then_inc(sem("gain_b_in"), 16)
            sp.dma_start(gcol[:], a["norm_cols"]).then_inc(sem("const_in"), 16)
            sp.dma_start(kvcol[:], a["kv_norm"]).then_inc(sem("const_in"), 16)
            sp.dma_start(wr[:], a["moe_router"]).then_inc(sem("const_in"), 16)
            sp.dma_start(rbias[:], a["moe_bias"].broadcast_to([P, E])).then_inc(sem("const_in"), 16)

            sp.wait_ge(sem("h_ready"), NT)
            sp.dma_start(h_dram.rearrange("(t p) d -> p t d", p=P), xn[:]).then_inc(sem("h_out"), 16)
            sp.wait_ge(sem("h_out"), 16)
            sp.dma_start(vtok, h_dram.rearrange("(c l) d -> c l d", l=STEP)).then_inc(sem("v_in"), 16)
            sp.wait_ge(sem("toep_zero"), 1)
            for half in range(2):
                sp.wait_ge(sem("taps_ready"), NB // 2 * (half + 1))
                gs = slice(half * (G // 2), (half + 1) * (G // 2))
                for m in range(STEP):
                    sp.dma_start(toep[CH * m:CH * (m + 1), gs, CH * m:P],
                                 taps[half][0:CH, :, 0:P - CH * m]).then_inc(sem("toep_in"), 16)

            def load(n, src, dst):
                if n >= RING:
                    name, count = release(n - RING)
                    sp.wait_ge(sem(name), count)
                elif n < 2:
                    sp.wait_ge(sem("toep_in"), 16 * 2 * STEP)
                elif n == 2:
                    sp.wait_ge(sem("y_copied"), 1)
                sp.dma_start(dst, src).then_inc(landed[n % RING], 16)

            w_glu = a["s5_w_glu"][0].rearrange("(k p) n -> p k n", p=P)
            glu_cols = [0, 2, 1, 3]
            for c in range(2):
                load(GLU0 + c, w_glu[:, :, glu_cols[c] * BK:(glu_cols[c] + 1) * BK], slot_of(GLU0 + c))

            sp.wait_ge(sem("y_copied"), 1)
            for q in range(4):
                sp.dma_start(y_dram.rearrange("(c l) (q d) -> q c l d", l=STEP, q=4)[q],
                             ytile[32 * q:32 * q + 32].rearrange("c l g i -> c l (g i)"))\
                    .then_inc(sem("y_out"), 16)
            sp.wait_ge(sem("y_out"), 64)
            sp.dma_start(mix, y_dram.rearrange("(t p) d -> p t d", p=P)).then_inc(sem("y_in"), 16)

            for c in range(2, GLU_CHUNKS):
                load(GLU0 + c, w_glu[:, :, glu_cols[c] * BK:(glu_cols[c] + 1) * BK], slot_of(GLU0 + c))
            if ffn:
                w1 = a["ffn_w1"][0].rearrange("(k p) n -> p k n", p=P)
                w3 = a["ffn_w3"][0].rearrange("(k p) n -> p k n", p=P)
                for j in range(FULL):
                    n = FFN0 + 3 * j
                    load(n, w1[:, :, j * BK:(j + 1) * BK], slot_of(n))
                    load(n + 1, w3[:, :, j * BK:(j + 1) * BK], slot_of(n + 1))
                    load(n + 2, a["ffn_w2"][0, j * BK:(j + 1) * BK, :].rearrange("(k p) n -> p k n", p=P),
                         down_slot(n + 2))
                n = FFN0 + 3 * FULL
                load(n, w1[:, :, FULL * BK:FD], slot_of(n)[:, :, 0:TAIL])
                sp.dma_start(slot_of(n)[:, :, TAIL:2 * TAIL], w3[:, :, FULL * BK:FD]).then_inc(sem("ffn_tail"), 16)
                load(n + 1, a["ffn_w2"][0, FULL * BK:FD, :].rearrange("(k p) n -> p k n", p=P),
                     down_slot(n + 1)[:, 0:2, :])
            if attn:
                w_kv = a["w_kv"].rearrange("(k p) n -> p k n", p=P)
                w_q = a["w_q"][0].rearrange("(k p) n -> p k n", p=P)
                w_o = a["w_o"][0].rearrange("(k p) n -> p k n", p=P)
                for first, count, w in ((KV0, KV_CHUNKS, w_kv), (Q0, Q_CHUNKS, w_q), (O0, O_CHUNKS, w_o)):
                    for c in range(count):
                        load(first + c, w[:, :, c * BK:(c + 1) * BK], slot_of(first + c))
            if moe:
                def experts(i):
                    for c, (kind, j) in enumerate(ORDER):
                        n = MOE0 + c
                        if kind == "w2":
                            src, dst = a["moe_w2"][0, bass.ds(i, 1), j * BK:(j + 1) * BK, :], down_slot(n)
                        else:
                            src, dst = a[f"moe_{kind}"][0, bass.ds(i, 1), :, j * BK:(j + 1) * BK], slot_of(n)
                        src = src.rearrange("o (k p) n -> p (o k) n", p=P)
                        if c >= RING:
                            name, least = release(n - RING)
                            sp.wait_ge(sem(name), i * STEPS + least)
                        elif isinstance(i, int):
                            name, least = release(n - RING)
                            sp.wait_ge(sem(name), least)
                        else:
                            name, least = release(n - RING + PER_EXPERT)
                            sp.wait_ge(sem(name), i * STEPS + (least - STEPS))
                        sp.dma_start(dst, src).then_inc(landed[n % RING], 16)

                experts(0)
                with sp.Fori(1, E) as i:
                    experts(i)
            sp.wait_ge(sem("x_final"), NT)
            sp.dma_start(out.rearrange("b (t p) d -> p (b t) d", p=P), x[:]).then_inc(sem("stored"), 16)
            sp.wait_ge(sem("stored"), 16)

        @block.gpsimd
        def _(pool):
            chain = Chain(pool, sem("pool_chain"))
            nc.gpsimd.memset(const[:, 0:1], EPS).then_inc(sem("eps_set"), 1)
            nc.gpsimd.memset(const[:, 1:2], HALF_PI).then_inc(sem("eps_set"), 1)
            nc.gpsimd.memset(const[:, 2:3], 0.0).then_inc(sem("eps_set"), 1)
            nc.gpsimd.iota(powers[:, 0:STEP + 1], [[1, STEP + 1]], base=0, channel_multiplier=0,
                           allow_small_or_imprecise_dtypes=True).then_inc(sem("iotas"), 1)
            nc.gpsimd.iota(powers[:, STEP + 1:NPOW], [[-1, STEP]], base=STEP - 1, channel_multiplier=0,
                           allow_small_or_imprecise_dtypes=True).then_inc(sem("iotas"), 1)
            nc.gpsimd.iota(iota_c[:], [[1, S]], base=0, channel_multiplier=0,
                           allow_small_or_imprecise_dtypes=True).then_inc(sem("iotas"), 1)
            for k in range(HALF):
                nc.gpsimd.memset(freq[:, k:k + 1], INV_FREQ[k]).then_inc(sem("iotas"), 1)
            chain(nc.gpsimd.memset(ident[:], 0.0))
            nc.gpsimd.affine_select(out=ident[:], in_=ident[:], compare_op=ALU.not_equal, fill=1.0, base=0,
                                    pattern=[[-1, P]], channel_multiplier=1).then_inc(sem("ident_ready"), 1)
            chain(nc.gpsimd.memset(swap[:], 0.0))
            chain(nc.gpsimd.affine_select(out=swap[:], in_=swap[:], compare_op=ALU.not_equal, fill=1.0,
                                          base=-64, pattern=[[-1, P]], channel_multiplier=1))
            nc.gpsimd.affine_select(out=swap[:], in_=swap[:], compare_op=ALU.not_equal, fill=-1.0,
                                    base=64, pattern=[[-1, P]], channel_multiplier=1)\
                .then_inc(sem("swap_ready"), 1)
            nc.gpsimd.memset(ones[:], 1.0).then_inc(sem("masks_ready"), 1)
            chain(nc.gpsimd.memset(tri[:], 1.0))
            nc.gpsimd.affine_select(out=tri[:], in_=tri[:], compare_op=ALU.is_gt, fill=0.0, base=0,
                                    pattern=[[1, P]], channel_multiplier=-1).then_inc(sem("masks_ready"), 1)
            chain(nc.gpsimd.memset(mask[:], 0.0))
            nc.gpsimd.affine_select(out=mask[:], in_=mask[:], compare_op=ALU.is_ge, fill=NEG, base=0,
                                    pattern=[[-1, P]], channel_multiplier=1).then_inc(sem("masks_ready"), 1)

            pool.wait_ge(sem("tables_ready"), 1)
            for b in range(2 * NB):
                g = slice((b % NB) * GB, (b % NB + 1) * GB)
                if b >= 2:
                    pool.wait_ge(sem("summed"), b - 1)
                left, right, n = (bbi, yy2, STEP) if b < NB else (ci, yy, STEP + 1)
                dst = prod[b % 2][:, 0:GB * n * CH].rearrange("p (g n i) -> p g n i", n=n, i=CH)
                nc.gpsimd.tensor_tensor(
                    dst, left[:, g, :].rearrange("p g (o i) -> p g o i", o=1).broadcast_to([P, GB, n, CH]),
                    right[:, :, g].rearrange("p n (g o) -> p g n o", o=1).broadcast_to([P, GB, n, CH]),
                    ALU.mult).then_inc(sem("product"), 1)

            def gain(buf, name, row, after):
                pool.wait_ge(sem(after), NT)
                pool.dma_start(buf[:], row.broadcast_to([P, D])).then_inc(sem(name), 16)

            gain(gain_a, "gain_1_in", a["norms"][0, 1:2, :], "h_ready")
            if ffn:
                gain(gain_b, "gain_2_in", a["norms"][0, 3:4, :], "gelu_in")
            if attn:
                gain(gain_a, "gain_3_in", a["norms"][1, 1:2, :], "added_0")
            if moe:
                gain(gain_b, "gain_4_in", a["norms"][1, 3:4, :], "added_1")

        @block.scalar
        def _(act):
            chain = Chain(act, sem("act_chain"))

            def spread(src, name):
                act.wait_ge(sem("eps_set"), 3)
                for t in range(NT):
                    nc.scalar.activation(xn[:, t, :], src[:, t, :], ACT.Square, accum_out=ss[:, t:t + 1])\
                        .then_inc(sem("squared"), 1)
                spread.n += NT
                act.wait_ge(sem("squared"), spread.n)
                nc.scalar.activation(sd[:], ss[:], ACT.Sqrt, bias=const[:, 0:1], scale=1.0 / D)\
                    .then_inc(sem("root"), 1)
            spread.n = 0

            act.wait_ge(sem("x_in"), 16)
            spread(x, "s5")
            act.wait_ge(sem("lam_in"), 80)
            nc.scalar.activation(small[:, 2, :], small[:, 2, :], ACT.Exp).then_inc(sem("dt_ready"), 1)
            act.wait_ge(sem("mag_in"), 1)
            nc.scalar.activation(mag, mag, ACT.Exp).then_inc(sem("mag_ready"), 1)
            nc.scalar.activation(small[:, 7, :], small[:, 7, :], ACT.Exp).then_inc(sem("mag_ready"), 1)
            for src, sin, cos, tmp, ready, done in (
                    (ang, sinn, cosn, tmpn, "ang_ready", "trig_ready"),
                    (sin_c, sin_c, cos_c, decay, "phi_ready", "turn_ready"),
                    (rope_sin[:], rope_sin[:], rope_cos[:], rope_tmp[:], "rope_ready", "rope_done")):
                act.wait_ge(sem(ready), 1)
                chain(nc.scalar.activation(tmp, src, ACT.Abs))
                nc.scalar.activation(sin, src, ACT.Sin).then_inc(sem(done), 1)
                nc.scalar.activation(cos, tmp, ACT.Sin, bias=const[:, 1:2], scale=-1.0).then_inc(sem(done), 1)

            act.wait_ge(sem("v_in"), 16)
            nc.scalar.activation(vgrp[:, 0:G // 2].rearrange("p g l i -> p l g i"),
                                 vtok[:, :, 0:D // 2].rearrange("p l (g i) -> p l g i", i=CH), ACT.Copy)                .then_inc(sem("v_grouped"), 1)
            act.wait_ge(sem("v_grouped"), 2)
            nc.scalar.activation(toep, const[:, 2:3].rearrange("p (g m) -> p g m", g=1).broadcast_to([P, G, P]),
                                 ACT.Copy).then_inc(sem("toep_zero"), 1)
            act.wait_ge(sem("u_transposed"), 1)
            nc.scalar.activation(useq, ps[:, 0:4, :].rearrange("p b (g c) -> p (b g) c", c=NC), ACT.Copy)\
                .then_inc(sem("useq_ready"), 1)
            for b in range(NB):
                act.wait_ge(sem("ba_transposed"), b + 1)
                if b >= 2:
                    act.wait_ge(sem("chunk_sums"), b - 1)
                nc.scalar.activation(wint[b % 2], ps[:, 2 * (b % 2):2 * (b % 2) + 2, :]
                                     .rearrange("p b (g m) -> p (b g) m", m=P), ACT.Copy)\
                    .then_inc(sem("wint_ready"), 1)
            for b in range(NB):
                act.wait_ge(sem("taps_made"), b + 1)
                half, at = b // (NB // 2), (b % (NB // 2)) * GB
                nc.scalar.activation(taps[half][0:CH, at:at + GB, :], ps[0:CH, 2 * (b % 2):2 * (b % 2) + 2, :]
                                     .rearrange("p b (g m) -> p (b g) m", m=P), ACT.Copy)\
                    .then_inc(sem("taps_ready"), 1)
            nc.scalar.activation(bsum, ps[:, 4:8, :].rearrange("p b (g c) -> p (b g) c", c=NC), ACT.Copy)\
                .then_inc(sem("bsum_ready"), 1)
            act.wait_ge(sem("y_made"), 1)
            nc.scalar.activation(ytile.rearrange("p l g i -> p g l i"),
                                 ps[:, 0:4, :].rearrange("p b (g l i) -> p (b g) l i", l=STEP, i=CH), ACT.Copy)\
                .then_inc(sem("y_copied"), 1)
            act.wait_ge(sem("gelu_in"), NT)
            for t in range(NT):
                nc.scalar.activation(xn[:, t, :], mix[:, t, :], ACT.Gelu_apprx_tanh).then_inc(sem("g_ready"), 1)
            for b in range(4):
                act.wait_ge(sem("g_transposed"), b + 1)
                nc.scalar.activation(xT[:, 2 * b:2 * b + 2, :], ps[:, b, :].rearrange("p (k s) -> p k s", k=2),
                                     ACT.Copy).then_inc(sem("gT_ready"), 1)
            for s in range(GLU_CHUNKS):
                act.wait_ge(sem("glu_gate"), s + 1)
                if s >= 2:
                    act.wait_ge(sem("glu_out"), s - 1)
                nc.scalar.activation(gate_sb[s % 2], ps[:, 2 * (s % 2) + 1, :], ACT.Sigmoid)\
                    .then_inc(sem("glu_sig"), 1)
            act.wait_ge(sem("glu_out"), GLU_CHUNKS)
            spread(mix, "post")

            if ffn:
                act.wait_ge(sem("added_0"), NT)
                spread(x, "ffn")
                for s in range(NT * (FULL + 1) + 1):
                    if s < NT * (FULL + 1):
                        act.wait_ge(sem("ffn_up"), s + 1)
                        if s >= 2:
                            act.wait_ge(sem("ffn_hid"), s - 1)
                        w = BK if s < NT * FULL else TAIL
                        nc.scalar.activation(gate_sb[s % 2][:, 0:w], ps[:, 2 * (s % 2), 0:w], ACT.Silu)\
                            .then_inc(sem("ffn_gate"), 1)
                    if s >= 1:
                        k = s - 1
                        act.wait_ge(sem("ffn_hidT"), k + 1)
                        if k >= 1:
                            act.wait_ge(sem("ffn_down"), k)
                        m = 4 if k < NT * FULL else TAIL // P
                        nc.scalar.activation(hidT[:, 0:m, :], ps[:, 2 * (k % 2), 0:m * P]
                                             .rearrange("p (m s) -> p m s", m=m), ACT.Copy)\
                            .then_inc(sem("ffn_hidT_ready"), 1)
                act.wait_ge(sem("ffn_down"), NT * (FULL + 1))
                for t in range(NT):
                    nc.scalar.activation(mix[:, t, :], ps[:, 4 + 2 * t:6 + 2 * t, :]
                                         .rearrange("p b n -> p (b n)"), ACT.Copy).then_inc(sem("ffn_copied"), 1)
                act.wait_ge(sem("ffn_copied"), NT)
                spread(mix, "post")

            if attn:
                act.wait_ge(sem("added_1"), NT)
                spread(x, "attn")

                def heads(bank, dst, count, name):
                    act.wait_ge(sem(name), count)
                    nc.scalar.activation(dst, ps[:, bank, :], ACT.Copy).then_inc(sem(name + "_copied"), 1)

                for s in range(2 * NT):
                    heads(s, mix[:, s % NT, (s // NT) * BK:(s // NT + 1) * BK], s + 1, "kv_made")
                for s in range(2 * NT, 4 * NT):
                    act.wait_ge(sem("kv_made"), s + 1)
                    c = s // NT - 2
                    nc.scalar.activation(v[:, s % NT, c * BK:(c + 1) * BK], ps[:, s, :], ACT.Copy)\
                        .then_inc(sem("v_copied"), 1)
                for b in range(4):
                    act.wait_ge(sem("k_transposed"), b + 1)
                    nc.scalar.activation(kT[:, 2 * b:2 * b + 2, :], ps[:, b, :].rearrange("p (k s) -> p k s", k=2),
                                         ACT.Copy).then_inc(sem("kT_ready"), 1)
                for s in range(2 * NT):
                    if s == 0:
                        act.wait_ge(sem("k_transposed"), 4)
                    heads(4 + s, mix[:, s % NT, (s // NT) * BK:(s // NT + 1) * BK], s + 1, "q_made")
                for b in range(4):
                    act.wait_ge(sem("q_transposed"), b + 1)
                    nc.scalar.activation(qT[:, 2 * b:2 * b + 2, :], ps[:, b, :].rearrange("p (k s) -> p k s", k=2),
                                         ACT.Copy).then_inc(sem("qT_ready"), 1)
                for h in range(HEADS + 1):
                    if h < HEADS:
                        act.wait_ge(sem("score_max"), h + 1)
                        if h >= 2:
                            act.wait_ge(sem("prob_transposed"), h - 1)
                        for t in range(NT):
                            cols = slice(0, P) if t == 0 else slice(P, 3 * P)
                            nc.scalar.activation(prob[h % 2][:, cols], att[h % 2][:, cols], ACT.Exp,
                                                 bias=soft[:, h, 1, t:t + 1], accum_out=soft[:, h, 2, t:t + 1])\
                                .then_inc(sem("exped"), 1)
                    if h >= 1:
                        k = h - 1
                        act.wait_ge(sem("prob_transposed"), k + 1)
                        if k >= 2:
                            act.wait_ge(sem("o_made"), k - 1)
                        nc.scalar.activation(probT[k % 2], ps[:, 2 + k % 2, 0:384]
                                             .rearrange("p (m s) -> p m s", m=3), ACT.Copy)\
                            .then_inc(sem("probT_ready"), 1)
                for s in range(2 * NT):
                    act.wait_ge(sem("proj_made"), s + 1)
                    nc.scalar.activation(mix[:, s % NT, (s // NT) * BK:(s // NT + 1) * BK], ps[:, s, :], ACT.Copy)\
                        .then_inc(sem("proj_copied"), 1)
                act.wait_ge(sem("proj_copied"), 2 * NT)
                spread(mix, "post")

            if moe:
                act.wait_ge(sem("added_2"), NT)
                spread(x, "moe")
                act.wait_ge(sem("gap_ready"), 1)
                nc.scalar.activation(rs[:, 4, :], rs[:, 4, :], ACT.Exp).then_inc(sem("gap_exp"), 1)

                def hidden(i, blocks):
                    one = BLOCKS // blocks
                    for s in range(UNITS * blocks + 1):
                        if s < UNITS * blocks:
                            act.wait_ge(sem("up1"), after_step(i, s, blocks))
                            if s >= 2:
                                act.wait_ge(sem("hid_ready"), after_step(i, s - 2, blocks))
                            nc.scalar.activation(gate_sb[s % 2], ps[:, 2 * (s % 2), :], ACT.Silu)\
                                .then_inc(sem("gate_ready"), one)
                        if s >= 1:
                            act.wait_ge(sem("hid_T"), after_step(i, s - 1, blocks))
                            if s >= 2:
                                act.wait_ge(sem("down"), after_step(i, s - 2, blocks))
                            nc.scalar.activation(hidT, ps[:, 2 * ((s - 1) % 2), :]
                                                 .rearrange("p (m s) -> p m s", m=4), ACT.Copy)\
                                .then_inc(sem("hidT_ready"), one)
                    act.wait_ge(sem("down"), (i + 1) * STEPS)
                    nc.scalar.activation(y_rows[:, 0:blocks, :], ps[:, 4:4 + 2 * blocks, :]
                                         .rearrange("p (t b) n -> p t (b n)", b=2), ACT.Copy)\
                        .then_inc(sem("y_rows"), 1)

                act.wait_ge(sem("routed"), 1)
                with act.Fori(0, E) as i:
                    act.wait_ge(sem("weighted_T"), i + 1)
                    nc.scalar.activation(weightedT, ps[:, 0, :].rearrange("p (t s) -> p t s", t=BLOCKS), ACT.Copy)\
                        .then_inc(sem("weightedT_ready"), 1)
                    by_blocks(act, i, hidden)
                act.wait_ge(sem("acc_done"), 1)
                spread(acc, "post")

        @block.vector
        def _(dve):
            chain = Chain(dve, sem("dve_chain"))
            rooted = [0]
            TT, TS, STT = nc.vector.tensor_tensor, nc.vector.tensor_scalar, nc.vector.scalar_tensor_tensor

            def inverse_root():
                rooted[0] += 1
                dve.wait_ge(sem("root"), rooted[0])
                chain(nc.vector.reciprocal(rstd[:], sd[:]))

            def reduce_angle(v, tmp):
                chain(TS(tmp, v, INV_2PI, ROUND, ALU.mult, ALU.add))
                chain(TS(tmp, tmp, -ROUND, None, ALU.add))
                chain(STT(out=v, in0=tmp, scalar=-TWO_PI_HI, in1=v, op0=ALU.mult, op1=ALU.add))
                chain(STT(out=v, in0=tmp, scalar=-TWO_PI_LO, in1=v, op0=ALU.mult, op1=ALU.add))
                return TS(v, v, PI_BELOW, -PI_BELOW, ALU.min, ALU.max)

            inverse_root()
            dve.wait_ge(sem("gain_a_in"), 16)
            for t in range(NT):
                STT(out=xn[:, t, :], in0=x[:, t, :], scalar=rstd[:, t:t + 1], in1=gain_a[:],
                    op0=ALU.mult, op1=ALU.mult).then_inc(sem("h_ready"), 1)
            sm = [small[:, k, :] for k in range(14)]
            lr, li, dt, zr, zi, tmp, r8, m8, den, am1, cfr, cfi, t1, t2 = sm
            dve.wait_ge(sem("dt_ready"), 1)
            dve.wait_ge(sem("iotas"), 3 + HALF)
            chain(TT(zr, lr, dt, ALU.mult))
            chain(TT(zi, li, dt, ALU.mult))
            chain(TS(m8, zr, float(STEP), None, ALU.mult))
            TT(mag, bcast_mid(zr, NPOW), bcast_last(powers[:], G), ALU.mult).then_inc(sem("mag_in"), 1)
            chain(reduce_angle(zi, tmp))
            chain(TT(ang, bcast_mid(zi, NPOW), bcast_last(powers[:], G), ALU.mult))
            reduce_angle(ang, tmpn).then_inc(sem("ang_ready"), 1)
            chain(TS(r8, zi, float(STEP), None, ALU.mult))
            chain(reduce_angle(r8, tmp))
            chain(TT(sin_c, bcast_last(r8, NC), bcast_mid(iota_c[:, 0:NC], G), ALU.mult))
            reduce_angle(sin_c, decay).then_inc(sem("phi_ready"), 1)
            dve.wait_ge(sem("pos_in"), 16)
            chain(nc.vector.tensor_copy(posf[:], posi[:]))
            chain(TT(rope_sin[:].rearrange("p (t k) -> p t k", t=NT), bcast_last(posf[:], HALF),
                     bcast_mid(freq[:], NT), ALU.mult))
            reduce_angle(rope_sin[:], rope_tmp[:]).then_inc(sem("rope_ready"), 1)

            dve.wait_ge(sem("v_in"), 16)
            nc.vector.tensor_copy(vgrp[:, G // 2:G].rearrange("p g l i -> p l g i"),
                                  vtok[:, :, D // 2:D].rearrange("p l (g i) -> p l g i", i=CH))                .then_inc(sem("v_grouped"), 1)

            dve.wait_ge(sem("mag_ready"), 2)
            dve.wait_ge(sem("trig_ready"), 2)
            chain(TT(cosn, cosn, mag, ALU.mult))
            chain(TT(sinn, sinn, mag, ALU.mult))
            re, im = slice(0, 64), slice(64, P)
            up, down = slice(0, STEP + 1), slice(STEP + 1, NPOW)
            chain(nc.vector.tensor_copy(xx[re], cosn[re, up, :]))
            chain(TS(xx[im], sinn[im, up, :], -1.0, None, ALU.mult))
            chain(TS(yy[re], sinn[re, up, :], -1.0, None, ALU.mult))
            chain(TS(yy[im], cosn[im, up, :], -1.0, None, ALU.mult))
            chain(nc.vector.tensor_copy(xx2[re], cosn[re, down, :]))
            chain(nc.vector.tensor_copy(xx2[im], sinn[im, down, :]))
            chain(TS(yy2[re], sinn[re, down, :], -1.0, None, ALU.mult))
            chain(nc.vector.tensor_copy(yy2[im], cosn[im, down, :]))
            ar, ai = cosn[:, 1, :], sinn[:, 1, :]
            chain(TT(t1, lr, lr, ALU.mult))
            chain(TT(t2, li, li, ALU.mult))
            chain(TT(t1, t1, t2, ALU.add))
            chain(nc.vector.reciprocal(den, t1))
            chain(TS(am1, ar, -1.0, None, ALU.add))
            chain(TT(t1, am1, lr, ALU.mult))
            chain(TT(t2, ai, li, ALU.mult))
            chain(TT(t1, t1, t2, ALU.add))
            chain(TT(cfr, t1, den, ALU.mult))
            chain(TT(t1, ai, lr, ALU.mult))
            chain(TT(t2, am1, li, ALU.mult))
            chain(TT(t1, t1, t2, ALU.subtract))
            chain(TT(cfi, t1, den, ALU.mult))
            dve.wait_ge(sem("bc_in"), 128)
            tmpb = view(work, 10432, G, CH)
            fr, fi = bcast_last(cfr, CH), bcast_last(cfi, CH)
            chain(TT(bbr, br, fr, ALU.mult))
            chain(TT(tmpb, bi, fi, ALU.mult))
            chain(TT(bbr, bbr, tmpb, ALU.subtract))
            chain(TT(bbi, bi, fr, ALU.mult))
            chain(TT(tmpb, br, fi, ALU.mult))
            chain(TT(bbi, bbi, tmpb, ALU.add))
            chain(nc.vector.tensor_copy(bstk[re], bbr[re]))
            dve.wait_ge(sem("turn_ready"), 2)
            nc.vector.tensor_copy(bstk[im], bbi[im]).then_inc(sem("tables_ready"), 1)
            for b in range(2 * NB):
                g = slice((b % NB) * GB, (b % NB + 1) * GB)
                if b < NB:
                    if b >= 2:
                        dve.wait_ge(sem("ba_transposed"), b - 1)
                    left, right, n = bbr, xx2, STEP
                    dst = ba[b % 2].rearrange("p g (n i) -> p g n i", n=n)
                else:
                    if b == NB:
                        dve.wait_ge(sem("u_transposed"), 1)
                    left, right, n = cr, xx, STEP + 1
                    dst = ca[:, g]
                chain(TT(dst, left[:, g, :].rearrange("p g (o i) -> p g o i", o=1).broadcast_to([P, GB, n, CH]),
                         right[:, :, g].rearrange("p n (g o) -> p g n o", o=1).broadcast_to([P, GB, n, CH]),
                         ALU.mult))
                dve.wait_ge(sem("product"), b + 1)
                TT(dst, dst, prod[b % 2][:, 0:GB * n * CH].rearrange("p (g n i) -> p g n i", n=n, i=CH),
                   ALU.add).then_inc(sem("summed"), 1)
            dve.wait_ge(sem("summed"), 2 * NB)
            chain(nc.vector.tensor_copy(decay, bcast_last(m8, NC)))
            chain(nc.vector.memset(decay[:, :, 0:1], 0.0))
            chain(nc.vector.memset(sprev[:, :, 0:1], 0.0))
            dve.wait_ge(sem("bsum_ready"), 1)
            dve.wait_ge(sem("taps_ready"), NB)
            dve.wait_ge(sem("toep_in"), 16 * 2 * STEP)
            psg = [ps[:, 4 * k:4 * k + 4, :].rearrange("p b (g c) -> p (b g) c", c=NC) for k in range(2)]
            chain(TT(turn, bsum, cos_c, ALU.mult))
            dve.wait_ge(sem("swapped"), 1)
            chain(TT(state, psg[0], sin_c, ALU.mult))
            chain(TT(turn, turn, state, ALU.add))
            flat = "p g c -> p (g c)"
            nc.vector.tensor_tensor_scan(state.rearrange(flat), decay.rearrange(flat), turn.rearrange(flat),
                                         0.0, ALU.mult, ALU.add).then_inc(sem("scanned"), 1)
            dve.wait_ge(sem("scanned"), 1)
            chain(TT(turn, state, cos_c, ALU.mult))
            dve.wait_ge(sem("swapped"), 2)
            chain(TT(bsum, psg[1], sin_c, ALU.mult))
            TT(sprev[:, :, 1:NC + 1], turn, bsum, ALU.subtract).then_inc(sem("states_ready"), 1)
            dve.wait_ge(sem("gain_b_in"), 16)
            dve.wait_ge(sem("h_out"), 16)
            for t in range(NT):
                chain(TT(xn[:, t, :], xn[:, t, :], gain_b[:], ALU.mult))
            dve.wait_ge(sem("y_in"), 16)
            for t in range(NT):
                TT(mix[:, t, :], mix[:, t, :], xn[:, t, :], ALU.add).then_inc(sem("gelu_in"), 1)
            for s in range(GLU_CHUNKS):
                dve.wait_ge(sem("glu_sig"), s + 1)
                n, t = s // NT, s % NT
                TT(mix[:, t, n * BK:(n + 1) * BK], ps[:, 2 * (s % 2), :], gate_sb[s % 2], ALU.mult)\
                    .then_inc(sem("glu_out"), 1)

            def post(gain, gain_sem, name):
                inverse_root()
                dve.wait_ge(sem(gain_sem), 16)
                for t in range(NT):
                    chain(STT(out=xn[:, t, :], in0=mix[:, t, :], scalar=rstd[:, t:t + 1], in1=gain[:],
                              op0=ALU.mult, op1=ALU.mult))
                    TT(x[:, t, :], x[:, t, :], xn[:, t, :], ALU.add).then_inc(sem(name), 1)

            def pre(name, outs):
                inverse_root()
                for t in range(NT):
                    TS(xn[:, t, :], x[:, t, :], rstd[:, t:t + 1], None, ALU.mult).then_inc(sem(name + "_xn"), 1)
                for b in range(4):
                    dve.wait_ge(sem(name + "_transposed"), b + 1)
                    for dst, gains in outs:
                        TT(dst[:, 2 * b:2 * b + 2, :], ps[:, b, :].rearrange("p (k s) -> p k s", k=2),
                           bcast_last(gains[:, 2 * b:2 * b + 2], S), ALU.mult).then_inc(sem(name + "_xT"), 1)

            post(gain_a, "gain_1_in", "added_0" if ffn else "x_final")
            if ffn:
                dve.wait_ge(sem("const_in"), 64)
                pre("ffn", [(xT, gcol[:, 2, :])])
                for s in range(NT * (FULL + 1)):
                    dve.wait_ge(sem("ffn_gate"), s + 1)
                    if s < NT * FULL:
                        dve.wait_ge(sem("ffn_up3"), s + 1)
                    if s >= 2:
                        dve.wait_ge(sem("ffn_hidT"), s - 1)
                    full = s < NT * FULL
                    w = BK if full else TAIL
                    up3 = ps[:, 2 * (s % 2) + 1, 0:w] if full else ps[:, 2 * (s % 2), w:2 * w]
                    TT(hid[s % 2][:, 0:w], gate_sb[s % 2][:, 0:w], up3, ALU.mult).then_inc(sem("ffn_hid"), 1)
                post(gain_b, "gain_2_in", "added_1" if attn else "x_final")
            if attn:
                pre("attn", [(xT, kvcol[:]), (xTq, gcol[:, 4, :])])
                dve.wait_ge(sem("rope_done"), 2)

                def turn_heads(t, rows, done):
                    src = rows.rearrange("p (h d) -> p h d", d=DH)
                    x1, x2 = src[:, :, 0:HALF], src[:, :, HALF:ROT]
                    cos = bcast_mid(rope_cos[:, t * HALF:(t + 1) * HALF], 4)
                    sin = bcast_mid(rope_sin[:, t * HALF:(t + 1) * HALF], 4)
                    chain(TT(rot[0], x1, cos, ALU.mult))
                    chain(TT(rot[1], x2, sin, ALU.mult))
                    chain(TT(rot[2], x2, cos, ALU.mult))
                    chain(TT(rot[3], x1, sin, ALU.mult))
                    chain(TT(x1, rot[0], rot[1], ALU.subtract))
                    TT(x2, rot[2], rot[3], ALU.add).then_inc(sem(done), 1)
                    turned[0] += 1
                    dve.wait_ge(sem(done), turned[0])

                turned = [0]
                for s in range(2 * NT):
                    dve.wait_ge(sem("kv_made_copied"), s + 1)
                    turn_heads(s % NT, mix[:, s % NT, (s // NT) * BK:(s // NT + 1) * BK], "k_turned")
                turned = [0]
                for s in range(2 * NT):
                    dve.wait_ge(sem("q_made_copied"), s + 1)
                    turn_heads(s % NT, mix[:, s % NT, (s // NT) * BK:(s // NT + 1) * BK], "q_turned")
                dve.wait_ge(sem("masks_ready"), 3)
                scale = float(DH) ** -0.5

                def normalise(h):
                    dve.wait_ge(sem("exped"), NT * (h + 1))
                    chain(nc.vector.reciprocal(soft[:, h, 3, :], soft[:, h, 2, :]))
                    p = prob[h % 2]
                    TS(p[:, 0:P], p[:, 0:P], soft[:, h, 3, 0:1], None, ALU.mult).then_inc(sem("prob_ready"), 1)
                    TS(p[:, P:3 * P], p[:, P:3 * P], soft[:, h, 3, 1:2], None, ALU.mult)\
                        .then_inc(sem("prob_ready"), 1)

                for h in range(HEADS + 2):
                    if h < HEADS:
                        dve.wait_ge(sem("scores"), h + 1)
                        if h >= 2:
                            dve.wait_ge(sem("exped"), NT * (h - 1))
                        s, src = att[h % 2], ps[:, h % 2, 0:384]
                        chain(STT(out=s[:, 0:P], in0=src[:, 0:P], scalar=scale, in1=mask[:],
                                  op0=ALU.mult, op1=ALU.add))
                        chain(TS(s[:, P:2 * P], src[:, P:2 * P], scale, None, ALU.mult))
                        STT(out=s[:, 2 * P:3 * P], in0=src[:, 2 * P:3 * P], scalar=scale, in1=mask[:],
                            op0=ALU.mult, op1=ALU.add).then_inc(sem("scores_read"), 1)
                        dve.wait_ge(sem("scores_read"), h + 1)
                        chain(nc.vector.reduce_max(soft[:, h, 0, 0:1], s[:, 0:P], AX_X))
                        chain(nc.vector.reduce_max(soft[:, h, 0, 1:2], s[:, P:3 * P], AX_X))
                        TS(soft[:, h, 1, :], soft[:, h, 0, :], -1.0, None, ALU.mult).then_inc(sem("score_max"), 1)
                    if 1 <= h <= HEADS:
                        normalise(h - 1)
                    if h >= 2:
                        k = h - 2
                        dve.wait_ge(sem("o_made"), k + 1)
                        nc.vector.tensor_copy(oT[:, k, :], ps[:, 4 + k % 2, 0:S]).then_inc(sem("oT_ready"), 1)
                post(gain_a, "gain_3_in", "added_2" if moe else "x_final")
            if moe:
                pre("moe", [(xT, gcol[:, 6, :])])
                lg, eq, cand, oh1, oh2, sel, w, iota_e, far = (rt[:, k] for k in range(9))
                m1, i1, m2, i2, gap, den, w1, w2 = (rs[:, k, :] for k in range(8))
                wide = lambda ap: bcast_last(ap, E)
                chain(nc.vector.tensor_copy(iota_e, bcast_mid(iota_c[:, 0:E], NT)))
                chain(TS(far, iota_e, 99.0, None, ALU.add))
                dve.wait_ge(sem("logits"), 1)
                chain(TT(lg, ps[:, 4, 0:NT * E].rearrange("p (t e) -> p t e", t=NT), bcast_mid(rbias[:], NT),
                         ALU.add))
                for m, i, oh in ((m1, i1, oh1), (m2, i2, oh2)):
                    chain(nc.vector.reduce_max(m, lg, AX_X))
                    chain(TT(eq, lg, wide(m), ALU.is_equal))
                    chain(STT(out=cand, in0=eq, scalar=-99.0, in1=far, op0=ALU.mult, op1=ALU.add))
                    chain(nc.vector.tensor_reduce(i, cand, axis=AX_X, op=ALU.min))
                    chain(TT(oh, iota_e, wide(i), ALU.is_equal))
                    if oh is oh1:
                        chain(STT(out=lg, in0=oh, scalar=NEG, in1=lg, op0=ALU.mult, op1=ALU.add))
                TT(gap, m2, m1, ALU.subtract).then_inc(sem("gap_ready"), 1)
                TT(sel, oh1, oh2, ALU.add).then_inc(sem("sel_ready"), 1)
                dve.wait_ge(sem("gap_exp"), 1)
                chain(TS(den, gap, 1.0, None, ALU.add))
                chain(nc.vector.reciprocal(w1, den))
                chain(TT(w2, gap, w1, ALU.mult))
                chain(TT(cand, oh1, wide(w1), ALU.mult))
                chain(TT(w, oh2, wide(w2), ALU.mult))
                chain(TT(w, w, cand, ALU.add))
                chain(nc.vector.tensor_copy(wgt[:, :, 0:E], w))
                chain(nc.vector.memset(wgt[:, :, E:E + 1], 0.0))
                dve.wait_ge(sem("places"), 1)
                place = ps[:, 5, 0:NT * E].rearrange("p (t e) -> p t e", t=NT)
                chain(STT(out=cand, in0=place, scalar=1.0, in1=sel, op0=ALU.add, op1=ALU.mult))
                chain(TS(slot[:, :, 0:E], cand, -1.0, None, ALU.add))
                chain(nc.vector.memset(slot[:, :, E:E + 1], -1.0))
                chain(nc.vector.memset(count[:, E:E + 1], 0))
                nc.vector.tensor_copy(count[:, 0:E], ps[:, 6, 0:E]).then_inc(sem("routed"), 1)
                for t in range(NT):
                    nc.vector.memset(acc[:, t, :], 0.0).then_inc(sem("added"), 2)
                dve.wait_ge(sem("added"), 4)
                dve.wait_ge(sem("routed"), 1)

                def one_hots(i):
                    for t in range(NT):
                        TS(onehot[:, t, :], iota_c[:], slot[:, t, bass.ds(i, 1)], None, ALU.is_equal)\
                            .then_inc(sem("onehot_ready"), 1)

                def gathered_in(i, blocks):
                    dve.wait_ge(sem("gathered"), i + 1)
                    for b in range(blocks):
                        TT(xTe[:, b], ps[:, 2 * b:2 * b + 2, :].rearrange("p b (k s) -> p (b k) s", s=P),
                           bcast_last(gcol[:, 6, :], P), ALU.mult).then_inc(sem("xTe_ready"), BLOCKS // blocks)

                def hidden(i, blocks):
                    for s in range(UNITS * blocks):
                        dve.wait_ge(sem("gate_ready"), after_step(i, s, blocks))
                        dve.wait_ge(sem("up3"), after_step(i, s, blocks))
                        if s >= 2:
                            dve.wait_ge(sem("hid_T"), after_step(i, s - 2, blocks))
                        TT(hid[s % 2], gate_sb[s % 2], ps[:, 2 * (s % 2) + 1, :], ALU.mult)\
                            .then_inc(sem("hid_ready"), BLOCKS // blocks)

                one_hots(0)
                by_blocks(dve, 0, gathered_in)
                with dve.Fori(0, E) as i:
                    dve.wait_ge(sem("gathered"), i + 1)
                    for t in range(NT):
                        TS(weighted[:, t, :], iota_c[:], slot[:, t, bass.ds(i, 1)], wgt[:, t, bass.ds(i, 1)],
                           ALU.is_equal, ALU.mult).then_inc(sem("weighted_ready"), 1)
                    one_hots(i + 1)
                    by_blocks(dve, i, hidden)
                    by_blocks(dve, i + 1, gathered_in)
                    for q in range(4):
                        dve.wait_ge(sem("combined"), i * 4 + q + 1)
                        dst = acc[:, q // 2, (q % 2) * BK:(q % 2 + 1) * BK]
                        TT(dst, dst, ps[:, 4 + q, :], ALU.add).then_inc(sem("added"), 1)
                    dve.wait_ge(sem("added"), i * 4 + 8)
                nc.vector.memset(rs[:, 2, :], 0.0).then_inc(sem("acc_done"), 1)
                post(gain_b, "gain_4_in", "x_final")

        @block.tensor
        def _(pe):
            mm = nc.tensor.matmul

            def use(ins):
                ins.then_inc(used, 1)

            def transposes(src, name):
                for b in range(4):
                    for k in range(2):
                        for t in range(NT):
                            kt = 2 * b + k
                            last = nc.tensor.transpose(ps[:, b, k * S + t * P:k * S + (t + 1) * P],
                                                       src[:, t, kt * P:(kt + 1) * P], ident[:])
                    last.then_inc(sem(name), 1)

            def rows(bank, lhs, t, w, n=BK, at=0):
                for kt in range(KT):
                    last = mm(ps[:, bank, at:at + n], lhs[:, kt, t * P:(t + 1) * P], w[:, kt, 0:n],
                              start=(kt == 0), stop=(kt == KT - 1))
                return last

            pe.wait_ge(sem("ident_ready"), 1)
            pe.wait_ge(sem("v_grouped"), 2)
            for g in range(G):
                last = nc.tensor.transpose(ps[:, g // 16, (g % 16) * NC:(g % 16 + 1) * NC],
                                           vgrp[:, g].rearrange("p l i -> p (l i)"), ident[0:NC, 0:NC])
            last.then_inc(sem("u_transposed"), 1)

            def chunk_sums(b):
                pe.wait_ge(sem("wint_ready"), b + 1)
                for k in range(GB):
                    last = mm(ps[:, 4 + b // 2, (b % 2) * GB * NC + k * NC:(b % 2) * GB * NC + (k + 1) * NC],
                              wint[b % 2][:, k, :], useq[:, b * GB + k, :], start=True, stop=True)
                last.then_inc(sem("chunk_sums"), 1)

            pe.wait_ge(sem("useq_ready"), 1)
            for b in range(NB):
                pe.wait_ge(sem("summed"), b + 1)
                if b >= 2:
                    pe.wait_ge(sem("wint_ready"), b - 1)
                for k in range(GB):
                    last = nc.tensor.transpose(ps[:, 2 * (b % 2) + k // 4, (k % 4) * P:(k % 4 + 1) * P],
                                               ba[b % 2][:, k, :], ident[:])
                last.then_inc(sem("ba_transposed"), 1)
                if b >= 1:
                    chunk_sums(b - 1)
            chunk_sums(NB - 1)
            for b in range(NB):
                pe.wait_ge(sem("summed"), NB + b + 1)
                if b >= 2:
                    pe.wait_ge(sem("taps_ready"), b - 1)
                for k in range(GB):
                    g = b * GB + k
                    last = mm(ps[0:CH, 2 * (b % 2) + k // 4, (k % 4) * P:(k % 4 + 1) * P], bstk[:, g, :],
                              ca[:, g, 0:STEP, :].rearrange("p n i -> p (n i)"), start=True, stop=True)
                last.then_inc(sem("taps_made"), 1)
            pe.wait_ge(sem("swap_ready"), 1)
            for k, (src, ready) in enumerate(((bsum, "bsum_ready"), (state, "scanned"))):
                pe.wait_ge(sem(ready), 1)
                if k == 0:
                    pe.wait_ge(sem("taps_ready"), NB)
                flat = src.rearrange("p g c -> p (g c)")
                for b in range(4):
                    last = mm(ps[:, 4 * k + b, :], swap[:], flat[:, b * BK:(b + 1) * BK], start=True, stop=True)
                last.then_inc(sem("swapped"), 1)
            pe.wait_ge(sem("states_ready"), 1)
            pe.wait_ge(sem("toep_in"), 16 * 2 * STEP)
            for g4 in range(GQ):
                for q in range(4):
                    g = q * GQ + g4
                    dst = ps[32 * q:32 * q + 32, g4 // 4, (g4 % 4) * P:(g4 % 4 + 1) * P]
                    mm(dst, sprev[:, g, 0:NC], ca[:, g, 1:STEP + 1, :].rearrange("p n i -> p (n i)"),
                       start=True, stop=False, tile_position=(0, 32 * q))
                    last = mm(dst, useq[:, g, :], toep[:, g, :], start=False, stop=True, tile_position=(0, 32 * q))
            last.then_inc(sem("y_made"), 1)

            pe.wait_ge(sem("y_copied"), 1)
            pe.wait_ge(sem("g_ready"), NT)
            transposes(xn, "g_transposed")
            pe.wait_ge(sem("gT_ready"), 4)
            for s in range(GLU_CHUNKS):
                n, t = s // NT, s % NT
                if s >= 2:
                    pe.wait_ge(sem("glu_out"), s - 1)
                for k in range(2):
                    if t == 0:
                        arrived(pe, GLU0 + 2 * n + k)
                    last = rows(2 * (s % 2) + k, xT, t, slot_of(GLU0 + 2 * n + k))
                last.then_inc(sem("glu_gate"), 1)

            if ffn:
                pe.wait_ge(sem("ffn_xn"), NT)
                pe.wait_ge(sem("glu_out"), GLU_CHUNKS)
                transposes(xn, "ffn_transposed")
                pe.wait_ge(sem("ffn_xT"), 4)
                last_s = NT * (FULL + 1)
                for s in range(last_s + 1):
                    if s < last_s:
                        j, t = s // NT, s % NT
                        n = FFN0 + 3 * j
                        if t == 0:
                            arrived(pe, n)
                            if j == FULL:
                                pe.wait_ge(sem("ffn_tail"), 16)
                        if s >= 2:
                            pe.wait_ge(sem("ffn_hidT_ready"), s - 1)
                            pe.wait_ge(sem("ffn_hid"), s - 1)
                        last = rows(2 * (s % 2), xT, t, slot_of(n))
                        last.then_inc(sem("ffn_up"), 1)
                    if s >= 1:
                        k = s - 1
                        m = 4 if k < NT * FULL else TAIL // P
                        pe.wait_ge(sem("ffn_hid"), k + 1)
                        for f in range(m):
                            last = nc.tensor.transpose(ps[:, 2 * (k % 2), f * P:(f + 1) * P],
                                                       hid[k % 2][:, f * P:(f + 1) * P], ident[:])
                        last.then_inc(sem("ffn_hidT"), 1)
                    if s < NT * FULL:
                        if t == 0:
                            arrived(pe, n + 1)
                        rows(2 * (s % 2) + 1, xT, t, slot_of(n + 1)).then_inc(sem("ffn_up3"), 1)
                    if s >= 1:
                        jk, tk = k // NT, k % NT
                        nk = FFN0 + 3 * jk + (2 if jk < FULL else 1)
                        if tk == 0:
                            arrived(pe, nk)
                        pe.wait_ge(sem("ffn_hidT_ready"), k + 1)
                        for f in range(m):
                            for half in range(2):
                                last = mm(ps[:, 4 + 2 * tk + half, :], hidT[:, f, :],
                                          down_slot(nk)[:, f, half * BK:(half + 1) * BK],
                                          start=(jk == 0 and f == 0), stop=(jk == FULL and f == m - 1))
                        last.then_inc(sem("ffn_down"), 1)

            if attn:
                pe.wait_ge(sem("attn_xn"), NT)
                transposes(xn, "attn_transposed")
                pe.wait_ge(sem("attn_xT"), 8)
                pe.wait_ge(sem("ffn_copied"), NT)
                for s in range(NT * KV_CHUNKS):
                    if s % NT == 0:
                        arrived(pe, KV0 + s // NT)
                    rows(s, xT, s % NT, slot_of(KV0 + s // NT)).then_inc(sem("kv_made"), 1)
                pe.wait_ge(sem("kv_made_copied"), 2 * NT)
                pe.wait_ge(sem("k_turned"), 2 * NT)
                transposes(mix, "k_transposed")
                pe.wait_ge(sem("v_copied"), 2 * NT)
                for s in range(NT * Q_CHUNKS):
                    if s % NT == 0:
                        arrived(pe, Q0 + s // NT)
                    rows(4 + s, xTq, s % NT, slot_of(Q0 + s // NT)).then_inc(sem("q_made"), 1)
                pe.wait_ge(sem("q_made_copied"), 2 * NT)
                pe.wait_ge(sem("q_turned"), 2 * NT)
                pe.wait_ge(sem("kT_ready"), 4)
                transposes(mix, "q_transposed")
                pe.wait_ge(sem("qT_ready"), 4)
                for h in range(HEADS + 2):
                    if h < HEADS:
                        if h >= 2:
                            pe.wait_ge(sem("scores_read"), h - 1)
                        mm(ps[:, h % 2, 0:P], qT[:, h, 0:P], kT[:, h, 0:P], start=True, stop=True)
                        mm(ps[:, h % 2, P:3 * P], qT[:, h, P:S], kT[:, h, :], start=True, stop=True)\
                            .then_inc(sem("scores"), 1)
                    if 1 <= h <= HEADS:
                        k = h - 1
                        pe.wait_ge(sem("prob_ready"), NT * (k + 1))
                        if k >= 2:
                            pe.wait_ge(sem("probT_ready"), k - 1)
                        for m in range(3):
                            last = nc.tensor.transpose(ps[:, 2 + k % 2, m * P:(m + 1) * P],
                                                       prob[k % 2][:, m * P:(m + 1) * P], ident[:])
                        last.then_inc(sem("prob_transposed"), 1)
                    if h >= 2:
                        k = h - 2
                        pe.wait_ge(sem("probT_ready"), k + 1)
                        if k >= 2:
                            pe.wait_ge(sem("oT_ready"), k - 1)
                        cols = slice(k * DH, (k + 1) * DH)
                        mm(ps[:, 4 + k % 2, 0:P], v[:, 0, cols], probT[k % 2][:, 0, :], start=True, stop=True)
                        mm(ps[:, 4 + k % 2, P:S], v[:, 0, cols], probT[k % 2][:, 1, :], start=True, stop=False)
                        mm(ps[:, 4 + k % 2, P:S], v[:, 1, cols], probT[k % 2][:, 2, :], start=False, stop=True)\
                            .then_inc(sem("o_made"), 1)
                pe.wait_ge(sem("oT_ready"), HEADS)
                for s in range(NT * O_CHUNKS):
                    if s % NT == 0:
                        arrived(pe, O0 + s // NT)
                    rows(s, oT, s % NT, slot_of(O0 + s // NT)).then_inc(sem("proj_made"), 1)

            if moe:
                pe.wait_ge(sem("moe_xn"), NT)
                pe.wait_ge(sem("proj_copied"), 2 * NT)
                transposes(xn, "moe_transposed")
                pe.wait_ge(sem("moe_xT"), 4)
                for t in range(NT):
                    last = rows(4, xT, t, wr, n=E, at=t * E)
                last.then_inc(sem("logits"), 1)
                pe.wait_ge(sem("sel_ready"), 1)
                pe.wait_ge(sem("masks_ready"), 3)
                sel = rt[:, 5]
                mm(ps[:, 5, 0:E], tri[:], sel[:, 0, :], start=True, stop=True)
                mm(ps[:, 5, E:2 * E], ones[:], sel[:, 0, :], start=True, stop=False)
                mm(ps[:, 5, E:2 * E], tri[:], sel[:, 1, :], start=False, stop=True)
                mm(ps[:, 6, 0:E], ones[:], sel[:, 0, :], start=True, stop=False)
                mm(ps[:, 6, 0:E], ones[:], sel[:, 1, :], start=False, stop=True).then_inc(sem("places"), 1)

                def expert_chunk(i, kind, j):
                    n = MOE0 + ORDER.index((kind, j))
                    pe.wait_ge(landed[n % RING], 16 * (n // RING + 1) + i * (16 * PER_EXPERT // RING))
                    return down_slot(n) if kind == "w2" else slot_of(n)

                def gather(i, blocks):
                    pe.wait_ge(sem("onehot_ready"), NT * i + NT)
                    for b in range(blocks):
                        for kt in range(KT):
                            for t in range(NT):
                                last = mm(ps[:, 2 * b + kt // 4, (kt % 4) * P:(kt % 4 + 1) * P],
                                          xn[:, t, kt * P:(kt + 1) * P], onehot[:, t, b * P:(b + 1) * P],
                                          start=(t == 0), stop=(t == NT - 1))
                    last.then_inc(sem("gathered"), 1)

                def hidden(i, blocks):
                    one, last_s = BLOCKS // blocks, UNITS * blocks
                    pe.wait_ge(sem("xTe_ready"), (i + 1) * BLOCKS)
                    for s in range(last_s + 1):
                        j, b = divmod(s, blocks)
                        k = s - 1
                        if s < last_s:
                            if b == 0:
                                w1 = expert_chunk(i, "w1", j)
                            if s >= 2:
                                pe.wait_ge(sem("hidT_ready"), after_step(i, s - 2, blocks))
                            for kt in range(KT):
                                last = mm(ps[:, 2 * (s % 2), :], xTe[:, b, kt, :], w1[:, kt, :],
                                          start=(kt == 0), stop=(kt == KT - 1))
                            last.then_inc(sem("up1"), one)
                        if s >= 1:
                            pe.wait_ge(sem("hid_ready"), after_step(i, k, blocks))
                            for f in range(4):
                                last = nc.tensor.transpose(ps[:, 2 * (k % 2), f * P:(f + 1) * P],
                                                           hid[k % 2][:, f * P:(f + 1) * P], ident[:])
                            last.then_inc(sem("hid_T"), one)
                        if s < last_s:
                            if b == 0:
                                w3 = expert_chunk(i, "w3", j)
                            for kt in range(KT):
                                last = mm(ps[:, 2 * (s % 2) + 1, :], xTe[:, b, kt, :], w3[:, kt, :],
                                          start=(kt == 0), stop=(kt == KT - 1))
                            last.then_inc(sem("up3"), one)
                        if s >= 1:
                            jk, bk = divmod(k, blocks)
                            if bk == 0:
                                w2 = expert_chunk(i, "w2", jk)
                            pe.wait_ge(sem("hidT_ready"), after_step(i, k, blocks))
                            if k == 0:
                                pe.wait_ge(sem("added"), i * 4 + 4)
                            for f in range(4):
                                for half in range(2):
                                    last = mm(ps[:, 4 + 2 * bk + half, :], hidT[:, f, :],
                                              w2[:, f, half * BK:(half + 1) * BK],
                                              start=(jk == 0 and f == 0), stop=(jk == UNITS - 1 and f == 3))
                            last.then_inc(sem("down"), one)

                def combine(i, blocks):
                    pe.wait_ge(sem("y_rows"), i + 1)
                    pe.wait_ge(sem("weightedT_ready"), i + 1)
                    for q in range(4):
                        t, half = q // 2, q % 2
                        for b in range(blocks):
                            last = mm(ps[:, 4 + q, :], weightedT[:, b, t * P:(t + 1) * P],
                                      y_rows[:, b, half * BK:(half + 1) * BK], start=(b == 0), stop=(b == blocks - 1))
                        last.then_inc(sem("combined"), 1)

                pe.wait_ge(sem("routed"), 1)
                by_blocks(pe, 0, gather)
                with pe.Fori(0, E) as i:
                    pe.wait_ge(sem("xTe_ready"), (i + 1) * BLOCKS)
                    pe.wait_ge(sem("weighted_ready"), NT * i + NT)
                    for b in range(BLOCKS):
                        for t in range(NT):
                            last = nc.tensor.transpose(ps[:, 0, b * S + t * P:b * S + (t + 1) * P],
                                                       weighted[:, t, b * P:(b + 1) * P], ident[:])
                    last.then_inc(sem("weighted_T"), 1)
                    pe.wait_ge(sem("weightedT_ready"), i + 1)
                    by_blocks(pe, i, hidden)
                    by_blocks(pe, i + 1, gather)
                    by_blocks(pe, i, combine)


def kernel(**inputs):
    import numpy as _np
    import concourse.bacc as _bacc
    from concourse import mybir as _mybir
    from concourse.bass_utils import run_bass_kernel_spmd as _run

    nc = _bacc.Bacc("TRN2", target_bir_lowering=False, num_devices=1)
    arrays, args = {}, {}
    for name, value in lay_out(inputs).items():
        value = _np.ascontiguousarray(value)
        arrays[f"in_{name}"] = value
        args[name] = nc.dram_tensor(f"in_{name}", value.shape, _mybir.dt.from_np(value.dtype),
                                    kind="ExternalInput").ap()
    out = nc.dram_tensor("out_0", (1, S, D), F32, kind="ExternalOutput").ap()
    trunk(nc, args, out)
    r = _run(nc, [arrays], core_ids=[0])
    return r.results[0]["out_0"]
```

```python
from contextlib import ExitStack

import numpy as np

import concourse.bass as bass
from concourse import mybir

F32 = mybir.dt.float32
F32R = mybir.dt.float32r
I32 = mybir.dt.int32
ALU = mybir.AluOpType
ACT = mybir.ActivationFunctionType
AX_X = mybir.AxisListType.X

P = 128
D = 1024
S = 256
NT = S // P
KT = D // P
G, NSTATE, CH = 64, 64, 16
STEP = 8
NC = S // STEP
GB = 8
NB = G // GB
GQ = G // 4
HEADS, DH, ROT = 8, 128, 32
HALF = ROT // 2
FD = 2816
E, FE = 8, 3584
BK = 512
EPS = 1e-6
NEG = -1e30
INV_2PI = 0.15915494309189535
TWO_PI_HI = 6.28125
TWO_PI_LO = 0.0019353071795864769
ROUND = 12582912.0
PI_BELOW = 3.1415925
HALF_PI = 1.5707963267948966
CYCLE = 2 * PI_BELOW

RING = 7
SLOT = KT * BK
GLU_CHUNKS, KV_CHUNKS, Q_CHUNKS, O_CHUNKS = 4, 4, 2, 2
FULL = FD // BK
TAIL = FD - FULL * BK
UNITS = FE // BK
BLOCKS = S // P
STEPS = BLOCKS * UNITS
NPOW = 2 * STEP + 1
ARENA = 44572
INV_FREQ = [float(1.0 / f) for f in
            (np.float32(500000.0) ** (np.arange(HALF, dtype=np.float32) / np.float32(HALF)))]
STAGES = ["s5", "ffn", "attn", "all"]

RING = 7
SPLIT = 3
PIECE = 4 * BK
FULL = FD // BK
TAIL = FD - FULL * BK
UNITS = FE // BK
BLOCKS = S // P
STEPS = BLOCKS * UNITS
FFN_STEPS = NT * (FULL + 1)


def swiglu_pieces(units, tail):
    order = []
    for j in range(units + 1):
        if j < units:
            order += [("w1", j, 0), ("w1", j, 1)]
        if j >= 1:
            order += [("w2", j - 1, 0)] + [("w2", j - 1, 1)] * (not (tail and j == units))
        if j < units and not (tail and j == units - 1):
            order += [("w3", j, 0), ("w3", j, 1)]
    return order


GLU_ORDER = [(kind, n, k) for n in range(NT) for kind in ("value", "gate") for k in range(2)]
FFN_ORDER = swiglu_pieces(FULL + 1, True)
ORDER = swiglu_pieces(UNITS, False)
GLU0 = 0
FFN0 = GLU0 + len(GLU_ORDER)
KV0 = FFN0 + len(FFN_ORDER)
Q0 = KV0 + 2 * (2 * D // BK)
O0 = Q0 + 2 * (D // BK)
MOE0 = O0 + 2 * (D // BK)
PER_EXPERT = len(ORDER)
assert PER_EXPERT % RING == 0 and PER_EXPERT % SPLIT == 0


def wait(eng, sem, value):
    if not isinstance(value, int) or value > 0:
        eng.wait_ge(sem, value)


class Chain:

    def __init__(self, eng, sem):
        self.eng, self.sem, self.n, self.extra = eng, sem, 0, 0

    def __call__(self, ins):
        ins.then_inc(self.sem, 1)
        self.n += 1
        self.eng.wait_ge(self.sem, self.n + self.extra)


def lay_out(inputs):
    a = {k: np.asarray(v) for k, v in inputs.items()}
    a["positions"] = a["positions"].reshape(NT, P).T
    a["norm_cols"] = a["norms"].reshape(8, KT, P).transpose(2, 0, 1)
    a["kv_norm"] = a["kv_norm"].reshape(KT, P).T
    a["moe_router"] = a["moe_router"].reshape(KT, P, E).transpose(1, 0, 2)
    a["lam_re"], a["lam_im"] = a.pop("s5_lam_re")[0].T, a.pop("s5_lam_im")[0].T
    for k in ("re", "im"):
        a["b_" + k] = a.pop("s5_b_" + k)[0].transpose(1, 0, 2)
        a["c_" + k] = a.pop("s5_c_" + k)[0].transpose(2, 0, 1)
    return a


def trunk(nc, a, out, until="all"):
    ctx = ExitStack()
    with ctx:
        def sb(name, shape, dt=F32):
            return ctx.enter_context(nc.sbuf_tensor(name, shape, dt))

        sems = {}

        def sem(name):
            if name not in sems:
                sems[name] = ctx.enter_context(nc.semaphore(name))
            return sems[name]

        x = sb("x", [P, NT, D])
        xn = sb("xn", [P, NT, D])
        gain_a = sb("gain_a", [P, D])
        gain_b = sb("gain_b", [P, D])
        ident = sb("ident", [P, P])
        swap = sb("swap", [P, P])
        tri = sb("tri", [P, P])
        ones = sb("ones", [P, P])
        iota_c = sb("iota_c", [P, S])
        mask = sb("mask", [P, P])
        powers = sb("powers", [P, NPOW])
        gcol = sb("gcol", [P, 8, KT])
        kvcol = sb("kvcol", [P, KT])
        ss = sb("ss", [P, NT])
        sd = sb("sd", [P, NT])
        rstd = sb("rstd", [P, NT])
        const = sb("const", [P, 3])
        wr = sb("wr", [P, KT, E])
        rbias = sb("rbias", [P, E])
        rt = sb("rt", [P, 9, NT, E])
        rs = sb("rs", [P, 8, NT])
        slot = sb("slot", [P, NT, E + 1])
        wgt = sb("wgt", [P, NT, E + 1])
        count = sb("count", [P, E + 1], I32)
        posi = sb("posi", [P, NT], I32)
        posf = sb("posf", [P, NT])
        freq = sb("freq", [P, HALF])
        rope_sin = sb("rope_sin", [P, NT * HALF])
        rope_cos = sb("rope_cos", [P, NT * HALF])
        rope_tmp = sb("rope_tmp", [P, NT * HALF])
        small = sb("small", [P, 14, G])
        with nc.sbuf_tensor("s5_ring", [P, 28672], F32) as ring, nc.sbuf_tensor("s5_work", [P, 15900], F32) as work:
            pass
        raw = sb("raw", [P, RING, PIECE])
        high = sb("high", [P, SPLIT, PIECE], F32R)
        low = sb("low", [P, SPLIT, PIECE], F32R)
        xT_hi = sb("xT_hi", [P, KT * S], F32R)
        xT_lo = sb("xT_lo", [P, KT * S], F32R)
        hidT_hi = sb("hidT_hi", [P, BLOCKS, 4, P], F32R)
        hidT_lo = sb("hidT_lo", [P, BLOCKS, 4, P], F32R)
        mix_at = sb("mix", [P, NT * D])
        late = sb("late", [P, 7900])
        ps = ctx.enter_context(nc.psum_tensor("ps", [P, 8, BK], F32))

        def view(buf, at, *shape):
            n = 1
            for k in shape:
                n *= k
            if len(shape) == 1:
                return buf[:, at:at + n]
            names = "abcd"[:len(shape)]
            return buf[:, at:at + n].rearrange(f"p ({' '.join(names)}) -> p {' '.join(names)}",
                                               **{names[i]: shape[i] for i in range(1, len(shape))})

        mix = view(mix_at, 0, NT, D)
        SLOT = 4096
        cr, ci, br, bi = (view(ring, 1024 * k, G, CH) for k in range(4))
        bbr, bbi = (view(ring, SLOT + 1024 * k, G, CH) for k in range(2))
        bstk = view(ring, 2 * SLOT + 19456, G, CH)
        ca = view(ring, 2 * SLOT, G, STEP + 1, CH)
        vtok = ring[0:NC, 2 * SLOT + 9216:2 * SLOT + 9216 + STEP * D].rearrange("p (l d) -> p l d", l=STEP)
        vgrp = ring[0:NC, 2 * SLOT:2 * SLOT + STEP * D].rearrange("p (g l i) -> p g l i", l=STEP, i=CH)
        toep = view(ring, 2 * SLOT + 9216, G, P)
        cos_c = view(ring, 2 * SLOT + 17408, G, NC)
        useq = view(work, 0, G, NC)
        sin_c = view(work, 2048, G, NC)
        decay = view(work, 4096, G, NC)
        sprev = view(work, 6144, G, NC + 1)
        xx, yy = (view(work, 8256 + 576 * k, STEP + 1, G) for k in range(2))
        xx2, yy2 = (view(work, 9408 + 512 * k, STEP, G) for k in range(2))
        ang, mag, cosn, sinn, tmpn = (view(work, 10432 + 1088 * k, NPOW, G) for k in range(5))
        prod = [work[:, 4096 + 1152 * k:4096 + 1152 * (k + 1)] for k in range(2)]
        ba = [view(work, 10432 + 1024 * k, GB, P) for k in range(2)]
        wint = [view(work, 12480 + 1024 * k, GB, P) for k in range(2)]
        taps = [view(work, 10432, G // 2, P), view(ring, SLOT, G // 2, P)]
        state, bsum = view(ring, 0, G, NC), view(ring, 2048, G, NC)
        sums = view(ring, SLOT, G // 4, P)
        ytile = view(work, 10304, STEP, GQ, CH)
        xT = [t[:].rearrange("p (k s) -> p k s", s=S) for t in (xT_hi, xT_lo)]
        hidT = [hidT_hi, hidT_lo]
        tmpT = view(late, 2048, KT, S)
        gate_sb = [view(late, 512 * k, BK) for k in range(2)]
        hid = [view(late, 1024 + 512 * k, BK) for k in range(2)]
        kT, qT, v = view(late, 0, HEADS, S), tmpT, view(late, 4096, NT, D)
        probT = [view(late, 6144 + 384 * k, 3, P) for k in range(2)]
        rot = [view(late, 6912 + 64 * k, 4, HALF) for k in range(4)]
        soft = view(late, 7168, HEADS, 4, NT)
        att = [view(mix_at, 384 * k, 384) for k in range(2)]
        prob = [view(mix_at, 768 + 384 * k, 384) for k in range(2)]
        acc = mix
        xTe = [t[:].rearrange("p (b k s) -> p b k s", b=BLOCKS, s=P) for t in (xT_hi, xT_lo)]
        tmpTe = view(late, 2048, BLOCKS, KT, P)
        y_rows = view(late, 4096, BLOCKS, D)
        onehot = view(late, 6144, NT, S)
        weighted = view(late, 6656, NT, S)
        weightedT = view(late, 7168, BLOCKS, S)

        def bcast_last(ap, n):
            return ap.rearrange("p (k o) -> p k o", o=1).broadcast_to([P, ap.shape[1], n])

        def bcast_mid(ap, n):
            return ap.rearrange("p (o k) -> p o k", o=1).broadcast_to([P, n, ap.shape[1]])

        def by_blocks(eng, i, steps):
            tokens = eng.value_load(count[0:1, bass.ds(i, 1)], min_val=0, max_val=S)
            with eng.If(tokens > P):
                steps(i, 2)
            with eng.Else():
                steps(i, 1)

        def after(base, j, b, blocks):
            return base + BLOCKS * j + (b + 1) * (BLOCKS // blocks)

        landed = [sem(f"piece_landed_{k}") for k in range(RING)]

        def piece(buf, n, down=False):
            return buf.rearrange("p (k n) -> p k n", k=2 if down else 4)

        def split_of(n, down=False):
            return [piece(t[:, n % SPLIT, :], n, down) for t in (high, low)]

        TAIL_PIECES = [FFN0 + c for c, (kind, j, k) in enumerate(FFN_ORDER) if kind == "w1" and j == FULL]

        def width(order, j, units):
            return TAIL if order is FFN_ORDER and j == units - 1 else BK

        class Splitter:

            def __init__(self, make, at, end):
                self.make, self.at, self.end = make, at, end

            def upto(self, n):
                for k in range(self.at, min(n, self.end)):
                    self.make(k, 0)
                self.at = max(self.at, min(n, self.end))

        def expert_pieces(make, i):
            walk = Splitter(lambda k, _: make(k, i), MOE0 + SPLIT, MOE0 + PER_EXPERT + SPLIT)
            return walk

        stop = STAGES.index(until)
        ffn, attn, moe = stop >= 1, stop >= 2, stop >= 3
        END = [FFN0, KV0, MOE0, MOE0 + SPLIT][stop]

        block = ctx.enter_context(nc.Block())

        @block.sync
        def _(sp):
            sp.dma_start(x[:], a["x"].rearrange("b (t p) d -> p (b t) d", p=P)).then_inc(sem("x_in"), 16)
            sp.dma_start(gain_a[:], a["norms"][0, 0:1, :].broadcast_to([P, D])).then_inc(sem("gain_a_in"), 16)
            for half in range(2):
                rows = slice(64 * half, 64 * half + 64)
                sp.dma_start(small[rows, 0, :], a["lam_re"]).then_inc(sem("lam_in"), 16)
                sp.dma_start(small[rows, 1, :], a["lam_im"]).then_inc(sem("lam_in"), 16)
            sp.dma_start(small[:, 2, :], a["s5_log_dt"].broadcast_to([P, G])).then_inc(sem("lam_in"), 16)
            sp.dma_start(posi[:], a["positions"]).then_inc(sem("pos_in"), 16)
            for name, dst in (("b_re", br), ("b_im", bi), ("c_re", cr), ("c_im", ci)):
                for half in range(2):
                    sp.dma_start(dst[64 * half:64 * half + 64], a[name]).then_inc(sem("bc_in"), 16)
            sp.dma_start(gain_b[:], a["s5_d"].broadcast_to([P, D])).then_inc(sem("gain_b_in"), 16)
            sp.dma_start(gcol[:], a["norm_cols"]).then_inc(sem("const_in"), 16)
            sp.dma_start(kvcol[:], a["kv_norm"]).then_inc(sem("const_in"), 16)
            sp.dma_start(wr[:], a["moe_router"]).then_inc(sem("const_in"), 16)
            sp.dma_start(rbias[:], a["moe_bias"].broadcast_to([P, E])).then_inc(sem("const_in"), 16)

            for t in range(NT):
                sp.wait_ge(sem("h_ready"), t + 1)
                sp.dma_start(vtok[t * NC // NT:(t + 1) * NC // NT], xn[:, t, :]).then_inc(sem("v_in"), 16)
            sp.wait_ge(sem("toep_zero"), 1)
            for half in range(2):
                sp.wait_ge(sem("taps_ready"), NB // 2 * (half + 1))
                gs = slice(half * (G // 2), (half + 1) * (G // 2))
                for m in range(STEP):
                    sp.dma_start(toep[CH * m:CH * (m + 1), gs, CH * m:P],
                                 taps[half][0:CH, :, 0:P - CH * m]).then_inc(sem("toep_in"), 16)

            def load(n, src, down=False, cols=BK):
                if n >= RING:
                    sp.wait_ge(sem("low_ready"), n - RING + 1)
                dst = piece(raw[:, n % RING, :], n, down)
                sp.dma_start(dst[:, :, 0:cols] if cols < BK else dst, src).then_inc(landed[n % RING], 16)

            def up_rows(w, k):
                return w.rearrange("(k p) n -> p k n", p=P)[:, 4 * k:4 * k + 4, :]

            def down_rows(w, j, k):
                at = j * BK + k * 2 * P
                return w[at:at + 2 * P, :].rearrange("(k p) n -> p k n", p=P)

            def glu(n):
                kind, block, k = GLU_ORDER[n]
                at = (kind == "gate") * D + block * BK
                load(GLU0 + n, up_rows(a["s5_w_glu"][0], k)[:, :, at:at + BK])

            sp.wait_ge(sem("toep_in"), 16 * 2 * STEP)
            sp.wait_ge(sem("states_ready"), 1)
            for n in range(4):
                glu(n)
            sp.wait_ge(sem("y_copied"), 1)
            for t in range(NT):
                for q in range(4):
                    rows = slice(q * NC + t * NC // NT, q * NC + (t + 1) * NC // NT)
                    sp.dma_start(mix[:, t, q * D // 4:(q + 1) * D // 4],
                                 ytile[rows].rearrange("c l g i -> c l (g i)")).then_inc(sem(f"y_in_{t}"), 16)
            for n in range(4, len(GLU_ORDER)):
                glu(n)
            if ffn:
                for c, (kind, j, k) in enumerate(FFN_ORDER):
                    n = FFN0 + c
                    if kind == "w2":
                        load(n, down_rows(a["ffn_w2"][0], j, k), down=True)
                    elif j < FULL:
                        load(n, up_rows(a["ffn_" + kind][0], k)[:, :, j * BK:(j + 1) * BK])
                    else:
                        load(n, up_rows(a["ffn_w1"][0], k)[:, :, FULL * BK:FD], cols=TAIL)
                        sp.dma_start(piece(raw[:, n % RING, :], n)[:, :, TAIL:2 * TAIL],
                                     up_rows(a["ffn_w3"][0], k)[:, :, FULL * BK:FD]).then_inc(sem("ffn_tail"), 16)
            if attn:
                for first, end, w in ((KV0, Q0, a["w_kv"]), (Q0, O0, a["w_q"][0]), (O0, MOE0, a["w_o"][0])):
                    for n in range(first, end):
                        c, k = divmod(n - first, 2)
                        load(n, up_rows(w, k)[:, :, c * BK:(c + 1) * BK])
            if moe:
                with sp.Fori(0, E) as i:
                    for c, (kind, j, k) in enumerate(ORDER):
                        n = MOE0 + c
                        w = a[f"moe_{kind}"][0, bass.ds(i, 1)]
                        if kind == "w2":
                            at = j * BK + k * 2 * P
                            src = w[:, at:at + 2 * P, :]
                        else:
                            src = w[:, 4 * k * P:4 * (k + 1) * P, j * BK:(j + 1) * BK]
                        sp.wait_ge(sem("low_ready"), i * PER_EXPERT + n - RING + 1)
                        sp.dma_start(piece(raw[:, n % RING, :], n, kind == "w2"),
                                     src.rearrange("o (k p) n -> p (o k) n", p=P)).then_inc(landed[n % RING], 16)
            sp.wait_ge(sem("x_final"), NT)
            sp.dma_start(out.rearrange("b (t p) d -> p (b t) d", p=P), x[:]).then_inc(sem("stored"), 16)
            sp.wait_ge(sem("stored"), 16)

        @block.gpsimd
        def _(pool):
            chain = Chain(pool, sem("pool_chain"))
            nc.gpsimd.memset(const[:, 0:1], EPS).then_inc(sem("eps_set"), 1)
            nc.gpsimd.memset(const[:, 1:2], HALF_PI).then_inc(sem("eps_set"), 1)
            nc.gpsimd.memset(const[:, 2:3], 0.0).then_inc(sem("eps_set"), 1)
            nc.gpsimd.iota(powers[:, 0:STEP + 1], [[1, STEP + 1]], base=0, channel_multiplier=0,
                           allow_small_or_imprecise_dtypes=True).then_inc(sem("iotas"), 1)
            nc.gpsimd.iota(powers[:, STEP + 1:NPOW], [[-1, STEP]], base=STEP - 1, channel_multiplier=0,
                           allow_small_or_imprecise_dtypes=True).then_inc(sem("iotas"), 1)
            nc.gpsimd.iota(iota_c[:], [[1, S]], base=0, channel_multiplier=0,
                           allow_small_or_imprecise_dtypes=True).then_inc(sem("iotas"), 1)
            for k in range(HALF):
                nc.gpsimd.memset(freq[:, k:k + 1], INV_FREQ[k]).then_inc(sem("iotas"), 1)
            chain(nc.gpsimd.memset(ident[:], 0.0))
            nc.gpsimd.affine_select(out=ident[:], in_=ident[:], compare_op=ALU.not_equal, fill=1.0, base=0,
                                    pattern=[[-1, P]], channel_multiplier=1).then_inc(sem("ident_ready"), 1)
            chain(nc.gpsimd.memset(swap[:], 0.0))
            chain(nc.gpsimd.affine_select(out=swap[:], in_=swap[:], compare_op=ALU.not_equal, fill=1.0,
                                          base=-64, pattern=[[-1, P]], channel_multiplier=1))
            nc.gpsimd.affine_select(out=swap[:], in_=swap[:], compare_op=ALU.not_equal, fill=-1.0,
                                    base=64, pattern=[[-1, P]], channel_multiplier=1)\
                .then_inc(sem("swap_ready"), 1)
            nc.gpsimd.memset(ones[:], 1.0).then_inc(sem("masks_ready"), 1)
            chain(nc.gpsimd.memset(tri[:], 1.0))
            nc.gpsimd.affine_select(out=tri[:], in_=tri[:], compare_op=ALU.is_gt, fill=0.0, base=0,
                                    pattern=[[1, P]], channel_multiplier=-1).then_inc(sem("masks_ready"), 1)
            chain(nc.gpsimd.memset(mask[:], 0.0))
            nc.gpsimd.affine_select(out=mask[:], in_=mask[:], compare_op=ALU.is_ge, fill=NEG, base=0,
                                    pattern=[[-1, P]], channel_multiplier=1).then_inc(sem("masks_ready"), 1)

            pool.wait_ge(sem("iotas"), 3 + HALF)
            pool.wait_ge(sem("r8_ready"), 1)
            chain(nc.gpsimd.tensor_tensor(sin_c, bcast_last(small[:, 6, :], NC), bcast_mid(iota_c[:, 0:NC], G),
                                          ALU.mult))
            chain(nc.gpsimd.tensor_scalar(cos_c, sin_c, ROUND, None, ALU.add))
            chain(nc.gpsimd.tensor_scalar(cos_c, cos_c, -ROUND, None, ALU.add))
            nc.gpsimd.tensor_tensor(sin_c, sin_c, cos_c, ALU.subtract).then_inc(sem("phi_ready"), 1)

            pool.wait_ge(sem("tables_ready"), 1)
            for b in range(2 * NB):
                g = slice((b % NB) * GB, (b % NB + 1) * GB)
                if b >= 2:
                    pool.wait_ge(sem("summed"), b - 1)
                left, right, n = (bbi, yy2, STEP) if b < NB else (ci, yy, STEP + 1)
                dst = prod[b % 2][:, 0:GB * n * CH].rearrange("p (g n i) -> p g n i", n=n, i=CH)
                nc.gpsimd.tensor_tensor(
                    dst, left[:, g, :].rearrange("p g (o i) -> p g o i", o=1).broadcast_to([P, GB, n, CH]),
                    right[:, :, g].rearrange("p n (g o) -> p g n o", o=1).broadcast_to([P, GB, n, CH]),
                    ALU.mult).then_inc(sem("product"), 1)

            def gain(buf, name, row, after):
                pool.wait_ge(sem(after), NT)
                pool.dma_start(buf[:], row.broadcast_to([P, D])).then_inc(sem(name), 16)

            gain(gain_a, "gain_1_in", a["norms"][0, 1:2, :], "h_ready")
            if ffn:
                gain(gain_b, "gain_2_in", a["norms"][0, 3:4, :], "gelu_in")
            if attn:
                gain(gain_a, "gain_3_in", a["norms"][1, 1:2, :], "added_0")
            if moe:
                gain(gain_b, "gain_4_in", a["norms"][1, 3:4, :], "added_1")

        @block.scalar
        def _(act):
            chain = Chain(act, sem("act_chain"))

            def spread(src, name):
                act.wait_ge(sem("eps_set"), 3)
                for t in range(NT):
                    nc.scalar.activation(xn[:, t, :], src[:, t, :], ACT.Square, accum_out=ss[:, t:t + 1])\
                        .then_inc(sem("squared"), 1)
                spread.n += NT
                act.wait_ge(sem("squared"), spread.n)
                nc.scalar.activation(sd[:], ss[:], ACT.Sqrt, bias=const[:, 0:1], scale=1.0 / D)\
                    .then_inc(sem("root"), 1)
            spread.n = 0

            def make_high(n, i):
                act.wait_ge(landed[n % RING], 16 * (n // RING + 1) + i * (16 * PER_EXPERT // RING))
                if n in TAIL_PIECES:
                    act.wait_ge(sem("ffn_tail"), 32)
                if n >= SPLIT:
                    act.wait_ge(sem("used"), i * PER_EXPERT + n - SPLIT + 1)
                nc.scalar.activation(high[:, n % SPLIT, :], raw[:, n % RING, :], ACT.Copy)\
                    .then_inc(sem("high_ready"), 1)

            pieces = Splitter(make_high, 0, END)

            def high_of_xT(name):
                for b in range(4):
                    act.wait_ge(sem(name + "_v"), b + 1)
                    high_of(tmpT[:, 2 * b:2 * b + 2, :], xT[0][:, 2 * b:2 * b + 2, :], name + "_high")

            def used(n, i=0):
                act.wait_ge(sem("used"), i * PER_EXPERT + n + 1)

            def high_of(src, dst, ready):
                nc.scalar.activation(dst, src, ACT.Copy).then_inc(sem(ready), 1)

            def swiglu(base, i, walk, order, at0, units, blocks, before_last_T=None):
                one, at = BLOCKS // blocks, {q: at0 + c for c, q in enumerate(order)}
                end = at0 + len(order)
                for j in range(units + 1):
                    if j >= 1:
                        walk.upto(min(at[("w1", j, 0)] + SPLIT if j < units else end, end))
                        if j == units and before_last_T:
                            before_last_T()
                        for b in range(blocks):
                            act.wait_ge(sem("hid_T"), after(base, j - 1, b, blocks))
                            m = width(order, j - 1, units) // P
                            if b == 0 and j >= 2:
                                used(at[("w2", j - 2, 1)], i)
                            nc.scalar.activation(hidT_hi[:, b, 0:m, :], ps[:, 2 + b, 0:m * P]
                                                 .rearrange("p (m s) -> p m s", m=m), ACT.Copy)\
                                .then_inc(sem("hidT_hi"), one)
                    if j < units:
                        walk.upto(min(at[("w1", j, 1)] + SPLIT, end))
                        used(at[("w1", j, 1)], i)
                        w = width(order, j, units)
                        for b in range(blocks):
                            if j >= 1:
                                act.wait_ge(sem("hid_ready"), after(base, j - 1, b, blocks))
                            nc.scalar.activation(gate_sb[b][:, 0:w], ps[:, b, 0:w], ACT.Silu)\
                                .then_inc(sem("gate_ready"), one)
                walk.upto(end)

            act.wait_ge(sem("x_in"), 16)
            spread(x, "s5")
            act.wait_ge(sem("lam_in"), 80)
            nc.scalar.activation(small[:, 2, :], small[:, 2, :], ACT.Exp).then_inc(sem("dt_ready"), 1)
            act.wait_ge(sem("mag_in"), 1)
            nc.scalar.activation(mag, mag, ACT.Exp).then_inc(sem("mag_ready"), 1)
            nc.scalar.activation(small[:, 7, :], small[:, 7, :], ACT.Exp).then_inc(sem("mag_ready"), 1)
            def trig(src, sin, cos, tmp, unit, ready, done):
                act.wait_ge(sem(ready), 1)
                chain(nc.scalar.activation(tmp, src, ACT.Abs))
                nc.scalar.activation(sin, src, ACT.Sin, scale=unit).then_inc(sem(done), 1)
                nc.scalar.activation(cos, tmp, ACT.Sin, bias=const[:, 1:2], scale=-unit).then_inc(sem(done), 1)

            trig(ang, sinn, cosn, tmpn, CYCLE, "ang_ready", "trig_ready")
            trig(rope_sin[:], rope_sin[:], rope_cos[:], rope_tmp[:], 1.0, "rope_ready", "rope_done")
            act.wait_ge(sem("v_in"), 16 * NT)
            nc.scalar.activation(vgrp.rearrange("p g l i -> p l g i"),
                                 vtok.rearrange("p l (g i) -> p l g i", i=CH), ACT.Copy)\
                .then_inc(sem("v_grouped"), 1)
            act.wait_ge(sem("v_grouped"), 1)
            nc.scalar.activation(toep, const[:, 2:3].rearrange("p (g m) -> p g m", g=1).broadcast_to([P, G, P]),
                                 ACT.Copy).then_inc(sem("toep_zero"), 1)
            act.wait_ge(sem("u_transposed"), 1)
            nc.scalar.activation(useq, ps[:, 0:4, :].rearrange("p b (g c) -> p (b g) c", c=NC), ACT.Copy)\
                .then_inc(sem("useq_ready"), 1)
            trig(sin_c, sin_c, cos_c, cos_c, CYCLE, "phi_ready", "turn_ready")
            for b in range(NB):
                act.wait_ge(sem("ba_transposed"), b + 1)
                if b >= 2:
                    act.wait_ge(sem("chunk_sums"), b - 1)
                nc.scalar.activation(wint[b % 2], ps[:, 2 * (b % 2):2 * (b % 2) + 2, :]
                                     .rearrange("p b (g m) -> p (b g) m", m=P), ACT.Copy)\
                    .then_inc(sem("wint_ready"), 1)
            act.wait_ge(sem("chunk_sums"), NB)
            nc.scalar.activation(sums, ps[:, 4:8, :].rearrange("p b (k m) -> p (b k) m", m=P), ACT.Copy)\
                .then_inc(sem("sums_copied"), 1)
            for b in range(NB):
                if b == 2:
                    act.wait_ge(sem("sums_T"), 1)
                    nc.scalar.activation(bsum, ps[:, 4:8, :].rearrange("p b (g c) -> p (b g) c", c=NC), ACT.Copy)\
                        .then_inc(sem("bsum_ready"), 1)
                act.wait_ge(sem("taps_made"), b + 1)
                half, at = b // (NB // 2), (b % (NB // 2)) * GB
                nc.scalar.activation(taps[half][0:CH, at:at + GB, :], ps[0:CH, 2 * (b % 2):2 * (b % 2) + 2, :]
                                     .rearrange("p b (g m) -> p (b g) m", m=P), ACT.Copy)\
                    .then_inc(sem("taps_ready"), 1)
            act.wait_ge(sem("y_made"), 1)
            nc.scalar.activation(ytile.rearrange("p l g i -> p g l i"),
                                 ps[:, 0:4, :].rearrange("p b (g l i) -> p (b g) l i", l=STEP, i=CH), ACT.Copy)\
                .then_inc(sem("y_copied"), 1)
            act.wait_ge(sem("gelu_in"), NT)
            for t in range(NT):
                nc.scalar.activation(xn[:, t, :], mix[:, t, :], ACT.Gelu_apprx_tanh).then_inc(sem("g_ready"), 1)
            pieces.upto(GLU0 + SPLIT)
            for b in range(4):
                act.wait_ge(sem("g_transposed"), b + 1)
                high_of(ps[:, b, :].rearrange("p (k s) -> p k s", k=2), xT[0][:, 2 * b:2 * b + 2, :], "g_high")
            for n in range(NT):
                pieces.upto(4 * n + 3 + SPLIT)
                used(4 * n + 3)
                for t in range(NT):
                    if n >= 1:
                        act.wait_ge(sem("glu_out"), NT * (n - 1) + t + 1)
                    nc.scalar.activation(gate_sb[t], ps[:, 4 * n + 2 + t, :], ACT.Sigmoid)\
                        .then_inc(sem("glu_sig"), 1)
            act.wait_ge(sem("glu_out"), NT * NT)
            spread(mix, "post")

            if ffn:
                act.wait_ge(sem("added_0"), NT)
                spread(x, "ffn")
                high_of_xT("ffn")
                swiglu(0, 0, pieces, FFN_ORDER, FFN0, FULL + 1, NT)
                used(KV0 - 1)
                for t in range(NT):
                    nc.scalar.activation(mix[:, t, :], ps[:, 4 + 2 * t:6 + 2 * t, :]
                                         .rearrange("p b n -> p (b n)"), ACT.Copy).then_inc(sem("ffn_copied"), 1)
                act.wait_ge(sem("ffn_copied"), NT)
                spread(mix, "post")

            if attn:
                act.wait_ge(sem("added_1"), NT)
                spread(x, "attn")

                def heads(bank, dst, name):
                    nc.scalar.activation(dst, ps[:, bank, :], ACT.Copy).then_inc(sem(name), 1)

                high_of_xT("kv")
                for c in range(4):
                    pieces.upto(KV0 + 2 * c + 1 + SPLIT)
                    used(KV0 + 2 * c + 1)
                    for t in range(NT):
                        if c < 2:
                            heads(2 * c + t, mix[:, t, c * BK:(c + 1) * BK], "k_copied")
                        else:
                            nc.scalar.activation(v[:, t, (c - 2) * BK:(c - 1) * BK], ps[:, 2 * c + t, :], ACT.Copy)\
                                .then_inc(sem("v_copied"), 1)
                high_of_xT("q")
                for b in range(4):
                    act.wait_ge(sem("k_transposed"), b + 1)
                    nc.scalar.activation(kT[:, 2 * b:2 * b + 2, :], ps[:, 4 + b, :]
                                         .rearrange("p (k s) -> p k s", k=2), ACT.Copy).then_inc(sem("kT_ready"), 1)
                for c in range(2):
                    pieces.upto(Q0 + 2 * c + 1 + SPLIT)
                    used(Q0 + 2 * c + 1)
                    for t in range(NT):
                        heads(2 * c + t, mix[:, t, c * BK:(c + 1) * BK], "q_copied")
                for b in range(4):
                    act.wait_ge(sem("q_transposed"), b + 1)
                    nc.scalar.activation(qT[:, 2 * b:2 * b + 2, :], ps[:, 4 + b, :]
                                         .rearrange("p (k s) -> p k s", k=2), ACT.Copy).then_inc(sem("qT_ready"), 1)
                pieces.upto(O0 + SPLIT)
                for h in range(HEADS + 2):
                    if h < HEADS:
                        act.wait_ge(sem("score_max"), h + 1)
                        if h >= 2:
                            act.wait_ge(sem("prob_transposed"), h - 1)
                        for t in range(NT):
                            cols = slice(0, P) if t == 0 else slice(P, 3 * P)
                            nc.scalar.activation(prob[h % 2][:, cols], att[h % 2][:, cols], ACT.Exp,
                                                 bias=soft[:, h, 1, t:t + 1], accum_out=soft[:, h, 2, t:t + 1])\
                                .then_inc(sem("exped"), 1)
                    if h >= 2:
                        k = h - 2
                        act.wait_ge(sem("o_made"), k + 1)
                        high_of(ps[:, 4 + k % 2, 0:S], xT[0][:, k, :], "o_high")
                    if 1 <= h <= HEADS:
                        k = h - 1
                        act.wait_ge(sem("prob_transposed"), k + 1)
                        if k >= 2:
                            act.wait_ge(sem("o_made"), k - 1)
                        nc.scalar.activation(probT[k % 2], ps[:, 2 + k % 2, 0:384]
                                             .rearrange("p (m s) -> p m s", m=3), ACT.Copy)\
                            .then_inc(sem("probT_ready"), 1)
                for c in range(2):
                    pieces.upto(O0 + 2 * c + 1 + SPLIT)
                    used(O0 + 2 * c + 1)
                    for t in range(NT):
                        nc.scalar.activation(mix[:, t, c * BK:(c + 1) * BK], ps[:, 2 * c + t, :], ACT.Copy)\
                            .then_inc(sem("proj_copied"), 1)
                act.wait_ge(sem("proj_copied"), 2 * NT)
                spread(mix, "post")
                pieces.upto(MOE0 + SPLIT)

            if moe:
                act.wait_ge(sem("added_2"), NT)
                spread(x, "moe")

                def high_of_expert(b):
                    def steps(i, blocks):
                        if b < blocks:
                            act.wait_ge(sem("expert_v"), after(i * BLOCKS, 0, b, blocks))
                            nc.scalar.activation(xTe[0][:, b], tmpTe[:, b], ACT.Copy)\
                                .then_inc(sem("expert_high"), BLOCKS // blocks)
                    return steps

                def hidden(i, blocks):
                    walk = expert_pieces(make_high, i)
                    swiglu(i * STEPS + FFN_STEPS, i, walk, ORDER, MOE0, UNITS, blocks,
                           lambda: by_blocks(act, i + 1, high_of_expert(0)))
                    with act.If(i < E - 1):
                        walk.upto(MOE0 + PER_EXPERT + 2)
                    used(MOE0 + PER_EXPERT - 1, i)
                    nc.scalar.activation(y_rows[:, 0:blocks, :], ps[:, 4:4 + 2 * blocks, :]
                                         .rearrange("p (t b) n -> p t (b n)", b=2), ACT.Copy)\
                        .then_inc(sem("y_rows"), 1)
                    with act.If(i < E - 1):
                        walk.upto(MOE0 + PER_EXPERT + SPLIT)

                act.wait_ge(sem("gap_ready"), 1)
                nc.scalar.activation(rs[:, 4, :], rs[:, 4, :], ACT.Exp).then_inc(sem("gap_exp"), 1)
                act.wait_ge(sem("routed"), 1)
                for b in range(BLOCKS):
                    by_blocks(act, 0, high_of_expert(b))
                with act.Fori(0, E) as i:
                    act.wait_ge(sem("weighted_T"), i + 1)
                    nc.scalar.activation(weightedT, ps[:, 3, :].rearrange("p (t s) -> p t s", t=BLOCKS), ACT.Copy)\
                        .then_inc(sem("weightedT_ready"), 1)
                    by_blocks(act, i, hidden)
                    by_blocks(act, i + 1, high_of_expert(1))
                act.wait_ge(sem("acc_done"), 1)
                spread(acc, "post")

        @block.vector
        def _(dve):
            chain = Chain(dve, sem("dve_chain"))
            rooted = [0]
            TT, TS, STT = nc.vector.tensor_tensor, nc.vector.tensor_scalar, nc.vector.scalar_tensor_tensor

            def inverse_root():
                rooted[0] += 1
                dve.wait_ge(sem("root"), rooted[0])
                chain(nc.vector.reciprocal(rstd[:], sd[:]))

            def reduce_angle(v, tmp):
                chain(TS(tmp, v, INV_2PI, ROUND, ALU.mult, ALU.add))
                chain(TS(tmp, tmp, -ROUND, None, ALU.add))
                chain(STT(out=v, in0=tmp, scalar=-TWO_PI_HI, in1=v, op0=ALU.mult, op1=ALU.add))
                chain(STT(out=v, in0=tmp, scalar=-TWO_PI_LO, in1=v, op0=ALU.mult, op1=ALU.add))
                return TS(v, v, PI_BELOW, -PI_BELOW, ALU.min, ALU.max)

            def less_integer(v, tmp):
                chain(TS(tmp, v, ROUND, None, ALU.add))
                chain(TS(tmp, tmp, -ROUND, None, ALU.add))
                return TT(v, v, tmp, ALU.subtract)

            inverse_root()
            dve.wait_ge(sem("gain_a_in"), 16)
            for t in range(NT):
                STT(out=xn[:, t, :], in0=x[:, t, :], scalar=rstd[:, t:t + 1], in1=gain_a[:],
                    op0=ALU.mult, op1=ALU.mult).then_inc(sem("h_ready"), 1)
            sm = [small[:, k, :] for k in range(14)]
            lr, li, dt, zr, zi, tmp, r8, m8, den, am1, cfr, cfi, t1, t2 = sm
            dve.wait_ge(sem("dt_ready"), 1)
            dve.wait_ge(sem("iotas"), 3 + HALF)
            chain(TT(zr, lr, dt, ALU.mult))
            chain(TT(zi, li, dt, ALU.mult))
            chain(TS(m8, zr, float(STEP), None, ALU.mult))
            TT(mag, bcast_mid(zr, NPOW), bcast_last(powers[:], G), ALU.mult).then_inc(sem("mag_in"), 1)
            chain(reduce_angle(zi, tmp))
            chain(TS(zi, zi, INV_2PI, None, ALU.mult))
            chain(TT(ang, bcast_mid(zi, NPOW), bcast_last(powers[:], G), ALU.mult))
            less_integer(ang, tmpn).then_inc(sem("ang_ready"), 1)
            chain(TS(r8, zi, float(STEP), None, ALU.mult))
            less_integer(r8, tmp).then_inc(sem("r8_ready"), 1)
            dve.wait_ge(sem("pos_in"), 16)
            chain(nc.vector.tensor_copy(posf[:], posi[:]))
            chain(TT(rope_sin[:].rearrange("p (t k) -> p t k", t=NT), bcast_last(posf[:], HALF),
                     bcast_mid(freq[:], NT), ALU.mult))
            reduce_angle(rope_sin[:], rope_tmp[:]).then_inc(sem("rope_ready"), 1)

            dve.wait_ge(sem("mag_ready"), 2)
            dve.wait_ge(sem("trig_ready"), 2)
            chain(TT(cosn, cosn, mag, ALU.mult))
            chain(TT(sinn, sinn, mag, ALU.mult))
            re, im = slice(0, 64), slice(64, P)
            up, down = slice(0, STEP + 1), slice(STEP + 1, NPOW)
            chain(nc.vector.tensor_copy(xx[re], cosn[re, up, :]))
            chain(TS(xx[im], sinn[im, up, :], -1.0, None, ALU.mult))
            chain(TS(yy[re], sinn[re, up, :], -1.0, None, ALU.mult))
            chain(TS(yy[im], cosn[im, up, :], -1.0, None, ALU.mult))
            chain(nc.vector.tensor_copy(xx2[re], cosn[re, down, :]))
            chain(nc.vector.tensor_copy(xx2[im], sinn[im, down, :]))
            chain(TS(yy2[re], sinn[re, down, :], -1.0, None, ALU.mult))
            chain(nc.vector.tensor_copy(yy2[im], cosn[im, down, :]))
            ar, ai = cosn[:, 1, :], sinn[:, 1, :]
            chain(TT(t1, lr, lr, ALU.mult))
            chain(TT(t2, li, li, ALU.mult))
            chain(TT(t1, t1, t2, ALU.add))
            chain(nc.vector.reciprocal(den, t1))
            chain(TS(am1, ar, -1.0, None, ALU.add))
            chain(TT(t1, am1, lr, ALU.mult))
            chain(TT(t2, ai, li, ALU.mult))
            chain(TT(t1, t1, t2, ALU.add))
            chain(TT(cfr, t1, den, ALU.mult))
            chain(TT(t1, ai, lr, ALU.mult))
            chain(TT(t2, am1, li, ALU.mult))
            chain(TT(t1, t1, t2, ALU.subtract))
            chain(TT(cfi, t1, den, ALU.mult))
            dve.wait_ge(sem("bc_in"), 128)
            tmpb = view(work, 10432, G, CH)
            fr, fi = bcast_last(cfr, CH), bcast_last(cfi, CH)
            chain(TT(bbr, br, fr, ALU.mult))
            chain(TT(tmpb, bi, fi, ALU.mult))
            chain(TT(bbr, bbr, tmpb, ALU.subtract))
            chain(TT(bbi, bi, fr, ALU.mult))
            chain(TT(tmpb, br, fi, ALU.mult))
            chain(TT(bbi, bbi, tmpb, ALU.add))
            chain(nc.vector.tensor_copy(bstk[re], bbr[re]))
            nc.vector.tensor_copy(bstk[im], bbi[im]).then_inc(sem("tables_ready"), 1)
            for b in range(2 * NB):
                g = slice((b % NB) * GB, (b % NB + 1) * GB)
                if b < NB:
                    if b >= 2:
                        dve.wait_ge(sem("ba_transposed"), b - 1)
                    left, right, n = bbr, xx2, STEP
                    dst = ba[b % 2].rearrange("p g (n i) -> p g n i", n=n)
                else:
                    if b == NB:
                        dve.wait_ge(sem("u_transposed"), 1)
                    left, right, n = cr, xx, STEP + 1
                    dst = ca[:, g]
                chain(TT(dst, left[:, g, :].rearrange("p g (o i) -> p g o i", o=1).broadcast_to([P, GB, n, CH]),
                         right[:, :, g].rearrange("p n (g o) -> p g n o", o=1).broadcast_to([P, GB, n, CH]),
                         ALU.mult))
                dve.wait_ge(sem("product"), b + 1)
                TT(dst, dst, prod[b % 2][:, 0:GB * n * CH].rearrange("p (g n i) -> p g n i", n=n, i=CH),
                   ALU.add).then_inc(sem("summed"), 1)
            dve.wait_ge(sem("summed"), 2 * NB)
            chain(nc.vector.tensor_copy(decay, bcast_last(m8, NC)))
            chain(nc.vector.memset(decay[:, :, 0:1], 0.0))
            chain(nc.vector.memset(sprev[:, :, 0:1], 0.0))
            dve.wait_ge(sem("turn_ready"), 2)
            dve.wait_ge(sem("swapped"), 1)
            swapped = ps[:, 4:8, :].rearrange("p b (g c) -> p (b g) c", c=NC)
            chain(TT(state, swapped, sin_c, ALU.mult))
            chain(TT(bsum, bsum, cos_c, ALU.mult))
            chain(TT(bsum, bsum, state, ALU.add))
            flat = "p g c -> p (g c)"
            nc.vector.tensor_tensor_scan(state.rearrange(flat), decay.rearrange(flat), bsum.rearrange(flat),
                                         0.0, ALU.mult, ALU.add).then_inc(sem("scanned"), 1)
            dve.wait_ge(sem("scanned"), 1)
            chain(TT(bsum, state, cos_c, ALU.mult))
            dve.wait_ge(sem("swapped"), 2)
            chain(TT(decay, swapped, sin_c, ALU.mult))
            TT(sprev[:, :, 1:NC + 1], bsum, decay, ALU.subtract).then_inc(sem("states_ready"), 1)
            dve.wait_ge(sem("gain_b_in"), 16)
            dve.wait_ge(sem("v_in"), 16 * NT)
            for t in range(NT):
                chain(TT(xn[:, t, :], xn[:, t, :], gain_b[:], ALU.mult))
            for t in range(NT):
                dve.wait_ge(sem(f"y_in_{t}"), 64)
                TT(mix[:, t, :], mix[:, t, :], xn[:, t, :], ALU.add).then_inc(sem("gelu_in"), 1)
            def make_low(n, i):
                dve.wait_ge(sem("high_ready"), i * PER_EXPERT + n + 1)
                TT(low[:, n % SPLIT, :], raw[:, n % RING, :], high[:, n % SPLIT, :].bitcast(F32), ALU.subtract)\
                    .then_inc(sem("low_ready"), 1)

            pieces = Splitter(make_low, 0, END)

            def used(n, i=0):
                dve.wait_ge(sem("used"), i * PER_EXPERT + n + 1)

            def swiglu(base, i, walk, order, at0, units, blocks, before_last_T=None):
                one, at = BLOCKS // blocks, {q: at0 + c for c, q in enumerate(order)}
                end = at0 + len(order)
                for j in range(units + 1):
                    if j >= 1:
                        walk.upto(min(at[("w1", j, 0)] + SPLIT if j < units else end, end))
                        if j == units and before_last_T:
                            before_last_T()
                        m = width(order, j - 1, units) // P
                        for b in range(blocks):
                            dve.wait_ge(sem("hidT_hi"), after(base, j - 1, b, blocks))
                            TT(hidT_lo[:, b, 0:m, :], ps[:, 2 + b, 0:m * P].rearrange("p (m s) -> p m s", m=m),
                               hidT_hi[:, b, 0:m, :].bitcast(F32), ALU.subtract).then_inc(sem("hidT_ready"), one)
                    if j < units:
                        w = width(order, j, units)
                        last_up = at[("w3", j, 1)] if w == BK else at[("w1", j, 1)]
                        walk.upto(min(last_up + SPLIT, end))
                        used(last_up, i)
                        for b in range(blocks):
                            dve.wait_ge(sem("gate_ready"), after(base, j, b, blocks))
                            if j >= 1:
                                dve.wait_ge(sem("hid_T"), after(base, j - 1, b, blocks))
                            up3 = ps[:, 2 + b, 0:w] if w == BK else ps[:, b, w:2 * w]
                            TT(hid[b][:, 0:w], gate_sb[b][:, 0:w], up3, ALU.mult).then_inc(sem("hid_ready"), one)
                walk.upto(end)

            pieces.upto(GLU0 + SPLIT)
            for b in range(4):
                dve.wait_ge(sem("g_high"), b + 1)
                TT(xT[1][:, 2 * b:2 * b + 2, :], ps[:, b, :].rearrange("p (k s) -> p k s", k=2),
                   xT[0][:, 2 * b:2 * b + 2, :].bitcast(F32), ALU.subtract).then_inc(sem("gT_ready"), 1)
            for n in range(NT):
                pieces.upto(4 * n + 3 + SPLIT)
                for t in range(NT):
                    dve.wait_ge(sem("glu_sig"), NT * n + t + 1)
                    TT(mix[:, t, n * BK:(n + 1) * BK], ps[:, 4 * n + t, :], gate_sb[t], ALU.mult)\
                        .then_inc(sem("glu_out"), 1)

            def post(gain, gain_sem, name):
                inverse_root()
                dve.wait_ge(sem(gain_sem), 16)
                for t in range(NT):
                    chain(STT(out=xn[:, t, :], in0=mix[:, t, :], scalar=rstd[:, t:t + 1], in1=gain[:],
                              op0=ALU.mult, op1=ALU.mult))
                    TT(x[:, t, :], x[:, t, :], xn[:, t, :], ALU.add).then_inc(sem(name), 1)

            def normed(name):
                inverse_root()
                for t in range(NT):
                    TS(xn[:, t, :], x[:, t, :], rstd[:, t:t + 1], None, ALU.mult).then_inc(sem(name + "_xn"), 1)

            def by_channel(name, gains):
                for b in range(4):
                    dve.wait_ge(sem("q_in_transposed" if name == "q" else name + "_transposed"), b + 1)
                    TT(tmpT[:, 2 * b:2 * b + 2, :], ps[:, b, :].rearrange("p (k s) -> p k s", k=2),
                       bcast_last(gains[:, 2 * b:2 * b + 2], S), ALU.mult).then_inc(sem(name + "_v"), 1)
                if name == "moe":
                    return
                for b in range(4):
                    dve.wait_ge(sem(name + "_high"), b + 1)
                    TT(xT[1][:, 2 * b:2 * b + 2, :], tmpT[:, 2 * b:2 * b + 2, :],
                       xT[0][:, 2 * b:2 * b + 2, :].bitcast(F32), ALU.subtract).then_inc(sem(name + "_xT"), 1)

            post(gain_a, "gain_1_in", "added_0" if ffn else "x_final")
            if ffn:
                dve.wait_ge(sem("const_in"), 64)
                normed("ffn")
                by_channel("ffn", gcol[:, 2, :])
                swiglu(0, 0, pieces, FFN_ORDER, FFN0, FULL + 1, NT)
                post(gain_b, "gain_2_in", "added_1" if attn else "x_final")
            if attn:
                normed("attn")
                by_channel("kv", kvcol[:])
                dve.wait_ge(sem("rope_done"), 2)

                turned = [0]

                def turn_heads(t, rows, done):
                    src = rows.rearrange("p (h d) -> p h d", d=DH)
                    x1, x2 = src[:, :, 0:HALF], src[:, :, HALF:ROT]
                    cos = bcast_mid(rope_cos[:, t * HALF:(t + 1) * HALF], 4)
                    sin = bcast_mid(rope_sin[:, t * HALF:(t + 1) * HALF], 4)
                    chain(TT(rot[0], x1, cos, ALU.mult))
                    chain(TT(rot[1], x2, sin, ALU.mult))
                    chain(TT(rot[2], x2, cos, ALU.mult))
                    chain(TT(rot[3], x1, sin, ALU.mult))
                    chain(TT(x1, rot[0], rot[1], ALU.subtract))
                    TT(x2, rot[2], rot[3], ALU.add).then_inc(sem(done), 1)
                    turned[0] += 1
                    dve.wait_ge(sem(done), turned[0])

                for c in range(4):
                    pieces.upto(KV0 + 2 * c + 1 + SPLIT)
                    if c < 2:
                        for t in range(NT):
                            dve.wait_ge(sem("k_copied"), 2 * c + t + 1)
                            turn_heads(t, mix[:, t, c * BK:(c + 1) * BK], "k_turned")
                by_channel("q", gcol[:, 4, :])
                turned = [0]
                for c in range(2):
                    pieces.upto(Q0 + 2 * c + 1 + SPLIT)
                    for t in range(NT):
                        dve.wait_ge(sem("q_copied"), 2 * c + t + 1)
                        turn_heads(t, mix[:, t, c * BK:(c + 1) * BK], "q_turned")
                pieces.upto(O0 + SPLIT)
                dve.wait_ge(sem("masks_ready"), 3)
                scale = float(DH) ** -0.5

                def normalise(h):
                    dve.wait_ge(sem("exped"), NT * (h + 1))
                    chain(nc.vector.reciprocal(soft[:, h, 3, :], soft[:, h, 2, :]))
                    p = prob[h % 2]
                    TS(p[:, 0:P], p[:, 0:P], soft[:, h, 3, 0:1], None, ALU.mult).then_inc(sem("prob_ready"), 1)
                    TS(p[:, P:3 * P], p[:, P:3 * P], soft[:, h, 3, 1:2], None, ALU.mult)\
                        .then_inc(sem("prob_ready"), 1)

                for h in range(HEADS + 2):
                    if h < HEADS:
                        dve.wait_ge(sem("scores"), h + 1)
                        if h >= 2:
                            dve.wait_ge(sem("exped"), NT * (h - 1))
                        s, src = att[h % 2], ps[:, h % 2, 0:384]
                        chain(STT(out=s[:, 0:P], in0=src[:, 0:P], scalar=scale, in1=mask[:],
                                  op0=ALU.mult, op1=ALU.add))
                        chain(TS(s[:, P:2 * P], src[:, P:2 * P], scale, None, ALU.mult))
                        STT(out=s[:, 2 * P:3 * P], in0=src[:, 2 * P:3 * P], scalar=scale, in1=mask[:],
                            op0=ALU.mult, op1=ALU.add).then_inc(sem("scores_read"), 1)
                        dve.wait_ge(sem("scores_read"), h + 1)
                        chain(nc.vector.reduce_max(soft[:, h, 0, 0:1], s[:, 0:P], AX_X))
                        chain(nc.vector.reduce_max(soft[:, h, 0, 1:2], s[:, P:3 * P], AX_X))
                        TS(soft[:, h, 1, :], soft[:, h, 0, :], -1.0, None, ALU.mult).then_inc(sem("score_max"), 1)
                    if 1 <= h <= HEADS:
                        normalise(h - 1)
                    if h >= 2:
                        k = h - 2
                        dve.wait_ge(sem("o_high"), k + 1)
                        TT(xT[1][:, k, :], ps[:, 4 + k % 2, 0:S], xT[0][:, k, :].bitcast(F32), ALU.subtract)\
                            .then_inc(sem("oT_ready"), 1)
                pieces.upto(MOE0 + SPLIT - 1)
                post(gain_a, "gain_3_in", "added_2" if moe else "x_final")
                pieces.upto(MOE0 + SPLIT)
            if moe:
                normed("moe")
                by_channel("moe", gcol[:, 6, :])
                lg, eq, cand, oh1, oh2, sel, w, iota_e, far = (rt[:, k] for k in range(9))
                m1, i1, m2, i2, gap, den, w1, w2 = (rs[:, k, :] for k in range(8))
                wide = lambda ap: bcast_last(ap, E)
                chain(nc.vector.tensor_copy(iota_e, bcast_mid(iota_c[:, 0:E], NT)))
                chain(TS(far, iota_e, 99.0, None, ALU.add))
                dve.wait_ge(sem("logits"), 1)
                chain(TT(lg, ps[:, 4, 0:NT * E].rearrange("p (t e) -> p t e", t=NT), bcast_mid(rbias[:], NT),
                         ALU.add))
                for m, i, oh in ((m1, i1, oh1), (m2, i2, oh2)):
                    chain(nc.vector.reduce_max(m, lg, AX_X))
                    chain(TT(eq, lg, wide(m), ALU.is_equal))
                    chain(STT(out=cand, in0=eq, scalar=-99.0, in1=far, op0=ALU.mult, op1=ALU.add))
                    chain(nc.vector.tensor_reduce(i, cand, axis=AX_X, op=ALU.min))
                    chain(TT(oh, iota_e, wide(i), ALU.is_equal))
                    if oh is oh1:
                        chain(STT(out=lg, in0=oh, scalar=NEG, in1=lg, op0=ALU.mult, op1=ALU.add))
                TT(gap, m2, m1, ALU.subtract).then_inc(sem("gap_ready"), 1)
                TT(sel, oh1, oh2, ALU.add).then_inc(sem("sel_ready"), 1)
                dve.wait_ge(sem("gap_exp"), 1)
                chain(TS(den, gap, 1.0, None, ALU.add))
                chain(nc.vector.reciprocal(w1, den))
                chain(TT(w2, gap, w1, ALU.mult))
                chain(TT(cand, oh1, wide(w1), ALU.mult))
                chain(TT(w, oh2, wide(w2), ALU.mult))
                chain(TT(w, w, cand, ALU.add))
                chain(nc.vector.tensor_copy(wgt[:, :, 0:E], w))
                chain(nc.vector.memset(wgt[:, :, E:E + 1], 0.0))
                dve.wait_ge(sem("places"), 1)
                place = ps[:, 5, 0:NT * E].rearrange("p (t e) -> p t e", t=NT)
                chain(STT(out=cand, in0=place, scalar=1.0, in1=sel, op0=ALU.add, op1=ALU.mult))
                chain(TS(slot[:, :, 0:E], cand, -1.0, None, ALU.add))
                chain(nc.vector.memset(slot[:, :, E:E + 1], -1.0))
                chain(nc.vector.memset(count[:, E:E + 1], 0))
                nc.vector.tensor_copy(count[:, 0:E], ps[:, 6, 0:E]).then_inc(sem("routed"), 1)
                for t in range(NT):
                    nc.vector.memset(acc[:, t, :], 0.0).then_inc(sem("added"), 2)
                dve.wait_ge(sem("added"), 4)
                dve.wait_ge(sem("routed"), 1)

                def one_hots(i):
                    for t in range(NT):
                        TS(onehot[:, t, :], iota_c[:], slot[:, t, bass.ds(i, 1)], None, ALU.is_equal)\
                            .then_inc(sem("onehot_ready"), 1)

                def weighted_one_hots(i):
                    for t in range(NT):
                        TS(weighted[:, t, :], iota_c[:], slot[:, t, bass.ds(i, 1)], wgt[:, t, bass.ds(i, 1)],
                           ALU.is_equal, ALU.mult).then_inc(sem("weighted_ready"), 1)

                def gathered_in(b):
                    def steps(i, blocks):
                        if b < blocks:
                            dve.wait_ge(sem("gathered"), after(i * BLOCKS, 0, b, blocks))
                            TT(tmpTe[:, b], ps[:, 2 * b:2 * b + 2, :].rearrange("p b (k s) -> p (b k) s", s=P),
                               bcast_last(gcol[:, 6, :], P), ALU.mult).then_inc(sem("expert_v"), BLOCKS // blocks)
                            dve.wait_ge(sem("expert_high"), after(i * BLOCKS, 0, b, blocks))
                            TT(xTe[1][:, b], tmpTe[:, b], xTe[0][:, b].bitcast(F32), ALU.subtract)\
                                .then_inc(sem("xTe_ready"), BLOCKS // blocks)
                    return steps

                def hidden(i, blocks):
                    walk = expert_pieces(make_low, i)
                    swiglu(i * STEPS + FFN_STEPS, i, walk, ORDER, MOE0, UNITS, blocks,
                           lambda: by_blocks(dve, i + 1, gathered_in(0)))
                    with dve.If(i < E - 1):
                        walk.upto(MOE0 + PER_EXPERT + SPLIT)

                one_hots(0)
                weighted_one_hots(0)
                for b in range(BLOCKS):
                    by_blocks(dve, 0, gathered_in(b))
                with dve.Fori(0, E) as i:
                    dve.wait_ge(sem("gathered"), i * BLOCKS + BLOCKS)
                    one_hots(i + 1)
                    dve.wait_ge(sem("weighted_T"), i + 1)
                    weighted_one_hots(i + 1)
                    by_blocks(dve, i, hidden)
                    by_blocks(dve, i + 1, gathered_in(1))
                    for q in range(4):
                        dve.wait_ge(sem("combined"), i * 4 + q + 1)
                        dst = acc[:, q // 2, (q % 2) * BK:(q % 2 + 1) * BK]
                        TT(dst, dst, ps[:, 4 + q, :], ALU.add).then_inc(sem("added"), 1)
                    dve.wait_ge(sem("added"), i * 4 + 8)
                nc.vector.memset(rs[:, 2, :], 0.0).then_inc(sem("acc_done"), 1)
                post(gain_b, "gain_4_in", "x_final")

        @block.tensor
        def _(pe):
            mm = nc.tensor.matmul

            def mm3(out, left, right, first, last):
                mm(out, left[0], right[0], start=first, stop=False)
                mm(out, left[0], right[1], start=False, stop=False)
                return mm(out, left[1], right[0], start=False, stop=last)

            def split_ready(n, i=0):
                pe.wait_ge(sem("low_ready"), i * PER_EXPERT + n + 1)

            def up_half(banks, lhs, n, k, i=0):
                split_ready(n, i)
                w = split_of(n)
                for b, bank in enumerate(banks):
                    for f in range(4):
                        last = mm3(ps[:, bank, :], lhs(b, 4 * k + f), [t[:, f, :] for t in w],
                                   k == 0 and f == 0, k == 1 and f == 3)
                last.then_inc(sem("used"), 1)

            def swiglu(base, i, order, at0, units, blocks, lhs, y_free, before_last_T=None,
                       up_banks_free=lambda: None):
                one, at = BLOCKS // blocks, {q: at0 + c for c, q in enumerate(order)}
                for j in range(units + 1):
                    if j < units:
                        if j >= 1:
                            pe.wait_ge(sem("gate_ready"), after(base, j - 1, blocks - 1, blocks))
                        up_half(range(blocks), lhs, at[("w1", j, 0)], 0, i)
                    if j >= 1:
                        m = width(order, j - 1, units) // P
                        if j == units and before_last_T:
                            pe.wait_ge(sem("gate_ready"), after(base, j - 1, blocks - 1, blocks))
                            before_last_T()
                        for b in range(blocks):
                            pe.wait_ge(sem("hid_ready"), after(base, j - 1, b, blocks))
                            for f in range(m):
                                last = nc.tensor.transpose(ps[:, 2 + b, f * P:(f + 1) * P],
                                                           hid[b][:, f * P:(f + 1) * P], ident[:])
                            last.then_inc(sem("hid_T"), one)
                    if j < units:
                        up_half(range(blocks), lhs, at[("w1", j, 1)], 1, i)
                    if j >= 1:
                        if j == 1:
                            y_free()
                        pe.wait_ge(sem("hidT_ready"), after(base, j - 1, blocks - 1, blocks))
                        for k in range(m // 2):
                            n = at[("w2", j - 1, k)]
                            split_ready(n, i)
                            w = split_of(n, down=True)
                            for b in range(blocks):
                                for f in range(2):
                                    for half in range(2):
                                        last = mm3(ps[:, 4 + 2 * b + half, :],
                                                   [t[:, b, 2 * k + f, :] for t in hidT],
                                                   [t[:, f, half * BK:(half + 1) * BK] for t in w],
                                                   j == 1 and k == 0 and f == 0,
                                                   j == units and k == m // 2 - 1 and f == 1)
                            last.then_inc(sem("used"), 1)
                    if j < units and width(order, j, units) == BK:
                        if j == 0:
                            up_banks_free()
                        for k in range(2):
                            up_half([2 + b for b in range(blocks)], lhs, at[("w3", j, k)], k, i)

            def by_token(b, kt):
                return [t[:, kt, b * P:(b + 1) * P] for t in xT]

            def transposes(src, name, bank=0):
                for b in range(4):
                    for k in range(2):
                        for t in range(NT):
                            kt = 2 * b + k
                            last = nc.tensor.transpose(ps[:, bank + b, k * S + t * P:k * S + (t + 1) * P],
                                                       src[:, t, kt * P:(kt + 1) * P], ident[:])
                    last.then_inc(sem(name), 1)

            pe.wait_ge(sem("ident_ready"), 1)
            pe.wait_ge(sem("v_grouped"), 1)
            for g in range(G):
                last = nc.tensor.transpose(ps[:, g // 16, (g % 16) * NC:(g % 16 + 1) * NC],
                                           vgrp[:, g].rearrange("p l i -> p (l i)"), ident[0:NC, 0:NC])
            last.then_inc(sem("u_transposed"), 1)

            def chunk_sums(b):
                pe.wait_ge(sem("wint_ready"), b + 1)
                for k in range(GB):
                    g = b * GB + k
                    q, at = g % 4, (g // 4) % 4 * P
                    last = mm(ps[32 * q:32 * q + 32, 4 + g // 16, at:at + P], useq[:, g, :],
                              wint[b % 2][:, k, :], start=True, stop=True, tile_position=(0, 32 * q))
                last.then_inc(sem("chunk_sums"), 1)

            pe.wait_ge(sem("useq_ready"), 1)
            for b in range(NB):
                pe.wait_ge(sem("summed"), b + 1)
                if b >= 2:
                    pe.wait_ge(sem("wint_ready"), b - 1)
                for k in range(GB):
                    last = nc.tensor.transpose(ps[:, 2 * (b % 2) + k // 4, (k % 4) * P:(k % 4 + 1) * P],
                                               ba[b % 2][:, k, :], ident[:])
                last.then_inc(sem("ba_transposed"), 1)
                if b >= 1:
                    chunk_sums(b - 1)
            chunk_sums(NB - 1)
            def swap_parts(src):
                flat = src.rearrange("p g c -> p (g c)")
                for b in range(4):
                    last = mm(ps[:, 4 + b, :], swap[:], flat[:, b * BK:(b + 1) * BK], start=True, stop=True)
                last.then_inc(sem("swapped"), 1)

            pe.wait_ge(sem("swap_ready"), 1)
            for b in range(NB):
                if b == 2:
                    pe.wait_ge(sem("sums_copied"), 1)
                    for k in range(G // 4):
                        last = nc.tensor.transpose(ps[:, 4 + k // 4, (k % 4) * P:(k % 4 + 1) * P],
                                                   sums[:, k, :], ident[:])
                    last.then_inc(sem("sums_T"), 1)
                if b == 4:
                    pe.wait_ge(sem("bsum_ready"), 1)
                    swap_parts(bsum)
                pe.wait_ge(sem("summed"), NB + b + 1)
                if b >= 2:
                    pe.wait_ge(sem("taps_ready"), b - 1)
                for k in range(GB):
                    g = b * GB + k
                    last = mm(ps[0:CH, 2 * (b % 2) + k // 4, (k % 4) * P:(k % 4 + 1) * P], bstk[:, g, :],
                              ca[:, g, 0:STEP, :].rearrange("p n i -> p (n i)"), start=True, stop=True)
                last.then_inc(sem("taps_made"), 1)
            pe.wait_ge(sem("scanned"), 1)
            swap_parts(state)
            pe.wait_ge(sem("taps_ready"), NB)
            pe.wait_ge(sem("states_ready"), 1)
            pe.wait_ge(sem("toep_in"), 16 * 2 * STEP)
            for g4 in range(GQ):
                for q in range(4):
                    g = q * GQ + g4
                    dst = ps[32 * q:32 * q + 32, g4 // 4, (g4 % 4) * P:(g4 % 4 + 1) * P]
                    mm(dst, sprev[:, g, 0:NC], ca[:, g, 1:STEP + 1, :].rearrange("p n i -> p (n i)"),
                       start=True, stop=False, tile_position=(0, 32 * q))
                    last = mm(dst, useq[:, g, :], toep[:, g, :], start=False, stop=True, tile_position=(0, 32 * q))
            last.then_inc(sem("y_made"), 1)

            pe.wait_ge(sem("y_copied"), 1)
            pe.wait_ge(sem("g_ready"), NT)
            transposes(xn, "g_transposed")
            pe.wait_ge(sem("gT_ready"), 4)
            for n in range(NT):
                for c in range(4):
                    up_half([4 * n + 2 * (c // 2) + t for t in range(NT)], by_token, GLU0 + 4 * n + c, c % 2)

            if ffn:
                pe.wait_ge(sem("ffn_xn"), NT)
                pe.wait_ge(sem("glu_out"), NT * NT)
                transposes(xn, "ffn_transposed")
                pe.wait_ge(sem("ffn_xT"), 4)
                swiglu(0, 0, FFN_ORDER, FFN0, FULL + 1, NT, by_token, lambda: None)

            if attn:
                pe.wait_ge(sem("attn_xn"), NT)
                transposes(xn, "kv_transposed")
                pe.wait_ge(sem("kv_xT"), 4)
                pe.wait_ge(sem("ffn_copied"), NT)
                for n in range(KV0, Q0):
                    c, k = divmod(n - KV0, 2)
                    up_half([2 * c + t for t in range(NT)], by_token, n, k)
                pe.wait_ge(sem("k_copied"), 2 * NT)
                transposes(xn, "q_in_transposed")
                pe.wait_ge(sem("k_turned"), 2 * NT)
                pe.wait_ge(sem("v_copied"), 2 * NT)
                transposes(mix, "k_transposed", 4)
                pe.wait_ge(sem("q_xT"), 4)
                for n in range(Q0, O0):
                    c, k = divmod(n - Q0, 2)
                    up_half([2 * c + t for t in range(NT)], by_token, n, k)
                pe.wait_ge(sem("q_copied"), 2 * NT)
                pe.wait_ge(sem("q_turned"), 2 * NT)
                pe.wait_ge(sem("kT_ready"), 4)
                transposes(mix, "q_transposed", 4)
                pe.wait_ge(sem("qT_ready"), 4)
                for h in range(HEADS + 2):
                    if h < HEADS:
                        if h >= 2:
                            pe.wait_ge(sem("scores_read"), h - 1)
                        mm(ps[:, h % 2, 0:P], qT[:, h, 0:P], kT[:, h, 0:P], start=True, stop=True)
                        mm(ps[:, h % 2, P:3 * P], qT[:, h, P:S], kT[:, h, :], start=True, stop=True)\
                            .then_inc(sem("scores"), 1)
                    if 1 <= h <= HEADS:
                        k = h - 1
                        pe.wait_ge(sem("prob_ready"), NT * (k + 1))
                        if k >= 2:
                            pe.wait_ge(sem("probT_ready"), k - 1)
                        for m in range(3):
                            last = nc.tensor.transpose(ps[:, 2 + k % 2, m * P:(m + 1) * P],
                                                       prob[k % 2][:, m * P:(m + 1) * P], ident[:])
                        last.then_inc(sem("prob_transposed"), 1)
                    if h >= 2:
                        k = h - 2
                        pe.wait_ge(sem("probT_ready"), k + 1)
                        if k >= 2:
                            pe.wait_ge(sem("oT_ready"), k - 1)
                        cols = slice(k * DH, (k + 1) * DH)
                        mm(ps[:, 4 + k % 2, 0:P], v[:, 0, cols], probT[k % 2][:, 0, :], start=True, stop=True)
                        mm(ps[:, 4 + k % 2, P:S], v[:, 0, cols], probT[k % 2][:, 1, :], start=True, stop=False)
                        mm(ps[:, 4 + k % 2, P:S], v[:, 1, cols], probT[k % 2][:, 2, :], start=False, stop=True)\
                            .then_inc(sem("o_made"), 1)
                pe.wait_ge(sem("oT_ready"), HEADS)
                for n in range(O0, MOE0):
                    c, k = divmod(n - O0, 2)
                    up_half([2 * c + t for t in range(NT)], by_token, n, k)

            if moe:
                pe.wait_ge(sem("moe_xn"), NT)
                pe.wait_ge(sem("proj_copied"), 2 * NT)
                transposes(xn, "moe_transposed")
                pe.wait_ge(sem("moe_v"), 4)
                for t in range(NT):
                    for kt in range(KT):
                        last = mm(ps[:, 4, t * E:(t + 1) * E], tmpT[:, kt, t * P:(t + 1) * P], wr[:, kt, :],
                                  start=(kt == 0), stop=(kt == KT - 1))
                last.then_inc(sem("logits"), 1)
                pe.wait_ge(sem("sel_ready"), 1)
                pe.wait_ge(sem("masks_ready"), 3)
                sel = rt[:, 5]
                mm(ps[:, 5, 0:E], tri[:], sel[:, 0, :], start=True, stop=True)
                mm(ps[:, 5, E:2 * E], ones[:], sel[:, 0, :], start=True, stop=False)
                mm(ps[:, 5, E:2 * E], tri[:], sel[:, 1, :], start=False, stop=True)
                mm(ps[:, 6, 0:E], ones[:], sel[:, 0, :], start=True, stop=False)
                mm(ps[:, 6, 0:E], ones[:], sel[:, 1, :], start=False, stop=True).then_inc(sem("places"), 1)

                def gather(b):
                    def steps(i, blocks):
                        if b < blocks:
                            pe.wait_ge(sem("onehot_ready"), NT * i + NT)
                            for kt in range(KT):
                                for t in range(NT):
                                    last = mm(ps[:, 2 * b + kt // 4, (kt % 4) * P:(kt % 4 + 1) * P],
                                              xn[:, t, kt * P:(kt + 1) * P], onehot[:, t, b * P:(b + 1) * P],
                                              start=(t == 0), stop=(t == NT - 1))
                            last.then_inc(sem("gathered"), BLOCKS // blocks)
                    return steps

                def hidden(i, blocks):
                    swiglu(i * STEPS + FFN_STEPS, i, ORDER, MOE0, UNITS, blocks,
                           lambda b, kt: [t[:, b, kt, :] for t in xTe],
                           lambda: pe.wait_ge(sem("added"), i * 4 + 4),
                           lambda: by_blocks(pe, i + 1, gather(0)),
                           lambda: pe.wait_ge(sem("weightedT_ready"), i + 1))

                def combine(i, blocks):
                    pe.wait_ge(sem("y_rows"), i + 1)
                    pe.wait_ge(sem("weightedT_ready"), i + 1)
                    for q in range(4):
                        t, half = q // 2, q % 2
                        for b in range(blocks):
                            last = mm(ps[:, 4 + q, :], weightedT[:, b, t * P:(t + 1) * P],
                                      y_rows[:, b, half * BK:(half + 1) * BK], start=(b == 0), stop=(b == blocks - 1))
                        last.then_inc(sem("combined"), 1)

                pe.wait_ge(sem("routed"), 1)
                for b in range(BLOCKS):
                    by_blocks(pe, 0, gather(b))
                with pe.Fori(0, E) as i:
                    pe.wait_ge(sem("xTe_ready"), (i + 1) * BLOCKS)
                    pe.wait_ge(sem("weighted_ready"), NT * i + NT)
                    for b in range(BLOCKS):
                        for t in range(NT):
                            last = nc.tensor.transpose(ps[:, 3, b * S + t * P:b * S + (t + 1) * P],
                                                       weighted[:, t, b * P:(b + 1) * P], ident[:])
                    last.then_inc(sem("weighted_T"), 1)
                    by_blocks(pe, i, hidden)
                    by_blocks(pe, i + 1, gather(1))
                    by_blocks(pe, i, combine)


def kernel(**inputs):
    import numpy as _np
    import concourse.bacc as _bacc
    from concourse import mybir as _mybir
    from concourse.bass_utils import run_bass_kernel_spmd as _run

    nc = _bacc.Bacc("TRN2", target_bir_lowering=False, num_devices=1)
    arrays, args = {}, {}
    for name, value in lay_out(inputs).items():
        value = _np.ascontiguousarray(value)
        arrays[f"in_{name}"] = value
        args[name] = nc.dram_tensor(f"in_{name}", value.shape, _mybir.dt.from_np(value.dtype),
                                    kind="ExternalInput").ap()
    out = nc.dram_tensor("out_0", (1, S, D), F32, kind="ExternalOutput").ap()
    trunk(nc, args, out)
    r = _run(nc, [arrays], core_ids=[0])
    return r.results[0]["out_0"]
```

```python
from contextlib import ExitStack

import numpy as np

import concourse.bass as bass
from concourse import mybir

F32 = mybir.dt.float32
F32R = mybir.dt.float32r
I32 = mybir.dt.int32
ALU = mybir.AluOpType
ACT = mybir.ActivationFunctionType
AX_X = mybir.AxisListType.X

P = 128
D = 1024
S = 256
NT = S // P
KT = D // P
G, CH = 64, 16
STEP = 8
NC = S // STEP
GB = 8
NB = G // GB
GQ = G // 4
HEADS, DH, ROT = 8, 128, 32
HALF = ROT // 2
FD = 2816
E, FE = 8, 3584
BK = 512
EPS = 1e-6
NEG = -1e30
INV_2PI = 0.15915494309189535
TWO_PI_HI = 6.28125
TWO_PI_LO = 0.0019353071795864769
ROUND = 12582912.0
PI_BELOW = 3.1415925
HALF_PI = 1.5707963267948966
CYCLE = 2 * PI_BELOW

NPOW = 2 * STEP + 1
INV_FREQ = [float(1.0 / f) for f in
            (np.float32(500000.0) ** (np.arange(HALF, dtype=np.float32) / np.float32(HALF)))]

RING = 7
SPLIT = 3
PIECE = 4 * BK
FULL = FD // BK
TAIL = FD - FULL * BK
UNITS = FE // BK
BLOCKS = S // P
STEPS = BLOCKS * UNITS
FFN_STEPS = NT * (FULL + 1)


def swiglu_pieces(units, tail):
    order = []
    for j in range(units + 1):
        if j < units:
            order += [("w1", j, 0), ("w1", j, 1)]
        if j >= 1:
            order += [("w2", j - 1, 0)] + [("w2", j - 1, 1)] * (not (tail and j == units))
        if j < units and not (tail and j == units - 1):
            order += [("w3", j, 0), ("w3", j, 1)]
    return order


GLU_ORDER = [(kind, n, k) for n in range(NT) for kind in ("value", "gate") for k in range(2)]
FFN_ORDER = swiglu_pieces(FULL + 1, True)
ORDER = swiglu_pieces(UNITS, False)
GLU0 = 0
FFN0 = GLU0 + len(GLU_ORDER)
KV0 = FFN0 + len(FFN_ORDER)
Q0 = KV0 + 2 * (2 * D // BK)
O0 = Q0 + 2 * (D // BK)
MOE0 = O0 + 2 * (D // BK)
PER_EXPERT = len(ORDER)
assert PER_EXPERT % RING == 0 and PER_EXPERT % SPLIT == 0


class Chain:

    def __init__(self, eng, sem):
        self.eng, self.sem, self.n = eng, sem, 0

    def __call__(self, ins):
        ins.then_inc(self.sem, 1)
        self.n += 1
        self.eng.wait_ge(self.sem, self.n)


def lay_out(inputs):
    a = {k: np.asarray(v) for k, v in inputs.items()}
    a["positions"] = a["positions"].reshape(NT, P).T
    a["norm_cols"] = a["norms"].reshape(8, KT, P).transpose(2, 0, 1)
    a["kv_norm"] = a["kv_norm"].reshape(KT, P).T
    a["moe_router"] = a["moe_router"].reshape(KT, P, E).transpose(1, 0, 2)
    a["lam_re"], a["lam_im"] = a.pop("s5_lam_re")[0].T, a.pop("s5_lam_im")[0].T
    for k in ("re", "im"):
        a["b_" + k] = a.pop("s5_b_" + k)[0].transpose(1, 0, 2)
        a["c_" + k] = a.pop("s5_c_" + k)[0].transpose(2, 0, 1)
    return a


def trunk(nc, a, out):
    ctx = ExitStack()
    with ctx:
        def sb(name, shape, dt=F32):
            return ctx.enter_context(nc.sbuf_tensor(name, shape, dt))

        sems = {}

        def sem(name):
            if name not in sems:
                sems[name] = ctx.enter_context(nc.semaphore(name))
            return sems[name]

        x = sb("x", [P, NT, D])
        xn = sb("xn", [P, NT, D])
        gain_a = sb("gain_a", [P, D])
        gain_b = sb("gain_b", [P, D])
        ident = sb("ident", [P, P])
        swap = sb("swap", [P, P])
        tri = sb("tri", [P, P])
        ones = sb("ones", [P, P])
        iota_c = sb("iota_c", [P, S])
        mask = sb("mask", [P, P])
        powers = sb("powers", [P, NPOW])
        gcol = sb("gcol", [P, 8, KT])
        kvcol = sb("kvcol", [P, KT])
        ss = sb("ss", [P, NT])
        sd = sb("sd", [P, NT])
        rstd = sb("rstd", [P, NT])
        scratch = sb("scratch", [P, 1])
        const = sb("const", [P, 5])
        wr = sb("wr", [P, KT, E])
        rbias = sb("rbias", [P, E])
        rt = sb("rt", [P, 9, NT, E])
        rs = sb("rs", [P, 8, NT])
        slot = sb("slot", [P, NT, E + 1])
        wgt = sb("wgt", [P, NT, E + 1])
        count = sb("count", [P, E + 1], I32)
        posi = sb("posi", [P, NT], I32)
        posf = sb("posf", [P, NT])
        freq = sb("freq", [P, HALF])
        rope_sin = sb("rope_sin", [P, NT * HALF])
        rope_cos = sb("rope_cos", [P, NT * HALF])
        rope_tmp = sb("rope_tmp", [P, NT * HALF])
        small = sb("small", [P, 14, G])
        with nc.sbuf_tensor("s5_ring", [P, 28672], F32) as ring, nc.sbuf_tensor("s5_work", [P, 15900], F32) as work:
            pass
        raw = sb("raw", [P, RING, PIECE])
        high = sb("high", [P, SPLIT, PIECE], F32R)
        low = sb("low", [P, SPLIT, PIECE], F32R)
        xT_hi = sb("xT_hi", [P, KT * S], F32R)
        xT_lo = sb("xT_lo", [P, KT * S], F32R)
        hidT_hi = sb("hidT_hi", [P, BLOCKS, 4, P], F32R)
        hidT_lo = sb("hidT_lo", [P, BLOCKS, 4, P], F32R)
        mix_at = sb("mix", [P, NT * D])
        late = sb("late", [P, 7900])
        ps = ctx.enter_context(nc.psum_tensor("ps", [P, 8, BK], F32))

        def view(buf, at, *shape):
            n = 1
            for k in shape:
                n *= k
            if len(shape) == 1:
                return buf[:, at:at + n]
            names = "abcd"[:len(shape)]
            return buf[:, at:at + n].rearrange(f"p ({' '.join(names)}) -> p {' '.join(names)}",
                                               **{names[i]: shape[i] for i in range(1, len(shape))})

        mix = view(mix_at, 0, NT, D)
        SLOT = 4096
        cr, ci, br, bi = (view(ring, 1024 * k, G, CH) for k in range(4))
        bbr, bbi = (view(ring, SLOT + 1024 * k, G, CH) for k in range(2))
        bstk = view(ring, 2 * SLOT + 19456, G, CH)
        ca = view(ring, 2 * SLOT, G, STEP + 1, CH)
        vtok = ring[0:NC, 2 * SLOT + 9216:2 * SLOT + 9216 + STEP * D].rearrange("p (l d) -> p l d", l=STEP)
        vgrp = ring[0:NC, 2 * SLOT:2 * SLOT + STEP * D].rearrange("p (g l i) -> p g l i", l=STEP, i=CH)
        toep = view(ring, 2 * SLOT + 9216, G, P)
        cos_c = view(ring, 2 * SLOT + 17408, G, NC)
        useq = view(work, 0, G, NC)
        sin_c = view(work, 2048, G, NC)
        decay = view(work, 4096, G, NC)
        sprev = view(work, 6144, G, NC + 1)
        xx, yy = (view(work, 8256 + 576 * k, STEP + 1, G) for k in range(2))
        xx2, yy2 = (view(work, 9408 + 512 * k, STEP, G) for k in range(2))
        ang, mag, cosn, sinn, tmpn = (view(work, 10432 + 1088 * k, NPOW, G) for k in range(5))
        cross = view(work, 14784, G, CH)
        prod = [work[:, 4096 + 1152 * k:4096 + 1152 * (k + 1)] for k in range(2)]
        ba = [view(work, 10432 + 1024 * k, GB, P) for k in range(2)]
        wint = [view(work, 12480 + 1024 * k, GB, P) for k in range(2)]
        taps = [view(work, 10432, G // 2, P), view(ring, SLOT, G // 2, P)]
        state = view(ring, 0, G, NC)
        bsum = view(ring, 2048, G, NC)
        sums = view(ring, SLOT, G // 4, P)
        ytile = view(work, 10304, STEP, GQ, CH)
        xT = [t[:].rearrange("p (k s) -> p k s", s=S) for t in (xT_hi, xT_lo)]
        hidT = [hidT_hi, hidT_lo]
        tmpT = view(late, 2048, KT, S)
        gate_sb = [view(late, 512 * k, BK) for k in range(2)]
        hid = [view(late, 1024 + 512 * k, BK) for k in range(2)]
        kT, qT, v = view(late, 0, HEADS, S), tmpT, view(late, 4096, NT, D)
        probT = [view(late, 6144 + 384 * k, 3, P) for k in range(2)]
        rot = [view(late, 6912 + 64 * k, 4, HALF) for k in range(4)]
        soft = view(late, 7168, HEADS, 4, NT)
        prob = [view(mix_at, 384 * k, 384) for k in range(3)]
        SCORES = (0, 1, 6)
        SCALE = float(DH) ** -0.5
        acc = mix
        xTe = [t[:].rearrange("p (b k s) -> p b k s", b=BLOCKS, s=P) for t in (xT_hi, xT_lo)]
        tmpTe = view(late, 2048, BLOCKS, KT, P)
        y_rows = view(late, 4096, BLOCKS, D)
        onehot = view(late, 6144, NT, S)
        weighted = view(late, 6656, NT, S)
        weightedT = view(late, 7168, BLOCKS, S)

        def bcast_last(ap, n):
            return ap.rearrange("p (k o) -> p k o", o=1).broadcast_to([P, ap.shape[1], n])

        def bcast_mid(ap, n):
            return ap.rearrange("p (o k) -> p o k", o=1).broadcast_to([P, n, ap.shape[1]])

        def by_blocks(eng, i, steps):
            tokens = eng.value_load(count[0:1, bass.ds(i, 1)], min_val=0, max_val=S)
            with eng.If(tokens > P):
                steps(i, 2)
            with eng.Else():
                steps(i, 1)

        def after(base, j, b, blocks):
            return base + BLOCKS * j + (b + 1) * (BLOCKS // blocks)

        def product_rows(bank):
            return ps[:, bank:bank + 2, :].rearrange("p b n -> p (b n)")

        landed = [sem(f"piece_landed_{k}") for k in range(RING)]

        def piece(buf, n, down=False):
            return buf.rearrange("p (k n) -> p k n", k=2 if down else 4)

        def split_of(n, down=False):
            return [piece(t[:, n % SPLIT, :], n, down) for t in (high, low)]

        TAIL_PIECES = [FFN0 + c for c, (kind, j, k) in enumerate(FFN_ORDER) if kind == "w1" and j == FULL]

        def width(order, j, units):
            return TAIL if order is FFN_ORDER and j == units - 1 else BK

        class Splitter:

            def __init__(self, make, at, end, expert=0):
                self.make, self.at, self.end, self.expert = make, at, end, expert

            def upto(self, n):
                for k in range(self.at, min(n, self.end)):
                    self.make(k, self.expert)
                self.at = max(self.at, min(n, self.end))

        def expert_pieces(make, i):
            return Splitter(make, MOE0 + SPLIT, MOE0 + PER_EXPERT + SPLIT, i)

        block = ctx.enter_context(nc.Block())

        @block.sync
        def _(sp):
            for half in range(2):
                rows = slice(64 * half, 64 * half + 64)
                sp.dma_start(small[rows, 0, :], a["lam_re"]).then_inc(sem("lam_in"), 16)
                sp.dma_start(small[rows, 1, :], a["lam_im"]).then_inc(sem("lam_in"), 16)
            sp.dma_start(small[:, 2, :], a["s5_log_dt"].broadcast_to([P, G])).then_inc(sem("lam_in"), 16)
            sp.dma_start(x[:], a["x"].rearrange("b (t p) d -> p (b t) d", p=P)).then_inc(sem("x_in"), 16)
            sp.dma_start(gain_a[:], a["norms"][0, 0:1, :].broadcast_to([P, D])).then_inc(sem("gain_a_in"), 16)
            sp.dma_start(posi[:], a["positions"]).then_inc(sem("pos_in"), 16)
            for name, dst in (("b_re", br), ("b_im", bi), ("c_re", cr), ("c_im", ci)):
                for half in range(2):
                    sp.dma_start(dst[64 * half:64 * half + 64], a[name]).then_inc(sem("bc_in"), 16)
            sp.dma_start(gain_b[:], a["s5_d"].broadcast_to([P, D])).then_inc(sem("gain_b_in"), 16)
            sp.dma_start(gcol[:], a["norm_cols"]).then_inc(sem("const_in"), 16)
            sp.dma_start(kvcol[:], a["kv_norm"]).then_inc(sem("const_in"), 16)
            sp.dma_start(wr[:], a["moe_router"]).then_inc(sem("const_in"), 16)
            sp.dma_start(rbias[:], a["moe_bias"].broadcast_to([P, E])).then_inc(sem("const_in"), 16)

            for t in range(NT):
                sp.wait_ge(sem("h_ready"), t + 1)
                sp.dma_start(vtok[t * NC // NT:(t + 1) * NC // NT], xn[:, t, :]).then_inc(sem("v_in"), 16)
            sp.wait_ge(sem("toep_zero"), 1)
            for half in range(2):
                sp.wait_ge(sem("taps_ready"), NB // 2 * (half + 1))
                gs = slice(half * (G // 2), (half + 1) * (G // 2))
                for m in range(STEP):
                    sp.dma_start(toep[CH * m:CH * (m + 1), gs, CH * m:P],
                                 taps[half][0:CH, :, 0:P - CH * m]).then_inc(sem("toep_in"), 16)

            def load(n, src, down=False, cols=BK):
                if n >= RING:
                    sp.wait_ge(sem("low_ready"), n - RING + 1)
                dst = piece(raw[:, n % RING, :], n, down)
                sp.dma_start(dst[:, :, 0:cols] if cols < BK else dst, src).then_inc(landed[n % RING], 16)

            def up_rows(w, k):
                return w.rearrange("(k p) n -> p k n", p=P)[:, 4 * k:4 * k + 4, :]

            def down_rows(w, j, k):
                at = j * BK + k * 2 * P
                return w[at:at + 2 * P, :].rearrange("(k p) n -> p k n", p=P)

            def glu(n):
                kind, block, k = GLU_ORDER[n]
                at = (kind == "gate") * D + block * BK
                load(GLU0 + n, up_rows(a["s5_w_glu"][0], k)[:, :, at:at + BK])

            sp.wait_ge(sem("toep_in"), 16 * 2 * STEP)
            for n in (2, 3):
                glu(n)
            sp.wait_ge(sem("states_ready"), 1)
            for n in (0, 1):
                glu(n)
            sp.wait_ge(sem("y_copied"), 1)
            for t in range(NT):
                for q in range(4):
                    rows = slice(q * NC + t * NC // NT, q * NC + (t + 1) * NC // NT)
                    sp.dma_start(mix[:, t, q * D // 4:(q + 1) * D // 4],
                                 ytile[rows].rearrange("c l g i -> c l (g i)")).then_inc(sem(f"y_in_{t}"), 16)
            for n in range(4, len(GLU_ORDER)):
                glu(n)
            for c, (kind, j, k) in enumerate(FFN_ORDER):
                n = FFN0 + c
                if kind == "w2":
                    load(n, down_rows(a["ffn_w2"][0], j, k), down=True)
                elif j < FULL:
                    load(n, up_rows(a["ffn_" + kind][0], k)[:, :, j * BK:(j + 1) * BK])
                else:
                    load(n, up_rows(a["ffn_w1"][0], k)[:, :, FULL * BK:FD], cols=TAIL)
                    sp.dma_start(piece(raw[:, n % RING, :], n)[:, :, TAIL:2 * TAIL],
                                 up_rows(a["ffn_w3"][0], k)[:, :, FULL * BK:FD]).then_inc(sem("ffn_tail"), 16)
            for first, end, w in ((KV0, Q0, a["w_kv"]), (Q0, O0, a["w_q"][0]), (O0, MOE0, a["w_o"][0])):
                for n in range(first, end):
                    c, k = divmod(n - first, 2)
                    load(n, up_rows(w, k)[:, :, c * BK:(c + 1) * BK])
            with sp.Fori(0, E) as i:
                for c, (kind, j, k) in enumerate(ORDER):
                    n = MOE0 + c
                    w = a[f"moe_{kind}"][0, bass.ds(i, 1)]
                    if kind == "w2":
                        at = j * BK + k * 2 * P
                        src = w[:, at:at + 2 * P, :]
                    else:
                        src = w[:, 4 * k * P:4 * (k + 1) * P, j * BK:(j + 1) * BK]
                    sp.wait_ge(sem("low_ready"), i * PER_EXPERT + n - RING + 1)
                    sp.dma_start(piece(raw[:, n % RING, :], n, kind == "w2"),
                                 src.rearrange("o (k p) n -> p (o k) n", p=P)).then_inc(landed[n % RING], 16)
            for t in range(NT):
                sp.wait_ge(sem("x_final"), t + 1)
                sp.dma_start(out[0, t * P:(t + 1) * P, :], x[:, t, :]).then_inc(sem("stored"), 16)
            sp.wait_ge(sem("stored"), 16 * NT)

        @block.gpsimd
        def _(pool):
            chain = Chain(pool, sem("pool_chain"))
            nc.gpsimd.memset(const[:, 0:1], EPS).then_inc(sem("eps_set"), 1)
            nc.gpsimd.memset(const[:, 1:2], HALF_PI).then_inc(sem("eps_set"), 1)
            nc.gpsimd.memset(const[:, 2:3], 0.0).then_inc(sem("eps_set"), 1)
            chain(nc.gpsimd.memset(const[:, 3:4], ROUND))
            chain(nc.gpsimd.memset(const[:, 4:5], -ROUND))
            nc.gpsimd.iota(powers[:, 0:STEP + 1], [[1, STEP + 1]], base=0, channel_multiplier=0,
                           allow_small_or_imprecise_dtypes=True).then_inc(sem("iotas"), 1)
            nc.gpsimd.iota(powers[:, STEP + 1:NPOW], [[-1, STEP]], base=STEP - 1, channel_multiplier=0,
                           allow_small_or_imprecise_dtypes=True).then_inc(sem("iotas"), 1)
            nc.gpsimd.iota(iota_c[:], [[1, S]], base=0, channel_multiplier=0,
                           allow_small_or_imprecise_dtypes=True).then_inc(sem("iotas"), 1)
            for k in range(HALF):
                nc.gpsimd.memset(freq[:, k:k + 1], INV_FREQ[k]).then_inc(sem("iotas"), 1)
            chain(nc.gpsimd.memset(ident[:], 0.0))
            nc.gpsimd.affine_select(out=ident[:], in_=ident[:], compare_op=ALU.not_equal, fill=1.0, base=0,
                                    pattern=[[-1, P]], channel_multiplier=1).then_inc(sem("ident_ready"), 1)
            chain(nc.gpsimd.memset(swap[:], 0.0))
            chain(nc.gpsimd.affine_select(out=swap[:], in_=swap[:], compare_op=ALU.not_equal, fill=1.0,
                                          base=-64, pattern=[[-1, P]], channel_multiplier=1))
            nc.gpsimd.affine_select(out=swap[:], in_=swap[:], compare_op=ALU.not_equal, fill=-1.0,
                                    base=64, pattern=[[-1, P]], channel_multiplier=1)\
                .then_inc(sem("swap_ready"), 1)
            nc.gpsimd.memset(ones[:], 1.0).then_inc(sem("masks_ready"), 1)
            chain(nc.gpsimd.memset(tri[:], 1.0))
            nc.gpsimd.affine_select(out=tri[:], in_=tri[:], compare_op=ALU.is_gt, fill=0.0, base=0,
                                    pattern=[[1, P]], channel_multiplier=-1).then_inc(sem("masks_ready"), 1)
            chain(nc.gpsimd.memset(mask[:], 0.0))
            nc.gpsimd.affine_select(out=mask[:], in_=mask[:], compare_op=ALU.is_ge, fill=NEG, base=0,
                                    pattern=[[-1, P]], channel_multiplier=1).then_inc(sem("masks_ready"), 1)

            pool.wait_ge(sem("iotas"), 3 + HALF)
            pool.wait_ge(sem("r8_ready"), 1)
            chain(nc.gpsimd.tensor_tensor(sin_c, bcast_last(small[:, 6, :], NC), bcast_mid(iota_c[:, 0:NC], G),
                                          ALU.mult))
            rounds = [const[:, k:k + 1].rearrange("p (g c) -> p g c", c=1).broadcast_to([P, G, NC]) for k in (3, 4)]
            chain(nc.gpsimd.tensor_tensor(cos_c, sin_c, rounds[0], ALU.add))
            chain(nc.gpsimd.tensor_tensor(cos_c, cos_c, rounds[1], ALU.add))
            nc.gpsimd.tensor_tensor(sin_c, sin_c, cos_c, ALU.subtract).then_inc(sem("phi_ready"), 1)

            pool.wait_ge(sem("bc_in"), 128)
            pool.wait_ge(sem("factors_ready"), 1)
            fr = bcast_last(small[:, 10, :], CH)
            chain(nc.gpsimd.tensor_tensor(bbi, bi, fr, ALU.mult))
            pool.wait_ge(sem("cross_ready"), 1)
            nc.gpsimd.tensor_tensor(bbi, bbi, cross, ALU.add).then_inc(sem("bbi_ready"), 1)
            pool.wait_ge(sem("bbi_ready"), 1)

            pool.wait_ge(sem("tables_ready"), 1)
            for b in range(2 * NB):
                g = slice((b % NB) * GB, (b % NB + 1) * GB)
                if b >= 2:
                    pool.wait_ge(sem("summed"), b - 1)
                left, right, n = (bbi, yy2, STEP) if b < NB else (ci, yy, STEP + 1)
                dst = prod[b % 2][:, 0:GB * n * CH].rearrange("p (g n i) -> p g n i", n=n, i=CH)
                nc.gpsimd.tensor_tensor(
                    dst, left[:, g, :].rearrange("p g (o i) -> p g o i", o=1).broadcast_to([P, GB, n, CH]),
                    right[:, :, g].rearrange("p n (g o) -> p g n o", o=1).broadcast_to([P, GB, n, CH]),
                    ALU.mult).then_inc(sem("product"), 1)

            pool.wait_ge(sem("turn_ready"), 2)
            pool.wait_ge(sem("swapped"), 1)
            nc.gpsimd.tensor_tensor(bsum, bsum, cos_c, ALU.mult).then_inc(sem("bsum_turned"), 1)

            def gain(buf, name, row, after):
                pool.wait_ge(sem(after), NT)
                pool.dma_start(buf[:], row.broadcast_to([P, D])).then_inc(sem(name), 16)

            gain(gain_a, "gain_1_in", a["norms"][0, 1:2, :], "h_ready")
            gain(gain_b, "gain_2_in", a["norms"][0, 3:4, :], "gelu_in")
            gain(gain_a, "gain_3_in", a["norms"][1, 1:2, :], "added_0")
            gain(gain_b, "gain_4_in", a["norms"][1, 3:4, :], "added_1")

        @block.scalar
        def _(act):
            chain = Chain(act, sem("act_chain"))

            squared = [0]

            def squares(rows, ready=None):
                for t in range(NT):
                    if ready:
                        act.wait_ge(sem(ready), t + 1)
                    nc.scalar.activation(xn[:, t, :], rows[t], ACT.Square, accum_out=ss[:, t:t + 1])\
                        .then_inc(sem("squared"), 1)
                squared[0] += NT

            def root():
                act.wait_ge(sem("squared"), squared[0])
                nc.scalar.activation(sd[:], ss[:], ACT.Sqrt, bias=const[:, 0:1], scale=1.0 / D)\
                    .then_inc(sem("root"), 1)

            def load_root_table():
                nc.scalar.activation(scratch[:], const[:, 0:1], ACT.Sqrt)

            x_rows, mix_rows = ([buf[:, t, :] for t in range(NT)] for buf in (x, mix))

            def make_high(n, i):
                act.wait_ge(landed[n % RING], 16 * (n // RING + 1) + i * (16 * PER_EXPERT // RING))
                if n in TAIL_PIECES:
                    act.wait_ge(sem("ffn_tail"), 32)
                if n >= SPLIT:
                    act.wait_ge(sem("used"), i * PER_EXPERT + n - SPLIT + 1)
                nc.scalar.activation(high[:, n % SPLIT, :], raw[:, n % RING, :], ACT.Copy)\
                    .then_inc(sem("high_ready"), 1)

            pieces = Splitter(make_high, 0, MOE0 + SPLIT)

            def high_of_xT(name):
                for b in range(4):
                    act.wait_ge(sem(name + "_v"), b + 1)
                    high_of(tmpT[:, 2 * b:2 * b + 2, :], xT[0][:, 2 * b:2 * b + 2, :], name + "_high")

            def used(n, i=0):
                act.wait_ge(sem("used"), i * PER_EXPERT + n + 1)

            def high_of(src, dst, ready):
                nc.scalar.activation(dst, src, ACT.Copy).then_inc(sem(ready), 1)

            def swiglu(base, i, walk, order, at0, units, blocks, scaled=False):
                one, at = BLOCKS // blocks, {q: at0 + c for c, q in enumerate(order)}
                end = at0 + len(order)
                for j in range(units + 1):
                    if j >= 1:
                        walk.upto(min(at[("w1", j, 0)] + SPLIT if j < units else end, end))
                        for b in range(blocks):
                            act.wait_ge(sem("hid_T"), after(base, j - 1, b, blocks))
                            m = width(order, j - 1, units) // P
                            if b == 0 and j >= 2:
                                used(at[("w2", j - 2, 1)], i)
                            nc.scalar.activation(hidT_hi[:, b, 0:m, :], ps[:, 2 + b, 0:m * P]
                                                 .rearrange("p (m s) -> p m s", m=m), ACT.Copy)\
                                .then_inc(sem("hidT_hi"), one)
                    if j < units:
                        walk.upto(min(at[("w1", j, 1)] + SPLIT, end))
                        used(at[("w1", j, 1)], i)
                        w = width(order, j, units)
                        for b in range(blocks):
                            if j >= 1:
                                act.wait_ge(sem("hid_ready"), after(base, j - 1, b, blocks))
                            nc.scalar.activation(gate_sb[b][:, 0:w], ps[:, b, 0:w], ACT.Silu,
                                                 scale=rstd[:, b:b + 1] if scaled else 1.0)\
                                .then_inc(sem("gate_ready"), one)

            act.wait_ge(sem("lam_in"), 80)
            nc.scalar.activation(small[:, 2, :], small[:, 2, :], ACT.Exp).then_inc(sem("dt_ready"), 1)
            act.wait_ge(sem("mag_in"), 1)
            nc.scalar.activation(mag, mag, ACT.Exp).then_inc(sem("mag_ready"), 1)
            nc.scalar.activation(small[:, 7, :], small[:, 7, :], ACT.Exp).then_inc(sem("mag_ready"), 1)
            act.wait_ge(sem("x_in"), 16)
            act.wait_ge(sem("eps_set"), 3)
            squares(x_rows)
            root()
            def trig(src, sin, cos, tmp, unit, ready, done):
                act.wait_ge(sem(ready), 1)
                chain(nc.scalar.activation(tmp, src, ACT.Abs))
                nc.scalar.activation(sin, src, ACT.Sin, scale=unit).then_inc(sem(done), 1)
                nc.scalar.activation(cos, tmp, ACT.Sin, bias=const[:, 1:2], scale=-unit).then_inc(sem(done), 1)

            trig(ang, sinn, cosn, tmpn, CYCLE, "ang_ready", "trig_ready")
            act.wait_ge(sem("v_in"), 16 * NT)
            nc.scalar.activation(vgrp.rearrange("p g l i -> p l g i"),
                                 vtok.rearrange("p l (g i) -> p l g i", i=CH), ACT.Copy)\
                .then_inc(sem("v_grouped"), 1)
            act.wait_ge(sem("v_grouped"), 1)
            nc.scalar.activation(toep, const[:, 2:3].rearrange("p (g m) -> p g m", g=1).broadcast_to([P, G, P]),
                                 ACT.Copy).then_inc(sem("toep_zero"), 1)
            act.wait_ge(sem("u_transposed"), 1)
            nc.scalar.activation(useq, ps[:, 0:4, :].rearrange("p b (g c) -> p (b g) c", c=NC), ACT.Copy)\
                .then_inc(sem("useq_ready"), 1)
            for b in range(NB):
                act.wait_ge(sem("ba_transposed"), b + 1)
                if b >= 2:
                    act.wait_ge(sem("chunk_sums"), b - 1)
                nc.scalar.activation(wint[b % 2], ps[:, 2 * (b % 2):2 * (b % 2) + 2, :]
                                     .rearrange("p b (g m) -> p (b g) m", m=P), ACT.Copy)\
                    .then_inc(sem("wint_ready"), 1)
            act.wait_ge(sem("chunk_sums"), NB)
            nc.scalar.activation(sums, ps[:, 4:8, :].rearrange("p b (k m) -> p (b k) m", m=P), ACT.Copy)\
                .then_inc(sem("sums_copied"), 1)
            for b in range(NB):
                if b == 2:
                    act.wait_ge(sem("sums_T"), 1)
                    nc.scalar.activation(bsum, ps[:, 4:8, :].rearrange("p b (g c) -> p (b g) c", c=NC), ACT.Copy)\
                        .then_inc(sem("bsum_ready"), 1)
                if b == 3:
                    trig(sin_c, sin_c, cos_c, cos_c, CYCLE, "phi_ready", "turn_ready")
                act.wait_ge(sem("taps_made"), b + 1)
                half, at = b // (NB // 2), (b % (NB // 2)) * GB
                nc.scalar.activation(taps[half][0:CH, at:at + GB, :], ps[0:CH, 2 * (b % 2):2 * (b % 2) + 2, :]
                                     .rearrange("p b (g m) -> p (b g) m", m=P), ACT.Copy)\
                    .then_inc(sem("taps_ready"), 1)
            trig(rope_sin[:], rope_sin[:], rope_cos[:], rope_tmp[:], 1.0, "rope_ready", "rope_done")
            act.wait_ge(sem("y_made"), 2)
            pieces.upto(GLU0 + SPLIT)
            for t in range(NT):
                act.wait_ge(sem("gelu_in"), t + 1)
                nc.scalar.activation(xn[:, t, :], mix[:, t, :], ACT.Gelu_apprx_tanh).then_inc(sem("g_ready"), 1)
            for b in range(4):
                act.wait_ge(sem("g_transposed"), b + 1)
                high_of(ps[:, b, :].rearrange("p (k s) -> p k s", k=2), xT[0][:, 2 * b:2 * b + 2, :], "g_high")
            for n in range(NT):
                pieces.upto(4 * n + 3 + SPLIT)
                used(4 * n + 3)
                for t in range(NT):
                    if n >= 1:
                        act.wait_ge(sem("glu_out"), NT * (n - 1) + t + 1)
                    nc.scalar.activation(gate_sb[t], ps[:, 4 * n + 2 + t, :], ACT.Sigmoid)\
                        .then_inc(sem("glu_sig"), 1)
            load_root_table()
            act.wait_ge(sem("glu_out"), NT * NT)
            squares(mix_rows)
            root()

            squares(x_rows, "added_0")
            high_of_xT("ffn")
            root()
            pieces.upto(FFN0 + SPLIT)
            act.wait_ge(sem("rstd_ready"), 1)
            swiglu(0, 0, pieces, FFN_ORDER, FFN0, FULL + 1, NT, scaled=True)
            load_root_table()
            pieces.upto(KV0 + SPLIT - 1)
            used(KV0 - 1)
            squares([product_rows(4 + 2 * t) for t in range(NT)])
            root()

            squares(x_rows, "added_1")

            def heads(t, bank, dst, name):
                nc.scalar.activation(dst, ps[:, bank, :], ACT.Copy, scale=rstd[:, t:t + 1])\
                    .then_inc(sem(name), 1)

            high_of_xT("kv")
            root()
            pieces.upto(KV0 + SPLIT)
            act.wait_ge(sem("rstd_ready"), 2)
            for c in range(4):
                pieces.upto(KV0 + 2 * c + 1 + SPLIT)
                used(KV0 + 2 * c + 1)
                for t in range(NT):
                    if c < 2:
                        heads(t, 2 * c + t, mix[:, t, c * BK:(c + 1) * BK], "k_copied")
                    else:
                        heads(t, 2 * c + t, v[:, t, (c - 2) * BK:(c - 1) * BK], "v_copied")
            high_of_xT("q")
            for b in range(4):
                act.wait_ge(sem("k_transposed"), b + 1)
                nc.scalar.activation(kT[:, 2 * b:2 * b + 2, :], ps[:, 4 + b, :]
                                     .rearrange("p (k s) -> p k s", k=2), ACT.Copy).then_inc(sem("kT_ready"), 1)
            for c in range(2):
                pieces.upto(Q0 + 2 * c + 1 + SPLIT)
                used(Q0 + 2 * c + 1)
                for t in range(NT):
                    heads(t, 2 * c + t, mix[:, t, c * BK:(c + 1) * BK], "q_copied")
            for b in range(4):
                act.wait_ge(sem("q_transposed"), b + 1)
                nc.scalar.activation(qT[:, 2 * b:2 * b + 2, :], ps[:, 4 + b, :]
                                     .rearrange("p (k s) -> p k s", k=2), ACT.Copy).then_inc(sem("qT_ready"), 1)
            pieces.upto(O0 + SPLIT)
            for h in range(HEADS + 3):
                if h < HEADS:
                    act.wait_ge(sem("score_max"), h + 1)
                    if h >= 3:
                        act.wait_ge(sem("prob_transposed"), h - 2)
                    for t in range(NT):
                        cols = slice(0, P) if t == 0 else slice(P, 3 * P)
                        nc.scalar.activation(prob[h % 3][:, cols], ps[:, SCORES[h % 3], cols], ACT.Exp,
                                             scale=SCALE, bias=soft[:, h, 1, t:t + 1],
                                             accum_out=soft[:, h, 2, t:t + 1]).then_inc(sem("exped"), 1)
                if h >= 3:
                    k = h - 3
                    act.wait_ge(sem("o_made"), k + 1)
                    high_of(ps[:, 4 + k % 2, 0:S], xT[0][:, k, :], "o_high")
                if 2 <= h < HEADS + 2:
                    k = h - 2
                    act.wait_ge(sem("prob_transposed"), k + 1)
                    if k >= 2:
                        act.wait_ge(sem("o_made"), k - 1)
                    nc.scalar.activation(probT[k % 2], ps[:, 2 + k % 2, 0:384]
                                         .rearrange("p (m s) -> p m s", m=3), ACT.Copy)\
                        .then_inc(sem("probT_ready"), 1)
            load_root_table()
            pieces.upto(MOE0 + SPLIT - 1)
            used(MOE0 - 1)
            squares([product_rows(2 * t) for t in range(NT)])
            root()
            pieces.upto(MOE0 + SPLIT)

            squares(x_rows, "added_2")
            root()

            def high_of_expert(b):
                def steps(i, blocks):
                    if b < blocks:
                        act.wait_ge(sem("expert_v"), after(i * BLOCKS, 0, b, blocks))
                        nc.scalar.activation(xTe[0][:, b], tmpTe[:, b], ACT.Copy)\
                            .then_inc(sem("expert_high"), BLOCKS // blocks)
                return steps

            def hidden(i, blocks):
                walk = expert_pieces(make_high, i)
                swiglu(i * STEPS + FFN_STEPS, i, walk, ORDER, MOE0, UNITS, blocks)
                by_blocks(act, i + 1, high_of_expert(0))
                with act.If(i < E - 1):
                    walk.upto(MOE0 + PER_EXPERT + 2)
                for half in range(2):
                    if half == 0:
                        act.wait_ge(sem("first_halves"), i + 1)
                    else:
                        used(MOE0 + PER_EXPERT - 1, i)
                    for b in range(blocks):
                        last = nc.scalar.activation(y_rows[:, b, half * BK:(half + 1) * BK],
                                                    ps[:, 4 + 2 * b + half, :], ACT.Copy)
                    last.then_inc(sem("y_rows"), 1)
                with act.If(i < E - 1):
                    walk.upto(MOE0 + PER_EXPERT + SPLIT)

            act.wait_ge(sem("gap_ready"), 1)
            nc.scalar.activation(rs[:, 4, :], rs[:, 4, :], ACT.Exp).then_inc(sem("gap_exp"), 1)
            act.wait_ge(sem("routed"), 1)
            for b in range(BLOCKS):
                by_blocks(act, 0, high_of_expert(b))
            with act.Fori(0, E) as i:
                act.wait_ge(sem("weighted_T"), i + 1)
                nc.scalar.activation(weightedT, ps[:, 3, :].rearrange("p (t s) -> p t s", t=BLOCKS), ACT.Copy)\
                    .then_inc(sem("weightedT_ready"), 1)
                by_blocks(act, i, hidden)
                by_blocks(act, i + 1, high_of_expert(1))
            load_root_table()
            act.wait_ge(sem("acc_done"), 1)
            squares(mix_rows)
            root()

        @block.vector
        def _(dve):
            chain = Chain(dve, sem("dve_chain"))
            rooted = [0]
            TT, TS, STT = nc.vector.tensor_tensor, nc.vector.tensor_scalar, nc.vector.scalar_tensor_tensor

            def inverse_root():
                rooted[0] += 1
                dve.wait_ge(sem("root"), rooted[0])
                chain(nc.vector.reciprocal(rstd[:], sd[:]))

            def reduce_angle(v, tmp):
                chain(TS(tmp, v, INV_2PI, ROUND, ALU.mult, ALU.add))
                chain(TS(tmp, tmp, -ROUND, None, ALU.add))
                chain(STT(out=v, in0=tmp, scalar=-TWO_PI_HI, in1=v, op0=ALU.mult, op1=ALU.add))
                chain(STT(out=v, in0=tmp, scalar=-TWO_PI_LO, in1=v, op0=ALU.mult, op1=ALU.add))
                return TS(v, v, PI_BELOW, -PI_BELOW, ALU.min, ALU.max)

            def less_integer(v, tmp):
                chain(TS(tmp, v, ROUND, None, ALU.add))
                chain(TS(tmp, tmp, -ROUND, None, ALU.add))
                return TT(v, v, tmp, ALU.subtract)

            sm = [small[:, k, :] for k in range(14)]
            lr, li, dt, zr, zi, tmp, r8, m8, den, am1, cfr, cfi, t1, t2 = sm
            dve.wait_ge(sem("dt_ready"), 1)
            dve.wait_ge(sem("iotas"), 3 + HALF)
            chain(TT(zr, lr, dt, ALU.mult))
            chain(TT(zi, li, dt, ALU.mult))
            chain(TS(m8, zr, float(STEP), None, ALU.mult))
            TT(mag, bcast_mid(zr, NPOW), bcast_last(powers[:], G), ALU.mult).then_inc(sem("mag_in"), 1)
            chain(reduce_angle(zi, tmp))
            chain(TS(zi, zi, INV_2PI, None, ALU.mult))
            chain(TT(ang, bcast_mid(zi, NPOW), bcast_last(powers[:], G), ALU.mult))
            less_integer(ang, tmpn).then_inc(sem("ang_ready"), 1)
            chain(TS(r8, zi, float(STEP), None, ALU.mult))
            less_integer(r8, tmp).then_inc(sem("r8_ready"), 1)
            inverse_root()
            dve.wait_ge(sem("gain_a_in"), 16)
            for t in range(NT):
                STT(out=xn[:, t, :], in0=x[:, t, :], scalar=rstd[:, t:t + 1], in1=gain_a[:],
                    op0=ALU.mult, op1=ALU.mult).then_inc(sem("h_ready"), 1)
            dve.wait_ge(sem("mag_ready"), 2)
            dve.wait_ge(sem("trig_ready"), 2)
            chain(TT(cosn, cosn, mag, ALU.mult))
            chain(TT(sinn, sinn, mag, ALU.mult))
            re, im = slice(0, 64), slice(64, P)
            up, down = slice(0, STEP + 1), slice(STEP + 1, NPOW)
            chain(nc.vector.tensor_copy(xx[re], cosn[re, up, :]))
            chain(TS(xx[im], sinn[im, up, :], -1.0, None, ALU.mult))
            chain(TS(yy[re], sinn[re, up, :], -1.0, None, ALU.mult))
            chain(TS(yy[im], cosn[im, up, :], -1.0, None, ALU.mult))
            chain(nc.vector.tensor_copy(xx2[re], cosn[re, down, :]))
            chain(nc.vector.tensor_copy(xx2[im], sinn[im, down, :]))
            chain(TS(yy2[re], sinn[re, down, :], -1.0, None, ALU.mult))
            chain(nc.vector.tensor_copy(yy2[im], cosn[im, down, :]))
            ar, ai = cosn[:, 1, :], sinn[:, 1, :]
            chain(TT(t1, lr, lr, ALU.mult))
            chain(TT(t2, li, li, ALU.mult))
            chain(TT(t1, t1, t2, ALU.add))
            chain(nc.vector.reciprocal(den, t1))
            chain(TS(am1, ar, -1.0, None, ALU.add))
            chain(TT(t1, am1, lr, ALU.mult))
            chain(TT(t2, ai, li, ALU.mult))
            chain(TT(t1, t1, t2, ALU.add))
            chain(TT(cfr, t1, den, ALU.mult))
            chain(TT(t1, ai, lr, ALU.mult))
            chain(TT(t2, am1, li, ALU.mult))
            chain(TT(t1, t1, t2, ALU.subtract))
            TT(cfi, t1, den, ALU.mult).then_inc(sem("factors_ready"), 1)
            dve.wait_ge(sem("factors_ready"), 1)
            dve.wait_ge(sem("bc_in"), 128)
            tmpb = view(work, 10432, G, CH)
            fr, fi = bcast_last(cfr, CH), bcast_last(cfi, CH)
            TT(cross, br, fi, ALU.mult).then_inc(sem("cross_ready"), 1)
            chain(TT(bbr, br, fr, ALU.mult))
            chain(TT(tmpb, bi, fi, ALU.mult))
            chain(TT(bbr, bbr, tmpb, ALU.subtract))
            nc.vector.tensor_copy(bstk[re], bbr[re]).then_inc(sem("tables_ready"), 1)
            for b in range(2 * NB):
                g = slice((b % NB) * GB, (b % NB + 1) * GB)
                if b < NB:
                    if b == 2:
                        dve.wait_ge(sem("bbi_ready"), 1)
                        chain(nc.vector.tensor_copy(bstk[im], bbi[im]))
                    if b >= 2:
                        dve.wait_ge(sem("ba_transposed"), b - 1)
                    left, right, n = bbr, xx2, STEP
                    dst = ba[b % 2].rearrange("p g (n i) -> p g n i", n=n)
                else:
                    if b == NB:
                        dve.wait_ge(sem("u_transposed"), 1)
                    left, right, n = cr, xx, STEP + 1
                    dst = ca[:, g]
                chain(TT(dst, left[:, g, :].rearrange("p g (o i) -> p g o i", o=1).broadcast_to([P, GB, n, CH]),
                         right[:, :, g].rearrange("p n (g o) -> p g n o", o=1).broadcast_to([P, GB, n, CH]),
                         ALU.mult))
                dve.wait_ge(sem("product"), b + 1)
                TT(dst, dst, prod[b % 2][:, 0:GB * n * CH].rearrange("p (g n i) -> p g n i", n=n, i=CH),
                   ALU.add).then_inc(sem("summed"), 1)
            dve.wait_ge(sem("summed"), 2 * NB)
            chain(nc.vector.tensor_copy(decay, bcast_last(m8, NC)))
            chain(nc.vector.memset(decay[:, :, 0:1], 0.0))
            chain(nc.vector.memset(sprev[:, :, 0:1], 0.0))
            dve.wait_ge(sem("turn_ready"), 2)
            dve.wait_ge(sem("swapped"), 1)
            swapped = ps[:, 4:8, :].rearrange("p b (g c) -> p (b g) c", c=NC)
            chain(TT(state, swapped, sin_c, ALU.mult))
            dve.wait_ge(sem("bsum_turned"), 1)
            chain(TT(bsum, bsum, state, ALU.add))
            flat = "p g c -> p (g c)"
            nc.vector.tensor_tensor_scan(state.rearrange(flat), decay.rearrange(flat), bsum.rearrange(flat),
                                         0.0, ALU.mult, ALU.add).then_inc(sem("scanned"), 1)
            dve.wait_ge(sem("scanned"), 1)
            chain(TT(bsum, state, cos_c, ALU.mult))
            dve.wait_ge(sem("pos_in"), 16)
            chain(nc.vector.tensor_copy(posf[:], posi[:]))
            chain(TT(rope_sin[:].rearrange("p (t k) -> p t k", t=NT), bcast_last(posf[:], HALF),
                     bcast_mid(freq[:], NT), ALU.mult))
            reduce_angle(rope_sin[:], rope_tmp[:]).then_inc(sem("rope_ready"), 1)
            dve.wait_ge(sem("swapped"), 2)
            chain(TT(decay, swapped, sin_c, ALU.mult))
            TT(sprev[:, :, 1:NC + 1], bsum, decay, ALU.subtract).then_inc(sem("states_ready"), 1)
            dve.wait_ge(sem("gain_b_in"), 16)
            dve.wait_ge(sem("v_in"), 16 * NT)
            for t in range(NT):
                chain(TT(xn[:, t, :], xn[:, t, :], gain_b[:], ALU.mult))

            def make_low(n, i):
                dve.wait_ge(sem("high_ready"), i * PER_EXPERT + n + 1)
                TT(low[:, n % SPLIT, :], raw[:, n % RING, :], high[:, n % SPLIT, :].bitcast(F32), ALU.subtract)\
                    .then_inc(sem("low_ready"), 1)

            pieces = Splitter(make_low, 0, MOE0 + SPLIT)

            def used(n, i=0):
                dve.wait_ge(sem("used"), i * PER_EXPERT + n + 1)

            def swiglu(base, i, walk, order, at0, units, blocks, scaled=False):
                one, at = BLOCKS // blocks, {q: at0 + c for c, q in enumerate(order)}
                end = at0 + len(order)
                for j in range(units + 1):
                    if j >= 1:
                        walk.upto(min(at[("w1", j, 0)] + SPLIT if j < units else end, end))
                        m = width(order, j - 1, units) // P
                        for b in range(blocks):
                            dve.wait_ge(sem("hidT_hi"), after(base, j - 1, b, blocks))
                            TT(hidT_lo[:, b, 0:m, :], ps[:, 2 + b, 0:m * P].rearrange("p (m s) -> p m s", m=m),
                               hidT_hi[:, b, 0:m, :].bitcast(F32), ALU.subtract).then_inc(sem("hidT_ready"), one)
                    if j < units:
                        w = width(order, j, units)
                        last_up = at[("w3", j, 1)] if w == BK else at[("w1", j, 1)]
                        walk.upto(min(last_up + SPLIT, end))
                        used(last_up, i)
                        for b in range(blocks):
                            dve.wait_ge(sem("gate_ready"), after(base, j, b, blocks))
                            if j >= 1:
                                dve.wait_ge(sem("hid_T"), after(base, j - 1, b, blocks))
                            up3 = ps[:, 2 + b, 0:w] if w == BK else ps[:, b, w:2 * w]
                            if scaled:
                                ins = STT(out=hid[b][:, 0:w], in0=up3, scalar=rstd[:, b:b + 1],
                                          in1=gate_sb[b][:, 0:w], op0=ALU.mult, op1=ALU.mult)
                            else:
                                ins = TT(hid[b][:, 0:w], gate_sb[b][:, 0:w], up3, ALU.mult)
                            ins.then_inc(sem("hid_ready"), one)

            dve.wait_ge(sem("y_made"), 1)
            own, before = (ps[:, k:k + 4, :].rearrange("p b (g l i) -> p (b g) l i", l=STEP, i=CH) for k in (0, 4))
            y_all = ytile.rearrange("p l g i -> p g l i")
            chain(nc.vector.tensor_copy(y_all, own))
            dve.wait_ge(sem("y_made"), 2)
            TT(y_all, y_all, before, ALU.add).then_inc(sem("y_copied"), 1)
            pieces.upto(GLU0 + SPLIT - 1)
            for t in range(NT):
                dve.wait_ge(sem(f"y_in_{t}"), 64)
                TT(mix[:, t, :], mix[:, t, :], xn[:, t, :], ALU.add).then_inc(sem("gelu_in"), 1)
            pieces.upto(GLU0 + SPLIT)
            for b in range(4):
                dve.wait_ge(sem("g_high"), b + 1)
                TT(xT[1][:, 2 * b:2 * b + 2, :], ps[:, b, :].rearrange("p (k s) -> p k s", k=2),
                   xT[0][:, 2 * b:2 * b + 2, :].bitcast(F32), ALU.subtract).then_inc(sem("gT_ready"), 1)
            for n in range(NT):
                pieces.upto(4 * n + 3 + SPLIT)
                for t in range(NT):
                    dve.wait_ge(sem("glu_sig"), NT * n + t + 1)
                    TT(mix[:, t, n * BK:(n + 1) * BK], ps[:, 4 * n + t, :], gate_sb[t], ALU.mult)\
                        .then_inc(sem("glu_out"), 1)

            mix_rows = [mix[:, t, :] for t in range(NT)]

            def post(rows, gain, gain_sem, name):
                inverse_root()
                dve.wait_ge(sem(gain_sem), 16)
                for t in range(NT):
                    chain(STT(out=xn[:, t, :], in0=rows[t], scalar=rstd[:, t:t + 1], in1=gain[:],
                              op0=ALU.mult, op1=ALU.mult))
                    TT(x[:, t, :], x[:, t, :], xn[:, t, :], ALU.add).then_inc(sem(name), 1)

            def by_channel(name, gains, bank=0):
                for b in range(4 + 1):
                    if b < 4:
                        dve.wait_ge(sem("q_in_transposed" if name == "q" else name + "_transposed"), b + 1)
                        TT(tmpT[:, 2 * b:2 * b + 2, :], ps[:, bank + b, :].rearrange("p (k s) -> p k s", k=2),
                           bcast_last(gains[:, 2 * b:2 * b + 2], S), ALU.mult).then_inc(sem(name + "_v"), 1)
                    if b >= 1 and name != "moe":
                        dve.wait_ge(sem(name + "_high"), b)
                        TT(xT[1][:, 2 * b - 2:2 * b, :], tmpT[:, 2 * b - 2:2 * b, :],
                           xT[0][:, 2 * b - 2:2 * b, :].bitcast(F32), ALU.subtract).then_inc(sem(name + "_xT"), 1)

            def root_of_x():
                rooted[0] += 1
                dve.wait_ge(sem("root"), rooted[0])
                nc.vector.reciprocal(rstd[:], sd[:]).then_inc(sem("rstd_ready"), 1)

            post(mix_rows, gain_a, "gain_1_in", "added_0")
            dve.wait_ge(sem("const_in"), 64)
            by_channel("ffn", gcol[:, 2, :])
            pieces.upto(FFN0 + SPLIT)
            root_of_x()
            dve.wait_ge(sem("rstd_ready"), 1)
            swiglu(0, 0, pieces, FFN_ORDER, FFN0, FULL + 1, NT, scaled=True)
            pieces.upto(KV0 + SPLIT - 1)
            post([product_rows(4 + 2 * t) for t in range(NT)], gain_b, "gain_2_in", "added_1")
            by_channel("kv", kvcol[:])
            pieces.upto(KV0 + SPLIT)
            root_of_x()
            dve.wait_ge(sem("rope_done"), 2)

            turned = [0]

            def turn_heads(t, rows, done):
                src = rows.rearrange("p (h d) -> p h d", d=DH)
                x1, x2 = src[:, :, 0:HALF], src[:, :, HALF:ROT]
                cos = bcast_mid(rope_cos[:, t * HALF:(t + 1) * HALF], 4)
                sin = bcast_mid(rope_sin[:, t * HALF:(t + 1) * HALF], 4)
                chain(TT(rot[0], x1, cos, ALU.mult))
                chain(TT(rot[1], x2, sin, ALU.mult))
                chain(TT(rot[2], x2, cos, ALU.mult))
                chain(TT(rot[3], x1, sin, ALU.mult))
                chain(TT(x1, rot[0], rot[1], ALU.subtract))
                TT(x2, rot[2], rot[3], ALU.add).then_inc(sem(done), 1)
                turned[0] += 1
                dve.wait_ge(sem(done), turned[0])

            for c in range(4):
                pieces.upto(KV0 + 2 * c + 1 + SPLIT)
                if c < 2:
                    for t in range(NT):
                        dve.wait_ge(sem("k_copied"), 2 * c + t + 1)
                        turn_heads(t, mix[:, t, c * BK:(c + 1) * BK], "k_turned")
            by_channel("q", gcol[:, 4, :])
            turned = [0]
            for c in range(2):
                pieces.upto(Q0 + 2 * c + 1 + SPLIT)
                for t in range(NT):
                    dve.wait_ge(sem("q_copied"), 2 * c + t + 1)
                    turn_heads(t, mix[:, t, c * BK:(c + 1) * BK], "q_turned")
            pieces.upto(O0 + SPLIT)
            dve.wait_ge(sem("masks_ready"), 3)
            def normalise(h):
                dve.wait_ge(sem("exped"), NT * (h + 1))
                chain(nc.vector.reciprocal(soft[:, h, 3, :], soft[:, h, 2, :]))
                p = prob[h % 3]
                TS(p[:, 0:P], p[:, 0:P], soft[:, h, 3, 0:1], None, ALU.mult).then_inc(sem("prob_ready"), 1)
                TS(p[:, P:3 * P], p[:, P:3 * P], soft[:, h, 3, 1:2], None, ALU.mult)\
                    .then_inc(sem("prob_ready"), 1)

            for h in range(HEADS + 3):
                if h < HEADS:
                    dve.wait_ge(sem("scores"), h + 1)
                    s = ps[:, SCORES[h % 3], :]
                    chain(nc.vector.reduce_max(soft[:, h, 0, 0:1], s[:, 0:P], AX_X))
                    chain(nc.vector.reduce_max(soft[:, h, 0, 1:2], s[:, P:3 * P], AX_X))
                    TS(soft[:, h, 1, :], soft[:, h, 0, :], -SCALE, None, ALU.mult).then_inc(sem("score_max"), 1)
                if 1 <= h <= HEADS:
                    normalise(h - 1)
                if h >= 3:
                    k = h - 3
                    dve.wait_ge(sem("o_high"), k + 1)
                    TT(xT[1][:, k, :], ps[:, 4 + k % 2, 0:S], xT[0][:, k, :].bitcast(F32), ALU.subtract)\
                        .then_inc(sem("oT_ready"), 1)
            pieces.upto(MOE0 + SPLIT - 1)
            post([product_rows(2 * t) for t in range(NT)], gain_a, "gain_3_in", "added_2")
            pieces.upto(MOE0 + SPLIT)
            by_channel("moe", gcol[:, 6, :], 4)
            inverse_root()
            lg, eq, cand, oh1, oh2, sel, w, iota_e, far = (rt[:, k] for k in range(9))
            m1, i1, m2, i2, gap, den, w1, w2 = (rs[:, k, :] for k in range(8))
            wide = lambda ap: bcast_last(ap, E)
            chain(nc.vector.tensor_copy(iota_e, bcast_mid(iota_c[:, 0:E], NT)))
            chain(TS(far, iota_e, 99.0, None, ALU.add))
            for t in range(NT):
                TS(xn[:, t, :], x[:, t, :], rstd[:, t:t + 1], None, ALU.mult).then_inc(sem("moe_xn"), 1)
            for t in range(NT):
                nc.vector.memset(acc[:, t, :], 0.0).then_inc(sem("added"), 2)
            dve.wait_ge(sem("added"), 4)
            dve.wait_ge(sem("logits"), 1)
            for t in range(NT):
                chain(STT(out=lg[:, t, :], in0=ps[:, 0, t * E:(t + 1) * E], scalar=rstd[:, t:t + 1],
                          in1=rbias[:], op0=ALU.mult, op1=ALU.add))
            for m, i, oh in ((m1, i1, oh1), (m2, i2, oh2)):
                chain(nc.vector.reduce_max(m, lg, AX_X))
                chain(TT(eq, lg, wide(m), ALU.is_equal))
                chain(STT(out=cand, in0=eq, scalar=-99.0, in1=far, op0=ALU.mult, op1=ALU.add))
                chain(nc.vector.tensor_reduce(i, cand, axis=AX_X, op=ALU.min))
                chain(TT(oh, iota_e, wide(i), ALU.is_equal))
                if oh is oh1:
                    chain(STT(out=lg, in0=oh, scalar=NEG, in1=lg, op0=ALU.mult, op1=ALU.add))
            TT(gap, m2, m1, ALU.subtract).then_inc(sem("gap_ready"), 1)
            TT(sel, oh1, oh2, ALU.add).then_inc(sem("sel_ready"), 1)
            dve.wait_ge(sem("gap_exp"), 1)
            chain(TS(den, gap, 1.0, None, ALU.add))
            chain(nc.vector.reciprocal(w1, den))
            chain(TT(w2, gap, w1, ALU.mult))
            chain(TT(cand, oh1, wide(w1), ALU.mult))
            chain(TT(w, oh2, wide(w2), ALU.mult))
            chain(TT(w, w, cand, ALU.add))
            chain(nc.vector.tensor_copy(wgt[:, :, 0:E], w))
            chain(nc.vector.memset(wgt[:, :, E:E + 1], 0.0))
            dve.wait_ge(sem("places"), 1)
            place = ps[:, 1, 0:NT * E].rearrange("p (t e) -> p t e", t=NT)
            chain(STT(out=cand, in0=place, scalar=1.0, in1=sel, op0=ALU.add, op1=ALU.mult))
            chain(TS(slot[:, :, 0:E], cand, -1.0, None, ALU.add))
            chain(nc.vector.memset(slot[:, :, E:E + 1], -1.0))
            chain(nc.vector.memset(count[:, E:E + 1], 0))
            nc.vector.tensor_copy(count[:, 0:E], ps[:, 2, 0:E]).then_inc(sem("routed"), 1)
            dve.wait_ge(sem("routed"), 1)

            def one_hots(i):
                for t in range(NT):
                    TS(onehot[:, t, :], iota_c[:], slot[:, t, bass.ds(i, 1)], None, ALU.is_equal)\
                        .then_inc(sem("onehot_ready"), 1)

            def weighted_one_hots(i):
                for t in range(NT):
                    TS(weighted[:, t, :], iota_c[:], slot[:, t, bass.ds(i, 1)], wgt[:, t, bass.ds(i, 1)],
                       ALU.is_equal, ALU.mult).then_inc(sem("weighted_ready"), 1)

            def gathered_in(b):
                def steps(i, blocks):
                    if b < blocks:
                        dve.wait_ge(sem("gathered"), after(i * BLOCKS, 0, b, blocks))
                        TT(tmpTe[:, b], ps[:, 2 * b:2 * b + 2, :].rearrange("p b (k s) -> p (b k) s", s=P),
                           bcast_last(gcol[:, 6, :], P), ALU.mult).then_inc(sem("expert_v"), BLOCKS // blocks)
                        dve.wait_ge(sem("expert_high"), after(i * BLOCKS, 0, b, blocks))
                        TT(xTe[1][:, b], tmpTe[:, b], xTe[0][:, b].bitcast(F32), ALU.subtract)\
                            .then_inc(sem("xTe_ready"), BLOCKS // blocks)
                return steps

            def hidden(i, blocks):
                walk = expert_pieces(make_low, i)
                swiglu(i * STEPS + FFN_STEPS, i, walk, ORDER, MOE0, UNITS, blocks)
                by_blocks(dve, i + 1, gathered_in(0))
                with dve.If(i < E - 1):
                    walk.upto(MOE0 + PER_EXPERT + SPLIT)

            one_hots(0)
            weighted_one_hots(0)
            for b in range(BLOCKS):
                by_blocks(dve, 0, gathered_in(b))
            with dve.Fori(0, E) as i:
                dve.wait_ge(sem("gathered"), i * BLOCKS + BLOCKS)
                one_hots(i + 1)
                dve.wait_ge(sem("weighted_T"), i + 1)
                weighted_one_hots(i + 1)
                by_blocks(dve, i, hidden)
                by_blocks(dve, i + 1, gathered_in(1))
                for k, q in enumerate((0, 2, 1, 3)):
                    dve.wait_ge(sem("combined"), i * 4 + k + 1)
                    dst = acc[:, q // 2, (q % 2) * BK:(q % 2 + 1) * BK]
                    TT(dst, dst, ps[:, 4 + q, :], ALU.add).then_inc(sem("added"), 1)
                dve.wait_ge(sem("added"), i * 4 + 8)
            nc.vector.memset(rs[:, 2, :], 0.0).then_inc(sem("acc_done"), 1)
            post(mix_rows, gain_b, "gain_4_in", "x_final")

        @block.tensor
        def _(pe):
            mm = nc.tensor.matmul

            def mm3(out, left, right, first, last):
                mm(out, left[0], right[0], start=first, stop=False)
                mm(out, left[0], right[1], start=False, stop=False)
                return mm(out, left[1], right[0], start=False, stop=last)

            def split_ready(n, i=0):
                pe.wait_ge(sem("low_ready"), i * PER_EXPERT + n + 1)

            second_half = []

            def channels_ready(name):
                pe.wait_ge(sem(name), 2)
                second_half.append(name)

            def up_half(banks, lhs, n, k, i=0):
                split_ready(n, i)
                if k == 1 and second_half:
                    pe.wait_ge(sem(second_half.pop()), 4)
                w = split_of(n)
                for b, bank in enumerate(banks):
                    for f in range(4):
                        last = mm3(ps[:, bank, :], lhs(b, 4 * k + f), [t[:, f, :] for t in w],
                                   k == 0 and f == 0, k == 1 and f == 3)
                last.then_inc(sem("used"), 1)

            def swiglu(base, i, order, at0, units, blocks, lhs, y_free, around_last_T=None,
                       up_banks_free=lambda: None):
                one, at = BLOCKS // blocks, {q: at0 + c for c, q in enumerate(order)}
                for j in range(units + 1):
                    if j < units:
                        if j >= 1:
                            pe.wait_ge(sem("gate_ready"), after(base, j - 1, blocks - 1, blocks))
                        up_half(range(blocks), lhs, at[("w1", j, 0)], 0, i)
                    if j >= 1:
                        m = width(order, j - 1, units) // P
                        if j == units and around_last_T:
                            pe.wait_ge(sem("gate_ready"), after(base, j - 1, blocks - 1, blocks))
                            around_last_T(0)
                        for b in range(blocks):
                            pe.wait_ge(sem("hid_ready"), after(base, j - 1, b, blocks))
                            for f in range(m):
                                last = nc.tensor.transpose(ps[:, 2 + b, f * P:(f + 1) * P],
                                                           hid[b][:, f * P:(f + 1) * P], ident[:])
                            last.then_inc(sem("hid_T"), one)
                        if j == units and around_last_T:
                            around_last_T(1)
                    if j < units:
                        up_half(range(blocks), lhs, at[("w1", j, 1)], 1, i)
                    if j >= 1:
                        if j == 1:
                            y_free()
                        pe.wait_ge(sem("hidT_ready"), after(base, j - 1, blocks - 1, blocks))
                        for k in range(m // 2):
                            n = at[("w2", j - 1, k)]
                            split_ready(n, i)
                            w = split_of(n, down=True)
                            ends = j == units and k == m // 2 - 1
                            for half in range(2):
                                for b in range(blocks):
                                    for f in range(2):
                                        last = mm3(ps[:, 4 + 2 * b + half, :],
                                                   [t[:, b, 2 * k + f, :] for t in hidT],
                                                   [t[:, f, half * BK:(half + 1) * BK] for t in w],
                                                   j == 1 and k == 0 and f == 0, ends and f == 1)
                                if ends and half == 0 and around_last_T:
                                    last.then_inc(sem("first_halves"), 1)
                            last.then_inc(sem("used"), 1)
                    if j < units and width(order, j, units) == BK:
                        if j == 0:
                            up_banks_free()
                        for k in range(2):
                            up_half([2 + b for b in range(blocks)], lhs, at[("w3", j, k)], k, i)

            def by_token(b, kt):
                return [t[:, kt, b * P:(b + 1) * P] for t in xT]

            def transposes(src, ready, name, bank=0):
                for t in range(NT):
                    if ready:
                        pe.wait_ge(sem(ready), t + 1)
                    for b in range(4):
                        for k in range(2):
                            kt = 2 * b + k
                            last = nc.tensor.transpose(ps[:, bank + b, k * S + t * P:k * S + (t + 1) * P],
                                                       src[:, t, kt * P:(kt + 1) * P], ident[:])
                        if t == NT - 1:
                            last.then_inc(sem(name), 1)

            pe.wait_ge(sem("ident_ready"), 1)
            pe.wait_ge(sem("v_grouped"), 1)
            for g in range(G):
                last = nc.tensor.transpose(ps[:, g // 16, (g % 16) * NC:(g % 16 + 1) * NC],
                                           vgrp[:, g].rearrange("p l i -> p (l i)"), ident[0:NC, 0:NC])
            last.then_inc(sem("u_transposed"), 1)

            def chunk_sums(b):
                pe.wait_ge(sem("wint_ready"), b + 1)
                for k in range(GB):
                    g = b * GB + k
                    q, at = g % 4, (g // 4) % 4 * P
                    last = mm(ps[32 * q:32 * q + 32, 4 + g // 16, at:at + P], useq[:, g, :],
                              wint[b % 2][:, k, :], start=True, stop=True, tile_position=(0, 32 * q))
                last.then_inc(sem("chunk_sums"), 1)

            pe.wait_ge(sem("useq_ready"), 1)
            for b in range(NB):
                pe.wait_ge(sem("summed"), b + 1)
                if b >= 2:
                    pe.wait_ge(sem("wint_ready"), b - 1)
                for k in range(GB):
                    last = nc.tensor.transpose(ps[:, 2 * (b % 2) + k // 4, (k % 4) * P:(k % 4 + 1) * P],
                                               ba[b % 2][:, k, :], ident[:])
                last.then_inc(sem("ba_transposed"), 1)
                if b >= 1:
                    chunk_sums(b - 1)
            chunk_sums(NB - 1)
            def swap_parts(src):
                flat = src.rearrange("p g c -> p (g c)")
                for b in range(4):
                    last = mm(ps[:, 4 + b, :], swap[:], flat[:, b * BK:(b + 1) * BK], start=True, stop=True)
                last.then_inc(sem("swapped"), 1)

            pe.wait_ge(sem("swap_ready"), 1)
            for b in range(NB):
                if b == 2:
                    pe.wait_ge(sem("sums_copied"), 1)
                    for k in range(G // 4):
                        last = nc.tensor.transpose(ps[:, 4 + k // 4, (k % 4) * P:(k % 4 + 1) * P],
                                                   sums[:, k, :], ident[:])
                    last.then_inc(sem("sums_T"), 1)
                if b == 4:
                    pe.wait_ge(sem("bsum_ready"), 1)
                    swap_parts(bsum)
                pe.wait_ge(sem("summed"), NB + b + 1)
                if b >= 2:
                    pe.wait_ge(sem("taps_ready"), b - 1)
                for k in range(GB):
                    g = b * GB + k
                    last = mm(ps[0:CH, 2 * (b % 2) + k // 4, (k % 4) * P:(k % 4 + 1) * P], bstk[:, g, :],
                              ca[:, g, 0:STEP, :].rearrange("p n i -> p (n i)"), start=True, stop=True)
                last.then_inc(sem("taps_made"), 1)
            pe.wait_ge(sem("scanned"), 1)
            swap_parts(state)
            pe.wait_ge(sem("taps_ready"), NB)
            pe.wait_ge(sem("toep_in"), 16 * 2 * STEP)
            for own in (True, False):
                if not own:
                    pe.wait_ge(sem("states_ready"), 1)
                for g4 in range(GQ):
                    for q in range(4):
                        g = q * GQ + g4
                        dst = ps[32 * q:32 * q + 32, (0 if own else 4) + g4 // 4, (g4 % 4) * P:(g4 % 4 + 1) * P]
                        if own:
                            left, right = useq[:, g, :], toep[:, g, :]
                        else:
                            left = sprev[:, g, 0:NC]
                            right = ca[:, g, 1:STEP + 1, :].rearrange("p n i -> p (n i)")
                        last = mm(dst, left, right, start=True, stop=True, tile_position=(0, 32 * q))
                last.then_inc(sem("y_made"), 1)

            pe.wait_ge(sem("y_copied"), 1)
            transposes(xn, "g_ready", "g_transposed")
            channels_ready("gT_ready")
            for n in range(NT):
                for c in range(4):
                    up_half([4 * n + 2 * (c // 2) + t for t in range(NT)], by_token, GLU0 + 4 * n + c, c % 2)

            transposes(x, "added_0", "ffn_transposed")
            channels_ready("ffn_xT")
            swiglu(0, 0, FFN_ORDER, FFN0, FULL + 1, NT, by_token, lambda: None)

            transposes(x, "added_1", "kv_transposed")
            channels_ready("kv_xT")
            for n in range(KV0, Q0):
                c, k = divmod(n - KV0, 2)
                up_half([2 * c + t for t in range(NT)], by_token, n, k)
            pe.wait_ge(sem("k_copied"), 2 * NT)
            transposes(x, None, "q_in_transposed")
            pe.wait_ge(sem("k_turned"), 2 * NT)
            pe.wait_ge(sem("v_copied"), 2 * NT)
            transposes(mix, None, "k_transposed", 4)
            channels_ready("q_xT")
            for n in range(Q0, O0):
                c, k = divmod(n - Q0, 2)
                up_half([2 * c + t for t in range(NT)], by_token, n, k)
            pe.wait_ge(sem("q_copied"), 2 * NT)
            pe.wait_ge(sem("q_turned"), 2 * NT)
            pe.wait_ge(sem("kT_ready"), 4)
            transposes(mix, None, "q_transposed", 4)
            pe.wait_ge(sem("qT_ready"), 4)
            pe.wait_ge(sem("masks_ready"), 3)
            for h in range(HEADS + 3):
                if h < HEADS:
                    if h >= 3:
                        pe.wait_ge(sem("exped"), NT * (h - 2))
                    s = ps[:, SCORES[h % 3], :]
                    mm(s[:, 0:P], qT[:, h, 0:P], kT[:, h, 0:P], start=True, stop=False)
                    mm(s[:, 0:P], ident[:], mask[:], start=False, stop=True)
                    mm(s[:, P:2 * P], qT[:, h, P:S], kT[:, h, 0:P], start=True, stop=True)
                    mm(s[:, 2 * P:3 * P], qT[:, h, P:S], kT[:, h, P:S], start=True, stop=False)
                    mm(s[:, 2 * P:3 * P], ident[:], mask[:], start=False, stop=True)\
                        .then_inc(sem("scores"), 1)
                if 2 <= h < HEADS + 2:
                    k = h - 2
                    pe.wait_ge(sem("prob_ready"), NT * (k + 1))
                    if k >= 2:
                        pe.wait_ge(sem("probT_ready"), k - 1)
                    for m in range(3):
                        last = nc.tensor.transpose(ps[:, 2 + k % 2, m * P:(m + 1) * P],
                                                   prob[k % 3][:, m * P:(m + 1) * P], ident[:])
                    last.then_inc(sem("prob_transposed"), 1)
                if h >= 3:
                    k = h - 3
                    pe.wait_ge(sem("probT_ready"), k + 1)
                    if k >= 2:
                        pe.wait_ge(sem("oT_ready"), k - 1)
                    cols = slice(k * DH, (k + 1) * DH)
                    mm(ps[:, 4 + k % 2, 0:P], v[:, 0, cols], probT[k % 2][:, 0, :], start=True, stop=True)
                    mm(ps[:, 4 + k % 2, P:S], v[:, 0, cols], probT[k % 2][:, 1, :], start=True, stop=False)
                    mm(ps[:, 4 + k % 2, P:S], v[:, 1, cols], probT[k % 2][:, 2, :], start=False, stop=True)\
                        .then_inc(sem("o_made"), 1)
            pe.wait_ge(sem("oT_ready"), HEADS)
            for n in range(O0, MOE0):
                c, k = divmod(n - O0, 2)
                up_half([2 * t + c for t in range(NT)], by_token, n, k)

            transposes(x, "added_2", "moe_transposed", 4)
            pe.wait_ge(sem("moe_v"), 4)
            for t in range(NT):
                for kt in range(KT):
                    last = mm(ps[:, 0, t * E:(t + 1) * E], tmpT[:, kt, t * P:(t + 1) * P], wr[:, kt, :],
                              start=(kt == 0), stop=(kt == KT - 1))
            last.then_inc(sem("logits"), 1)
            pe.wait_ge(sem("sel_ready"), 1)
            pe.wait_ge(sem("masks_ready"), 3)
            sel = rt[:, 5]
            mm(ps[:, 1, 0:E], tri[:], sel[:, 0, :], start=True, stop=True)
            mm(ps[:, 1, E:2 * E], ones[:], sel[:, 0, :], start=True, stop=False)
            mm(ps[:, 1, E:2 * E], tri[:], sel[:, 1, :], start=False, stop=True)
            mm(ps[:, 2, 0:E], ones[:], sel[:, 0, :], start=True, stop=False)
            mm(ps[:, 2, 0:E], ones[:], sel[:, 1, :], start=False, stop=True).then_inc(sem("places"), 1)

            def gather_half(i, b, half):
                pe.wait_ge(sem("onehot_ready"), NT * i + NT)
                for k in range(4):
                    kt = 4 * half + k
                    for t in range(NT):
                        last = mm(ps[:, 2 * b + half, k * P:(k + 1) * P],
                                  xn[:, t, kt * P:(kt + 1) * P], onehot[:, t, b * P:(b + 1) * P],
                                  start=(t == 0), stop=(t == NT - 1))
                return last

            def gather_end(b):
                def steps(i, blocks):
                    if b < blocks:
                        if b > 0:
                            gather_half(i, b, 0)
                        gather_half(i, b, 1).then_inc(sem("gathered"), BLOCKS // blocks)
                return steps

            def gather_first(i, half):
                if half == 0:
                    gather_half(i, 0, 0)
                else:
                    by_blocks(pe, i, gather_end(0))

            def hidden(i, blocks):
                swiglu(i * STEPS + FFN_STEPS, i, ORDER, MOE0, UNITS, blocks,
                       lambda b, kt: [t[:, b, kt, :] for t in xTe],
                       lambda: pe.wait_ge(sem("added"), i * 4 + 4),
                       lambda half: gather_first(i + 1, half),
                       lambda: pe.wait_ge(sem("weightedT_ready"), i + 1))

            def combine(i, blocks):
                for q in (0, 2, 1, 3):
                    t, half = q // 2, q % 2
                    pe.wait_ge(sem("y_rows"), 2 * i + half + 1)
                    for b in range(blocks):
                        last = mm(ps[:, 4 + q, :], weightedT[:, b, t * P:(t + 1) * P],
                                  y_rows[:, b, half * BK:(half + 1) * BK], start=(b == 0), stop=(b == blocks - 1))
                    last.then_inc(sem("combined"), 1)

            pe.wait_ge(sem("routed"), 1)
            pe.wait_ge(sem("moe_xn"), NT)
            gather_first(0, 0)
            gather_first(0, 1)
            by_blocks(pe, 0, gather_end(1))
            with pe.Fori(0, E) as i:
                pe.wait_ge(sem("xTe_ready"), (i + 1) * BLOCKS)
                pe.wait_ge(sem("weighted_ready"), NT * i + NT)
                for b in range(BLOCKS):
                    for t in range(NT):
                        last = nc.tensor.transpose(ps[:, 3, b * S + t * P:b * S + (t + 1) * P],
                                                   weighted[:, t, b * P:(b + 1) * P], ident[:])
                last.then_inc(sem("weighted_T"), 1)
                by_blocks(pe, i, hidden)
                by_blocks(pe, i + 1, gather_end(1))
                by_blocks(pe, i, combine)


def kernel(**inputs):
    import numpy as _np
    import concourse.bacc as _bacc
    from concourse import mybir as _mybir
    from concourse.bass_utils import run_bass_kernel_spmd as _run

    nc = _bacc.Bacc("TRN2", target_bir_lowering=False, num_devices=1)
    arrays, args = {}, {}
    for name, value in lay_out(inputs).items():
        value = _np.ascontiguousarray(value)
        arrays[f"in_{name}"] = value
        args[name] = nc.dram_tensor(f"in_{name}", value.shape, _mybir.dt.from_np(value.dtype),
                                    kind="ExternalInput").ap()
    out = nc.dram_tensor("out_0", (1, S, D), F32, kind="ExternalOutput").ap()
    trunk(nc, args, out)
    r = _run(nc, [arrays], core_ids=[0])
    return r.results[0]["out_0"]
```
